# Optimizing a Trainium2 kernel written in Bass

```python
import jax, jax.numpy as jnp
from jax import lax
import numpy as np
import math

D_MODEL = 1024
BATCH = 1
SEQ = 512
DEPTH = 2

GDN_HEADS = 4
GDN_DK = 128
GDN_DV = 128
GDN_CHUNK = 64
CONV_K = 4
MLA_HEADS = 8
MLA_Q_LORA = 384
MLA_KV_LORA = 256
MLA_NOPE = 128
MLA_ROPE = 64
MLA_DV = 128
ROPE_THETA = 10000.0
Q_BLOCK = 128
LRU_WIDTH = 512
LRU_BLOCKS = 8
LRU_BW = LRU_WIDTH // LRU_BLOCKS
RG_C = 8.0

RMS_EPS = 1e-6
L2_EPS = 1e-6

GDN_WIDTH = GDN_HEADS * GDN_DV
MLA_WIDTH = MLA_HEADS * MLA_DV
MIX_WIDTH = GDN_WIDTH + MLA_WIDTH + LRU_WIDTH
MLA_QK = MLA_NOPE + MLA_ROPE
IN_SPLITS = (GDN_HEADS * GDN_DK, GDN_HEADS * GDN_DK, GDN_WIDTH, GDN_HEADS, GDN_HEADS, GDN_WIDTH,
             MLA_Q_LORA, MLA_KV_LORA, MLA_ROPE, MLA_WIDTH,
             LRU_WIDTH, LRU_WIDTH)
IN_WIDTH = sum(IN_SPLITS)


def rmsnorm(x, gain):
    xf = x.astype(jnp.float32)
    y = xf * lax.rsqrt(jnp.mean(xf * xf, axis=-1, keepdims=True) + RMS_EPS)
    return (y * gain.astype(jnp.float32)).astype(x.dtype)

def l2norm(x):
    return x * lax.rsqrt(jnp.sum(x * x, axis=-1, keepdims=True) + L2_EPS)

def causal_dwconv(x, w):
    K, C = w.shape
    return lax.conv_general_dilated(
        x, w[:, None, :].astype(x.dtype), window_strides=(1,), padding=[(K - 1, 0)],
        dimension_numbers=("NWC", "WIO", "NWC"), feature_group_count=C)

def gated_delta_rule(q, k, v, g, beta):
    B, S, H, DK = q.shape
    DV = v.shape[-1]
    C = GDN_CHUNK
    N = S // C

    def chunks(t):
        return t.reshape(B, N, C, H, t.shape[-1]).transpose(0, 1, 3, 2, 4)

    qc = chunks(q * DK ** -0.5)
    kc = chunks(k)
    vc = chunks(v)
    gc = jnp.cumsum(g.reshape(B, N, C, H).transpose(0, 1, 3, 2), axis=-1)
    bc = beta.reshape(B, N, C, H).transpose(0, 1, 3, 2)[..., None]
    tril = jnp.tril(jnp.ones((C, C), bool))
    strict = jnp.tril(jnp.ones((C, C), bool), -1)
    decay = jnp.exp(jnp.where(tril, gc[..., :, None] - gc[..., None, :], -jnp.inf))
    kbeta = kc * bc
    a_mat = jnp.where(strict, jnp.einsum('bnhid,bnhjd->bnhij', kbeta, kc) * decay, 0.0) \
        + jnp.eye(C, dtype=q.dtype)
    rhs = jnp.concatenate([vc * bc, kbeta * jnp.exp(gc)[..., None]], axis=-1)
    sol = lax.linalg.triangular_solve(a_mat, rhs, left_side=True, lower=True, unit_diagonal=True)
    u, w = sol[..., :DV], sol[..., DV:]
    attn = jnp.where(tril, jnp.einsum('bnhid,bnhjd->bnhij', qc, kc) * decay, 0.0)

    def step(state, inp):
        q_n, k_n, u_n, w_n, g_n, a_n = inp
        v_new = u_n - jnp.einsum('bhck,bhkv->bhcv', w_n, state)
        o = jnp.einsum('bhck,bhkv->bhcv', q_n * jnp.exp(g_n)[..., None], state) \
            + jnp.einsum('bhij,bhjv->bhiv', a_n, v_new)
        g_last = g_n[..., -1]
        state = state * jnp.exp(g_last)[..., None, None] + jnp.einsum(
            'bhck,bhcv->bhkv', k_n * jnp.exp(g_last[..., None] - g_n)[..., None], v_new)
        return state, o

    xs = (jnp.moveaxis(qc, 1, 0), jnp.moveaxis(kc, 1, 0), jnp.moveaxis(u, 1, 0),
          jnp.moveaxis(w, 1, 0), jnp.moveaxis(gc, 1, 0), jnp.moveaxis(attn, 1, 0))
    state0 = jnp.zeros((B, H, DK, DV), q.dtype)
    _, o = lax.scan(step, state0, xs)
    return o.transpose(1, 0, 3, 2, 4).reshape(B, S, H, DV)

def rope_tables(S):
    inv = 1.0 / (ROPE_THETA ** (jnp.arange(0, MLA_ROPE, 2, dtype=jnp.float32) / MLA_ROPE))
    ang = jnp.arange(S, dtype=jnp.float32)[:, None] * inv[None, :]
    ang = jnp.concatenate([ang, ang], axis=-1)
    return jnp.cos(ang)[None, :, None, :], jnp.sin(ang)[None, :, None, :]

def apply_rope(t, cos, sin):
    half = t.shape[-1] // 2
    rot = jnp.concatenate([-t[..., half:], t[..., :half]], axis=-1)
    return (t * cos + rot * sin).astype(t.dtype)

def causal_block_attention(q, k, v):
    B, H, S, D = q.shape
    nb = S // Q_BLOCK
    scale = D ** -0.5
    qb = q.reshape(B, H, nb, Q_BLOCK, D).transpose(2, 0, 1, 3, 4)
    kpos = jnp.arange(S)

    def one_block(args):
        qi, i = args
        s = jnp.einsum('bhqd,bhkd->bhqk', qi, k).astype(jnp.float32) * scale
        qpos = i * Q_BLOCK + jnp.arange(Q_BLOCK)
        s = jnp.where(kpos[None, :] <= qpos[:, None], s, -jnp.inf)
        p = jax.nn.softmax(s, axis=-1).astype(v.dtype)
        return jnp.einsum('bhqk,bhkd->bhqd', p, v)

    out = lax.map(one_block, (qb, jnp.arange(nb)))
    return out.transpose(1, 0, 3, 2, 4).reshape(B, S, H * v.shape[-1])

def rg_lru(x, w_r, b_r, w_i, b_i, a_param):
    B, S, W = x.shape
    xb = x.reshape(B, S, LRU_BLOCKS, LRU_BW)
    r = jax.nn.sigmoid(jnp.einsum('bsnc,ncd->bsnd', xb, w_r).reshape(B, S, W) + b_r)
    i = jax.nn.sigmoid(jnp.einsum('bsnc,ncd->bsnd', xb, w_i).reshape(B, S, W) + b_i)
    log_a = -RG_C * r * jax.nn.softplus(-a_param)
    a = jnp.exp(log_a)
    b = jnp.sqrt(-jnp.expm1(2.0 * log_a)) * (i * x)

    def combine(lhs, rhs):
        a1, b1 = lhs
        a2, b2 = rhs
        return a1 * a2, a2 * b1 + b2

    _, h = lax.associative_scan(combine, (a, b), axis=1)
    return h

def hybrid_layer(x, cos, sin, norm_gain, w_in, gdn_conv_w, gdn_a_log, gdn_dt_bias, gdn_out_norm,
                 mla_q_norm, mla_w_uq, mla_kv_norm, mla_w_ukv, lru_conv_w, lru_conv_b,
                 lru_w_r, lru_b_r, lru_w_i, lru_b_i, lru_a_param, w_out):
    B, S, _ = x.shape
    dt = x.dtype
    h = rmsnorm(x, norm_gain)
    proj = h @ w_in
    offsets = [int(o) for o in np.cumsum(IN_SPLITS)[:-1]]
    (gq, gk, gv, gb, ga, gz, mq, mkv, mkr, mz, lx, lz) = jnp.split(proj, offsets, axis=-1)

    qkv = jax.nn.silu(causal_dwconv(jnp.concatenate([gq, gk, gv], axis=-1), gdn_conv_w))
    qkv = qkv.astype(jnp.float32)
    q = l2norm(qkv[..., :GDN_HEADS * GDN_DK].reshape(B, S, GDN_HEADS, GDN_DK))
    k = l2norm(qkv[..., GDN_HEADS * GDN_DK:2 * GDN_HEADS * GDN_DK].reshape(B, S, GDN_HEADS, GDN_DK))
    v = qkv[..., 2 * GDN_HEADS * GDN_DK:].reshape(B, S, GDN_HEADS, GDN_DV)
    beta = jax.nn.sigmoid(gb.astype(jnp.float32))
    g = -jnp.exp(gdn_a_log.astype(jnp.float32)) * jax.nn.softplus(
        ga.astype(jnp.float32) + gdn_dt_bias.astype(jnp.float32))
    o_a = gated_delta_rule(q, k, v, g, beta)
    o_a = rmsnorm(o_a, gdn_out_norm).reshape(B, S, GDN_WIDTH).astype(dt) * jax.nn.silu(gz)

    qm = (rmsnorm(mq, mla_q_norm) @ mla_w_uq).reshape(B, S, MLA_HEADS, MLA_QK)
    kv = (rmsnorm(mkv, mla_kv_norm) @ mla_w_ukv).reshape(B, S, MLA_HEADS, MLA_NOPE + MLA_DV)
    q_pe = apply_rope(qm[..., MLA_NOPE:], cos, sin)
    k_pe = apply_rope(mkr[:, :, None, :], cos, sin)
    qf = jnp.concatenate([qm[..., :MLA_NOPE], q_pe], axis=-1)
    kf = jnp.concatenate([kv[..., :MLA_NOPE],
                          jnp.broadcast_to(k_pe, (B, S, MLA_HEADS, MLA_ROPE))], axis=-1)
    vm = kv[..., MLA_NOPE:]
    o_b = causal_block_attention(qf.transpose(0, 2, 1, 3), kf.transpose(0, 2, 1, 3),
                                 vm.transpose(0, 2, 1, 3)).astype(dt) * jax.nn.silu(mz)

    u = (causal_dwconv(lx, lru_conv_w) + lru_conv_b).astype(jnp.float32)
    o_c = rg_lru(u, lru_w_r.astype(jnp.float32), lru_b_r.astype(jnp.float32),
                 lru_w_i.astype(jnp.float32), lru_b_i.astype(jnp.float32),
                 lru_a_param.astype(jnp.float32)).astype(dt) * jax.nn.silu(lz)

    mixed = jnp.concatenate([o_a, o_b, o_c], axis=-1)
    return x + mixed @ w_out

def first_inputs(seed: int = 0) -> dict:
    key = jax.random.key(seed)
    ks = jax.random.split(key, 24)
    L = DEPTH
    f32 = jnp.float32

    def nrm(k, shape, scale):
        return scale * jax.random.normal(k, shape, f32)

    def gain(k, shape):
        return 1.0 + 0.01 * jax.random.normal(k, shape, f32)

    x = jax.random.normal(ks[0], (BATCH, SEQ, D_MODEL), f32)
    norm_gain = gain(ks[1], (L, D_MODEL))
    w_in = nrm(ks[2], (L, D_MODEL, IN_WIDTH), D_MODEL ** -0.5)
    gdn_conv_w = nrm(ks[3], (L, CONV_K, 2 * GDN_HEADS * GDN_DK + GDN_WIDTH), CONV_K ** -0.5)
    gdn_a_log = jnp.log(jax.random.uniform(ks[4], (L, GDN_HEADS), f32, 1.0, 16.0))
    dt0 = jnp.exp(jax.random.uniform(ks[5], (L, GDN_HEADS), f32, np.log(1e-3), np.log(1e-1)))
    gdn_dt_bias = dt0 + jnp.log(-jnp.expm1(-dt0))
    gdn_out_norm = gain(ks[6], (L, GDN_DV))
    mla_q_norm = gain(ks[7], (L, MLA_Q_LORA))
    mla_w_uq = nrm(ks[8], (L, MLA_Q_LORA, MLA_HEADS * MLA_QK), MLA_Q_LORA ** -0.5)
    mla_kv_norm = gain(ks[9], (L, MLA_KV_LORA))
    mla_w_ukv = nrm(ks[10], (L, MLA_KV_LORA, MLA_HEADS * (MLA_NOPE + MLA_DV)), MLA_KV_LORA ** -0.5)
    lru_conv_w = nrm(ks[11], (L, CONV_K, LRU_WIDTH), CONV_K ** -0.5)
    lru_conv_b = nrm(ks[12], (L, LRU_WIDTH), 0.01)
    lru_w_r = nrm(ks[13], (L, LRU_BLOCKS, LRU_BW, LRU_BW), LRU_BW ** -0.5)
    lru_b_r = nrm(ks[14], (L, LRU_WIDTH), 0.01)
    lru_w_i = nrm(ks[15], (L, LRU_BLOCKS, LRU_BW, LRU_BW), LRU_BW ** -0.5)
    lru_b_i = nrm(ks[16], (L, LRU_WIDTH), 0.01)
    a_target = jax.random.uniform(ks[17], (L, LRU_WIDTH), f32, 0.9, 0.999)
    sp = -jnp.log(a_target) / RG_C
    lru_a_param = -jnp.log(jnp.expm1(sp))
    w_out = nrm(ks[18], (L, MIX_WIDTH, D_MODEL), MIX_WIDTH ** -0.5)
    final_norm = gain(ks[19], (D_MODEL,))
    return {"x": x, "norm_gain": norm_gain, "w_in": w_in, "gdn_conv_w": gdn_conv_w,
            "gdn_a_log": gdn_a_log, "gdn_dt_bias": gdn_dt_bias, "gdn_out_norm": gdn_out_norm,
            "mla_q_norm": mla_q_norm, "mla_w_uq": mla_w_uq, "mla_kv_norm": mla_kv_norm,
            "mla_w_ukv": mla_w_ukv, "lru_conv_w": lru_conv_w, "lru_conv_b": lru_conv_b,
            "lru_w_r": lru_w_r, "lru_b_r": lru_b_r, "lru_w_i": lru_w_i, "lru_b_i": lru_b_i,
            "lru_a_param": lru_a_param, "w_out": w_out, "final_norm": final_norm}

def first_block(x, norm_gain, w_in, gdn_conv_w, gdn_a_log, gdn_dt_bias, gdn_out_norm,
              mla_q_norm, mla_w_uq, mla_kv_norm, mla_w_ukv, lru_conv_w, lru_conv_b,
              lru_w_r, lru_b_r, lru_w_i, lru_b_i, lru_a_param, w_out, final_norm):
    cos, sin = rope_tables(x.shape[1])
    h = x
    for l in range(DEPTH):
        h = hybrid_layer(h, cos, sin, norm_gain[l], w_in[l], gdn_conv_w[l], gdn_a_log[l],
                         gdn_dt_bias[l], gdn_out_norm[l], mla_q_norm[l], mla_w_uq[l],
                         mla_kv_norm[l], mla_w_ukv[l], lru_conv_w[l], lru_conv_b[l],
                         lru_w_r[l], lru_b_r[l], lru_w_i[l], lru_b_i[l], lru_a_param[l], w_out[l])
    return rmsnorm(h, final_norm)


DEPTH_2 = 1

GRID_W = 64
CTX_LEN = 256
HEAD_DIM = 64
A_HEADS = 4
R_HEADS = 4
R_DK = 64
R_DV = 128
A_QK = A_HEADS * 2 * HEAD_DIM
A_V = A_HEADS * 2 * HEAD_DIM
R_QK = R_HEADS * R_DK
R_V = R_HEADS * R_DV
D_IN = 2 * A_QK + A_V + 2 * R_QK + 2 * R_V
D_MIX = A_V + R_V
RET_CHUNK = 128
ROPE_BASE = 10000.0
N_EXPERTS = 64
N_GROUPS = 8
TOPK_GROUPS = 4
TOP_K = 8
D_EXPERT = D_MODEL // 4
D_SHARED = D_MODEL // 4
ROUTED_SCALE = 2.5
MOE_BLOCK = 128
NORM_EPS = 1e-6


def rmsnorm_2(x, g):
    xf = x.astype(jnp.float32)
    y = xf * lax.rsqrt(jnp.mean(xf * xf, axis=-1, keepdims=True) + NORM_EPS)
    return (y * g.astype(jnp.float32)).astype(x.dtype)

def modulate(h, shift, scale):
    return h * (1 + scale[:, None]) + shift[:, None]

def axial_rope_tables(n_tokens):
    n_rows = n_tokens // GRID_W
    rows = jnp.broadcast_to(jnp.arange(n_rows, dtype=jnp.float32)[:, None], (n_rows, GRID_W)).reshape(-1)
    cols = jnp.broadcast_to(jnp.arange(GRID_W, dtype=jnp.float32)[None, :], (n_rows, GRID_W)).reshape(-1)
    n_freq = HEAD_DIM // 4
    inv_freq = ROPE_BASE ** (-jnp.arange(n_freq, dtype=jnp.float32) / n_freq)
    ang = jnp.stack([rows[:, None] * inv_freq, cols[:, None] * inv_freq], axis=1)
    return jnp.cos(ang), jnp.sin(ang)

def apply_axial_rope(x, cos, sin):
    n_freq = HEAD_DIM // 4
    xr = x.reshape(x.shape[:-1] + (2, 2, n_freq)).astype(jnp.float32)
    shp = (cos.shape[0],) + (1,) * (x.ndim - 3) + (2, n_freq)
    c = cos.reshape(shp)
    s = sin.reshape(shp)
    x1, x2 = xr[..., 0, :], xr[..., 1, :]
    out = jnp.stack([x1 * c - x2 * s, x1 * s + x2 * c], axis=-2)
    return out.reshape(x.shape).astype(x.dtype)

def project_heads(h, w_in):
    bn, t, _ = h.shape
    p = h @ w_in
    sizes = (A_QK, A_QK, A_V, R_QK, R_QK, R_V, R_V)
    cuts = [sum(sizes[:i + 1]) for i in range(len(sizes) - 1)]
    dq, dk, dv, rq, rk, rv, rg = jnp.split(p, cuts, axis=-1)
    return (dq.reshape(bn, t, A_HEADS, 2, HEAD_DIM),
            dk.reshape(bn, t, A_HEADS, 2, HEAD_DIM),
            dv.reshape(bn, t, A_HEADS, 2 * HEAD_DIM),
            rq.reshape(bn, t, R_HEADS, R_DK),
            rk.reshape(bn, t, R_HEADS, R_DK),
            rv.reshape(bn, t, R_HEADS, R_DV),
            rg)

def diff_attend(q, k, v, lam):
    s = jnp.einsum('bqhmd,bkhmd->bhmqk', q, k).astype(jnp.float32)
    p = jax.nn.softmax(s, axis=-1)
    a = p[:, :, 0] - lam * p[:, :, 1]
    return jnp.einsum('bhqk,bkhe->bqhe', a.astype(v.dtype), v)

def retention_chunked(q, k, v, log_gamma, state0):
    b, t, h, dk = q.shape
    dv = v.shape[-1]
    n = t // RET_CHUNK
    f32 = jnp.float32
    qc = q.astype(f32).reshape(b, n, RET_CHUNK, h, dk)
    kc = k.astype(f32).reshape(b, n, RET_CHUNK, h, dk)
    vc = v.astype(f32).reshape(b, n, RET_CHUNK, h, dv)
    lg = log_gamma.astype(f32)
    pos = jnp.arange(RET_CHUNK, dtype=f32)
    rel = pos[:, None] - pos[None, :]
    decay = jnp.where(rel[None] >= 0, jnp.exp(jnp.maximum(rel, 0.0)[None] * lg[:, None, None]), 0.0)
    scores = jnp.einsum('bnihd,bnjhd->bnhij', qc, kc) * decay
    intra = jnp.einsum('bnhij,bnjhe->bnihe', scores, vc)
    k_dec = kc * jnp.exp((RET_CHUNK - 1 - pos)[:, None] * lg)[:, :, None]
    chunk_kv = jnp.einsum('bnjhd,bnjhe->nbhde', k_dec, vc)
    g_chunk = jnp.exp(RET_CHUNK * lg)[None, :, None, None]

    def step(s, kv_i):
        return g_chunk * s + kv_i, s

    state_final, state_prev = lax.scan(step, state0.astype(f32), chunk_kv)
    q_dec = qc * jnp.exp((pos + 1)[:, None] * lg)[:, :, None]
    cross = jnp.einsum('bnihd,nbhde->bnihe', q_dec, state_prev)
    out = (intra + cross).reshape(b, t, h, dv)
    return out.astype(v.dtype), state_final

def bidir_retention(q_c, k_c, v_c, q_x, k_x, v_x, logg_f, logg_b):
    b = q_x.shape[0]
    s0 = jnp.zeros((b, R_HEADS, R_DK, R_DV), jnp.float32)
    flip = lambda a: jnp.flip(a, axis=1)
    o_cf, s_cf = retention_chunked(q_c, k_c, v_c, logg_f, s0)
    o_xf, _ = retention_chunked(q_x, k_x, v_x, logg_f, s_cf)
    o_cb, s_cb = retention_chunked(flip(q_c), flip(k_c), flip(v_c), logg_b, s0)
    o_xb, _ = retention_chunked(flip(q_x), flip(k_x), flip(v_x), logg_b, s_cb)
    return o_cf + flip(o_cb), o_xf + flip(o_xb)

def mixer_merge(att, ret, gate, lam_init, dattn_norm_g, ret_norm_g, w_out):
    bn, t = att.shape[:2]
    a = (rmsnorm_2(att, dattn_norm_g) * (1 - lam_init)).reshape(bn, t, A_V)
    r = jax.nn.silu(gate) * rmsnorm_2(ret, ret_norm_g).reshape(bn, t, R_V)
    return jnp.concatenate([a, r], axis=-1) @ w_out

def moe_ffn(h, router_w, router_bias, w1, w3, w2, sw1, sw3, sw2):
    t, d = h.shape
    scores = jax.nn.sigmoid((h @ router_w).astype(jnp.float32))
    sel = scores + router_bias.astype(jnp.float32)
    grp = sel.reshape(t, N_GROUPS, N_EXPERTS // N_GROUPS)
    grp_score = lax.top_k(grp, 2)[0].sum(-1)
    _, top_g = lax.top_k(grp_score, TOPK_GROUPS)
    gmask = jax.nn.one_hot(top_g, N_GROUPS, dtype=jnp.float32).sum(axis=1) > 0
    emask = jnp.repeat(gmask, N_EXPERTS // N_GROUPS, axis=1)
    _, top_e = lax.top_k(jnp.where(emask, sel, -jnp.inf), TOP_K)
    wts = jnp.take_along_axis(scores, top_e, axis=1)
    wts = wts / jnp.sum(wts, axis=-1, keepdims=True) * ROUTED_SCALE
    n_assign = t * TOP_K
    e_flat = top_e.reshape(n_assign)
    t_flat = jnp.repeat(jnp.arange(t, dtype=jnp.int32), TOP_K)
    w_flat = wts.reshape(n_assign)
    order = jnp.argsort(e_flat)
    e_s, t_s, w_s = e_flat[order], t_flat[order], w_flat[order]
    counts = jax.ops.segment_sum(jnp.ones((n_assign,), jnp.int32), e_flat, num_segments=N_EXPERTS)
    padded = (counts + MOE_BLOCK - 1) // MOE_BLOCK * MOE_BLOCK
    pad_end = jnp.cumsum(padded)
    pad_start = pad_end - padded
    start = jnp.cumsum(counts) - counts
    dest = pad_start[e_s] + jnp.arange(n_assign, dtype=jnp.int32) - start[e_s]
    n_pad = -(-n_assign // MOE_BLOCK) * MOE_BLOCK + N_EXPERTS * MOE_BLOCK
    n_blk = n_pad // MOE_BLOCK
    tok_buf = jnp.full((n_pad,), t, jnp.int32).at[dest].set(t_s)
    w_buf = jnp.zeros((n_pad,), jnp.float32).at[dest].set(w_s)
    blk_exp = jnp.clip(jnp.searchsorted(pad_end, jnp.arange(n_blk, dtype=jnp.int32) * MOE_BLOCK, side='right'),
                       0, N_EXPERTS - 1).astype(jnp.int32)
    h_pad = jnp.concatenate([h, jnp.zeros((1, d), h.dtype)], axis=0)

    def body(acc, inp):
        tok, wt, e = inp
        xb = h_pad[tok]
        yb = (jax.nn.silu(xb @ w1[e]) * (xb @ w3[e])) @ w2[e]
        return acc.at[tok].add((yb * wt[:, None].astype(yb.dtype)).astype(acc.dtype)), None

    acc0 = jnp.zeros((t + 1, d), h.dtype)
    acc, _ = lax.scan(body, acc0, (tok_buf.reshape(n_blk, MOE_BLOCK), w_buf.reshape(n_blk, MOE_BLOCK), blk_exp))
    shared = (jax.nn.silu(h @ sw1) * (h @ sw3)) @ sw2
    return acc[:t] + shared

def hybrid_layer_2(x, xc, mod_x, mod_c, cos, sin, lam_init, update_ctx,
                 norm1_g, w_in, lambda_q1, lambda_k1, lambda_q2, lambda_k2, dattn_norm_g,
                 ret_decay_fwd, ret_decay_bwd, ret_norm_g, w_out,
                 norm2_g, router_w, router_bias, exp_w1, exp_w3, exp_w2,
                 shared_w1, shared_w3, shared_w2):
    b, s, d = x.shape
    sh1, sc1, g1, sh2, sc2, g2 = jnp.split(mod_x, 6, axis=-1)
    csh1, csc1, cg1, csh2, csc2, cg2 = jnp.split(mod_c, 6, axis=-1)

    hx = modulate(rmsnorm_2(x, norm1_g), sh1, sc1)
    hc = modulate(rmsnorm_2(xc, norm1_g), csh1, csc1)
    dq_x, dk_x, dv_x, rq_x, rk_x, rv_x, rg_x = project_heads(hx, w_in)
    dq_c, dk_c, dv_c, rq_c, rk_c, rv_c, rg_c = project_heads(hc, w_in)

    dq_x = apply_axial_rope(dq_x, cos, sin) * HEAD_DIM ** -0.5
    dk_x = apply_axial_rope(dk_x, cos, sin)
    rq_x = apply_axial_rope(rq_x, cos, sin)
    rk_x = apply_axial_rope(rk_x, cos, sin) * R_DK ** -0.5
    dq_c = dq_c * HEAD_DIM ** -0.5
    rk_c = rk_c * R_DK ** -0.5

    lam = (jnp.exp(jnp.sum(lambda_q1 * lambda_k1)) - jnp.exp(jnp.sum(lambda_q2 * lambda_k2))).astype(jnp.float32) + lam_init

    k_all = jnp.concatenate([dk_c, dk_x], axis=1)
    v_all = jnp.concatenate([dv_c, dv_x], axis=1)
    n_qblk = s // Q_BLOCK
    q_blocks = dq_x.reshape(b, n_qblk, Q_BLOCK, A_HEADS, 2, HEAD_DIM).swapaxes(0, 1)
    att_x = lax.map(lambda qb: diff_attend(qb, k_all, v_all, lam), q_blocks)
    att_x = att_x.swapaxes(0, 1).reshape(b, s, A_HEADS, 2 * HEAD_DIM)

    logg_f = jax.nn.log_sigmoid(ret_decay_fwd.astype(jnp.float32))
    logg_b = jax.nn.log_sigmoid(ret_decay_bwd.astype(jnp.float32))
    ret_c, ret_x = bidir_retention(rq_c, rk_c, rv_c, rq_x, rk_x, rv_x, logg_f, logg_b)

    y_x = mixer_merge(att_x, ret_x, rg_x, lam_init, dattn_norm_g, ret_norm_g, w_out)
    x = x + g1[:, None] * y_x
    h2 = modulate(rmsnorm_2(x, norm2_g), sh2, sc2)
    ffn_x = moe_ffn(h2.reshape(b * s, d), router_w, router_bias, exp_w1, exp_w3, exp_w2,
                    shared_w1, shared_w3, shared_w2).reshape(b, s, d)
    x = x + g2[:, None] * ffn_x

    if update_ctx:
        att_c = diff_attend(dq_c, dk_c, dv_c, lam)
        y_c = mixer_merge(att_c, ret_c, rg_c, lam_init, dattn_norm_g, ret_norm_g, w_out)
        xc = xc + cg1[:, None] * y_c
        bc, lc, _ = xc.shape
        h2c = modulate(rmsnorm_2(xc, norm2_g), csh2, csc2)
        ffn_c = moe_ffn(h2c.reshape(bc * lc, d), router_w, router_bias, exp_w1, exp_w3, exp_w2,
                        shared_w1, shared_w3, shared_w2).reshape(bc, lc, d)
        xc = xc + cg2[:, None] * ffn_c
    else:
        xc = None
    return x, xc

def second_inputs(seed: int = 0) -> dict:
    key = jax.random.key(seed)
    ks = jax.random.split(key, 32)
    f32 = jnp.float32

    def nrm(k, shape, scale):
        return jax.random.normal(k, shape, f32) * scale

    gamma0 = 1.0 - 2.0 ** (-5.0 - jnp.arange(R_HEADS, dtype=f32))
    logit0 = jnp.log(gamma0) - jnp.log1p(-gamma0)
    return {
        "x": nrm(ks[0], (BATCH, SEQ, D_MODEL), 1.0),
        "c": nrm(ks[1], (BATCH, D_MODEL), 1.0),
        "ctx": nrm(ks[2], (BATCH, CTX_LEN, D_MODEL), 1.0),
        "c_ctx": nrm(ks[3], (D_MODEL,), 1.0),
        "ada_w": nrm(ks[4], (DEPTH_2, D_MODEL, 6 * D_MODEL), 0.5 * D_MODEL ** -0.5),
        "ada_b": nrm(ks[5], (DEPTH_2, 6 * D_MODEL), 0.02),
        "norm1_g": 1.0 + nrm(ks[6], (DEPTH_2, D_MODEL), 0.05),
        "w_in": nrm(ks[7], (DEPTH_2, D_MODEL, D_IN), D_MODEL ** -0.5),
        "lambda_q1": nrm(ks[8], (DEPTH_2, HEAD_DIM), 0.1),
        "lambda_k1": nrm(ks[9], (DEPTH_2, HEAD_DIM), 0.1),
        "lambda_q2": nrm(ks[10], (DEPTH_2, HEAD_DIM), 0.1),
        "lambda_k2": nrm(ks[11], (DEPTH_2, HEAD_DIM), 0.1),
        "dattn_norm_g": 1.0 + nrm(ks[12], (DEPTH_2, 2 * HEAD_DIM), 0.05),
        "ret_decay_fwd": logit0[None] + nrm(ks[13], (DEPTH_2, R_HEADS), 0.1),
        "ret_decay_bwd": logit0[None] + nrm(ks[14], (DEPTH_2, R_HEADS), 0.1),
        "ret_norm_g": 1.0 + nrm(ks[15], (DEPTH_2, R_DV), 0.05),
        "w_out": nrm(ks[16], (DEPTH_2, D_MIX, D_MODEL), D_MIX ** -0.5),
        "norm2_g": 1.0 + nrm(ks[17], (DEPTH_2, D_MODEL), 0.05),
        "router_w": nrm(ks[18], (DEPTH_2, D_MODEL, N_EXPERTS), D_MODEL ** -0.5),
        "router_bias": nrm(ks[19], (DEPTH_2, N_EXPERTS), 0.01),
        "exp_w1": nrm(ks[20], (DEPTH_2, N_EXPERTS, D_MODEL, D_EXPERT), D_MODEL ** -0.5),
        "exp_w3": nrm(ks[21], (DEPTH_2, N_EXPERTS, D_MODEL, D_EXPERT), D_MODEL ** -0.5),
        "exp_w2": nrm(ks[22], (DEPTH_2, N_EXPERTS, D_EXPERT, D_MODEL), D_EXPERT ** -0.5),
        "shared_w1": nrm(ks[23], (DEPTH_2, D_MODEL, D_SHARED), D_MODEL ** -0.5),
        "shared_w3": nrm(ks[24], (DEPTH_2, D_MODEL, D_SHARED), D_MODEL ** -0.5),
        "shared_w2": nrm(ks[25], (DEPTH_2, D_SHARED, D_MODEL), D_SHARED ** -0.5),
        "final_norm_g": 1.0 + nrm(ks[26], (D_MODEL,), 0.05),
    }

def second_block(x, c, ctx, c_ctx, ada_w, ada_b, norm1_g, w_in, lambda_q1, lambda_k1, lambda_q2, lambda_k2,
              dattn_norm_g, ret_decay_fwd, ret_decay_bwd, ret_norm_g, w_out, norm2_g, router_w, router_bias,
              exp_w1, exp_w3, exp_w2, shared_w1, shared_w3, shared_w2, final_norm_g):
    s = x.shape[1]
    cos, sin = axial_rope_tables(s)
    xc = ctx
    for l in range(DEPTH_2):
        lam_init = 0.8 - 0.6 * math.exp(-0.3 * l)
        mod_x = jax.nn.silu(c) @ ada_w[l] + ada_b[l]
        mod_c = (jax.nn.silu(c_ctx) @ ada_w[l] + ada_b[l])[None]
        x, xc = hybrid_layer_2(x, xc, mod_x, mod_c, cos, sin, lam_init, l < DEPTH_2 - 1,
                             norm1_g[l], w_in[l], lambda_q1[l], lambda_k1[l], lambda_q2[l], lambda_k2[l],
                             dattn_norm_g[l], ret_decay_fwd[l], ret_decay_bwd[l], ret_norm_g[l], w_out[l],
                             norm2_g[l], router_w[l], router_bias[l], exp_w1[l], exp_w3[l], exp_w2[l],
                             shared_w1[l], shared_w3[l], shared_w2[l])
    return rmsnorm_2(x, final_norm_g)


def setup_inputs(seed=0):
    out = dict(first_inputs(seed))
    for name, value in second_inputs(seed + 1).items():
        if name != "x":
            out[name + "_2"] = value
    return out


def reference(
    x, norm_gain, w_in, gdn_conv_w, gdn_a_log, gdn_dt_bias, gdn_out_norm, mla_q_norm, mla_w_uq,
    mla_kv_norm, mla_w_ukv, lru_conv_w, lru_conv_b, lru_w_r, lru_b_r, lru_w_i, lru_b_i,
    lru_a_param, w_out, final_norm, c_2, ctx_2, c_ctx_2, ada_w_2, ada_b_2, norm1_g_2, w_in_2,
    lambda_q1_2, lambda_k1_2, lambda_q2_2, lambda_k2_2, dattn_norm_g_2, ret_decay_fwd_2,
    ret_decay_bwd_2, ret_norm_g_2, w_out_2, norm2_g_2, router_w_2, router_bias_2, exp_w1_2,
    exp_w3_2, exp_w2_2, shared_w1_2, shared_w3_2, shared_w2_2, final_norm_g_2,
):
    x = first_block(
        x, norm_gain, w_in, gdn_conv_w, gdn_a_log, gdn_dt_bias, gdn_out_norm, mla_q_norm,
        mla_w_uq, mla_kv_norm, mla_w_ukv, lru_conv_w, lru_conv_b, lru_w_r, lru_b_r, lru_w_i,
        lru_b_i, lru_a_param, w_out, final_norm,
    )
    return second_block(
        x, c_2, ctx_2, c_ctx_2, ada_w_2, ada_b_2, norm1_g_2, w_in_2, lambda_q1_2, lambda_k1_2,
        lambda_q2_2, lambda_k2_2, dattn_norm_g_2, ret_decay_fwd_2, ret_decay_bwd_2,
        ret_norm_g_2, w_out_2, norm2_g_2, router_w_2, router_bias_2, exp_w1_2, exp_w3_2,
        exp_w2_2, shared_w1_2, shared_w3_2, shared_w2_2, final_norm_g_2,
    )


_drawn_inputs = setup_inputs


def setup_inputs(seed=0):
    import zlib

    import numpy as np

    out = dict(_drawn_inputs(seed))
    spreads = {}
    factors = {'gdn_out_norm': 3.857,
     'mla_q_norm': 8.0,
     'mla_kv_norm': 8.0,
     'lru_b_r': 26.781,
     'lru_b_i': 20.252,
     'lambda_q2_2': 3.178,
     'lambda_k2_2': 8.0,
     'ret_norm_g_2': 3.54,
     'dattn_norm_g_2': 2.95}
    for name, (base, spread) in spreads.items():
        noise = np.random.default_rng([zlib.crc32(name.encode()), seed]).standard_normal(out[name].shape)
        drawn = base * np.exp(spread * noise) if base else spread * noise
        out[name] = __import__('jax').numpy.asarray(drawn.astype(out[name].dtype))
    for name, factor in factors.items():
        out[name] = (out[name] * factor).astype(out[name].dtype)
    return out
```

```python
import math
from contextlib import ExitStack

import numpy as np

import concourse.bass as bass
from concourse import mybir


P = 128
S = 512
D = 1024
KD = D // P
L = 2
CH = S // P
GH = 4
MH = 8
QL, KVL = 3, 2
LW = 4
NMIX = 16
RING = 4
SLOT = 1024
EPS = 1e-6

F32 = mybir.dt.float32
BF16 = mybir.dt.bfloat16
U8 = mybir.dt.uint8
I32 = mybir.dt.int32
U32 = mybir.dt.uint32
ALU = mybir.AluOpType
ACT = mybir.ActivationFunctionType
AX = mybir.AxisListType.X

K0, Q0, V0, GZ0, LX0, LZ0, MQ0, MKV0, MKR, MZ0, NPROJ = 0, 4, 8, 12, 16, 20, 24, 27, 29, 30, 38
UQ0, UK0, UV0, NSTREAM = 38, 50, 58, 66
NADA = 48
ADA_LAYER = NADA // L
LEVELS = 6

C_GAIN, C_CONV, C_LCONV, C_LB, C_BR, C_BI, C_AP, C_QN, C_KVN, C_ON, C_ALOG, C_DT, NCOL = (
    0, 8, 56, 72, 76, 80, 84, 88, 91, 93, 94, 98, 102)

K_ID, K_TRI, K_BIG, K_BIGT, K_PERM, K_COS, K_SIN, K_ONE, K_EPS, K_MHALF, NCONST = (
    0, 128, 256, 384, 512, 640, 1152, 1664, 1665, 1666, 1666 + 16)


def slots_of(plan):
    at, n = {}, 0
    for st in plan:
        if st[0] == "ada":
            at[st] = n
            n += 1
        elif st[0] == "proj":
            i = st[1]
            if i < UQ0:
                at[st] = n
                n += 1
            else:
                group, first = (2, UQ0) if i < UK0 else (4, UK0) if i < UV0 else (CH, UV0)
                if (i - first) % group == 0:
                    n += 1
                at[st] = n - 1
    return at, n


def layer_plan():
    rest = iter(range(NPROJ))
    plan = [("norm",), ("gates",), ("ada", 0)]

    def fill(n=1):
        plan.extend(("proj", next(rest)) for _ in range(n))

    fill(2)
    plan.append(("decay",))
    fill(2)
    plan.append(("l2sum", 0))
    fill()
    plan.append(("l2row", 0))
    fill(3)
    plan.append(("l2sum", 1))
    fill()
    plan.append(("l2row", 1))
    fill(4)
    for c in range(CH):
        plan.append(("prep", c))
        fill()
        plan.append(("first", c))
    for li in range(1, LEVELS + 1):
        plan += [("u", li, 0), ("u", li, 1)]
        fill()
        plan += [("x", li, 0), ("x", li, 1)]
    plan += [("wn", c) for c in range(CH)]
    for c in range(CH):
        plan.append(("value", c))
        fill()
        plan.append(("state", c))
        fill()
        plan.append(("gdnout", c))
    plan.append(("latsum",))
    plan.append(("lrugate", 0))
    plan.append(("lrugate", 1))
    fill()
    plan += [("latrow",), ("lrugate", 2), ("lrugate", 3)]
    plan += [("proj", i) for i in rest]
    spread, ada = [], iter(range(1, ADA_LAYER))
    for n, st in enumerate(plan):
        spread.append(st)
        if n >= 3 and st[0] in ("proj", "l2sum", "l2row", "prep", "decay") and not ("u", 1, 0) in spread:
            t = next(ada, None)
            if t is not None:
                spread.append(("ada", t))
    assert next(ada, None) is None
    spread.insert(spread.index(("u", 1, 0)), ("adaout",))
    plan = spread
    plan.append(("lruscan",))
    for t in range(UQ0, UQ0 + 12):
        plan.append(("proj", t))
    plan.append(("rope", 4))
    for t in range(UK0, NSTREAM):
        plan.append(("proj", t))
        if t - UK0 < 4:
            plan.append(("rope", t - UK0))
    return plan


PLAN = layer_plan()
SLOT_AT, SLOT_OUT = slots_of(PLAN)
NSLOT = SLOT_OUT + 2 * KD
assert NSLOT % RING == 0


def on_dve(i):
    return i < GZ0 or LX0 <= i < LZ0


def count_before(i, dve):
    return sum(1 for t in range(i) if on_dve(t) == dve)


def first_block(nc, stream, cols, gates_w, lru_w, mk, bf, xT, CST, cond, mod):
    ctx = ExitStack()
    with ctx:
        def sb(name, shape, dt=F32):
            return ctx.enter_context(nc.sbuf_tensor(name, shape, dt))

        def sem(name):
            return ctx.enter_context(nc.semaphore(name))

        bank = [ctx.enter_context(nc.psum_tensor(f"bank{i}", [P, 512], F32)) for i in range(8)]
        bank4 = [b[:].rearrange("p (h t) -> p h t", h=4) for b in bank]

        hT = sb("hT", [P, KD, S])
        mixed = sb("mixed", [P, NMIX, S])
        lat = sb("lat", [P, QL + KVL, S])
        kpe = sb("kpe", [P, S])
        ring = sb("ring", [P, RING, SLOT])
        col = sb("col", [P, NCOL])
        wgate = sb("wgate", [P, KD, 8])
        wlru = sb("wlru", [P, LW, 2, P])
        arena = sb("arena", [P, 21 * 1024])
        lruu = sb("lruu", [P, LW, S])

        def part(at, n):
            return arena[:, at * 512:(at + n) * 512]

        def chunked(at):
            return part(at, 4).rearrange("p (c h t) -> p c h t", c=CH, h=GH)

        kT, qT, vT = chunked(0), chunked(4), chunked(8)
        nA, at, X, Y, kdec = chunked(12), chunked(16), chunked(20), chunked(24), chunked(28)
        U = chunked(32)
        conv = part(36, 2).rearrange("p (b t) -> p b t", b=2)
        Sst = part(38, 1).rearrange("p (h t) -> p h t", h=GH)
        vnew = part(39, 1).rearrange("p (h t) -> p h t", h=GH)
        on = part(40, 1).rearrange("p (h t) -> p h t", h=GH)
        scr = part(41, 1)
        lr = part(12, 4).rearrange("p (j t) -> p j t", j=LW)
        li_ = part(16, 4).rearrange("p (j t) -> p j t", j=LW)
        la = part(20, 4).rearrange("p (j t) -> p j t", j=LW)
        lm = part(24, 4).rearrange("p (j t) -> p j t", j=LW)
        sqlat = part(4, 5).rearrange("p (j t) -> p j t", j=5)
        qn = part(0, 8).rearrange("p (h t) -> p h t", h=MH)
        kn = part(8, 8).rearrange("p (h t) -> p h t", h=MH)
        qpe = part(16, 4).rearrange("p (j t) -> p j t", j=4)
        vtok = part(20, 8).rearrange("p (c n) -> p c n", c=CH)
        PT = part(28, 8).rearrange("p (b k t) -> p b k t", b=2, k=4)
        Pr = part(36, 3).rearrange("p (b t) -> p b t", b=3)
        ropet = part(39, 2).rearrange("p (b t) -> p b t", b=2)

        sm = sb("sm", [P, 512])

        def small(at, n):
            return sm[:, at:at + n]

        z, az, e1, w1, ln1, d1, i0, r1, sp = (small(20 * i, 20) for i in range(9))
        beta, nbeta, nbe, egc, ekd, gcc, gl, egl, kdx, g16, eb = (small(180 + 16 * i, 16) for i in range(11))
        ealog = small(356, 4)
        nrm = small(360, 32)
        rn = small(392, 32)
        ss = small(424, 16)
        rs = small(440, 16)
        cpar, npar = small(456, 4), small(460, 4)
        mx = small(464, 4)
        lsum = small(468, 4)
        rl = small(472, 4)
        hs = small(476, 4)
        hr = small(480, 4)
        ls = small(484, 8)
        lrr = small(492, 8)
        scrS = sb("scrS", [P, 128])

        ident = CST[:, K_ID:K_ID + P]
        tri = CST[:, K_TRI:K_TRI + P]
        one = CST[:, K_ONE:K_ONE + 1]
        epsc = CST[:, K_EPS:K_EPS + 1]

        s = {n: sem(n) for n in (
            "small_in squared norm_sum norm_sqrt norm_rec norm_row h_ready gates_mm soft_v soft_a "
            "decay_mm decay_v decay_a proj_mm conv_step silu_done evict_a square_done l2_sum l2_sqrt l2_rec "
            "l2_row l2_done prep_mm prep_v first_mm inv_v u_mm u_sb x_mm wn_mm wn_sb vn_mm vn_sb state_mm "
            "state_v osq_a osum_v opow_p on_v ot_mm gdn_done ada_mm ada_v lat_sq lat_sum lat_sqrt lat_rec lat_row lat_done "
            "lru_mm lru_sig lru_a lru_v rope_mm rope_v s_mm max_v exp_a soft2_v t_mm pt_v pt_a pv_mm mla_done out_mm x_done "
            "slot_used").split()}
        w_ready = [sem(f"w_ready{r}") for r in range(RING)]
        allsems = list(s.values()) + w_ready

        def proj_emptied(eng, i):
            if i < NPROJ and on_dve(i):
                eng.wait_ge(s["conv_step"], 4 * (count_before(i, True) + 1))
            elif i < GZ0:
                raise AssertionError
            else:
                eng.wait_ge(s["evict_a"], i - count_before(min(i, NPROJ), True) + 1)

        def inv_after(li, c):
            return (8 * li + 2 * (c + 1)) if li < LEVELS else 8 * LEVELS + c + 1

        def x_mm_after(li, c):
            return 8 * (li - 1) + 2 * (c + 1) if li < LEVELS else 8 * (LEVELS - 1) + c + 1

        ATT = [(h, q) for h in range(MH) for q in range(CH)]

        ROPE_AT = {a[0]: n for n, a in enumerate([st[1:] for st in PLAN if st[0] == "rope"])}

        def rope_src(j):
            return MKR if j == 4 else UQ0 + 8 + j

        def evict_n(i):
            return i - count_before(min(i, NPROJ), True) + 1

        PT_ON_ACT = [n % 4 == 3 for n in range(len(ATT))]

        def wait_pt(eng, n):
            done = sum(1 for m in range(n + 1) if PT_ON_ACT[m] == PT_ON_ACT[n])
            eng.wait_ge(s["pt_a"] if PT_ON_ACT[n] else s["pt_v"], done)

        def pt_dst(n):
            h, q = ATT[n]
            return PT[:, h % 2, 0:q + 1, q * P:(q + 1) * P]

        with nc.Fori(0, L) as layer:
            with nc.Block() as block:

                @block.sync
                def _(sp_):
                    sp_.dma_start(col[:], cols[bass.ds(layer, 1)].rearrange("a p n -> p (a n)")).then_inc(s["small_in"], 16)
                    sp_.dma_start(wgate[:].rearrange("p k n -> p (k n)"),
                                  gates_w[bass.ds(layer, 1)].rearrange("a p n -> p (a n)")).then_inc(s["small_in"], 16)
                    sp_.dma_start(wlru[:].rearrange("p j g n -> p (j g n)"),
                                  lru_w[bass.ds(layer, 1)].rearrange("a p n -> p (a n)")).then_inc(s["small_in"], 16)
                    for r in range(RING):
                        sp_.dma_start(ring[:, r, :], stream[bass.ds(layer * NSLOT + r, 1)].rearrange("a p n -> p (a n)")
                                      ).then_inc(w_ready[r], 16)
                    with sp_.Fori(1, NSLOT // RING) as i:
                        for r in range(RING):
                            sp_.wait_ge(s["slot_used"], i * RING + (r + 1 - RING))
                            sp_.dma_start(ring[:, r, :],
                                          stream[bass.ds(layer * NSLOT + i * RING + r, 1)].rearrange("a p n -> p (a n)")
                                          ).then_inc(w_ready[r], 16)

                @block.tensor
                def _(pe):
                    mm = nc.tensor.matmul

                    def slot(j):
                        pe.wait_ge(w_ready[j % RING], 16 * (j // RING + 1))
                        return ring[:, j % RING, :]

                    def row_of(dst, colv):
                        return mm(dst, colv.to_broadcast([P, P]), ident, start=True, stop=True)

                    def norm():
                        for k in range(KD):
                            pe.wait_ge(s["squared"], k + 1)
                            for c in range(CH):
                                last = mm(bank[7][:, c * 8 + k:c * 8 + k + 1], hT[:, k, c * P:(c + 1) * P], one,
                                          start=True, stop=True)
                        last.then_inc(s["norm_sum"], 1)
                        pe.wait_ge(s["norm_rec"], 1)
                        for c in range(CH):
                            last = row_of(bank[2][:, c * P:(c + 1) * P], hr[:, c:c + 1])
                        last.then_inc(s["norm_row"], 1)

                    def gates():
                        pe.wait_ge(s["h_ready"], KD)
                        pe.wait_ge(s["small_in"], 48)
                        for c in range(CH):
                            for k in range(KD):
                                last = mm(bank[7][:, 64 + c * 8:64 + c * 8 + 8], hT[:, k, c * P:(c + 1) * P],
                                          wgate[:, k, :], start=(k == 0), stop=(k == KD - 1))
                        last.then_inc(s["gates_mm"], 1)

                    def proj(i):
                        b = bank[i % 2]
                        if i >= 2:
                            proj_emptied(pe, i - 2)
                        if i < NPROJ:
                            w = slot(SLOT_AT[("proj", i)])
                            for k in range(KD):
                                last = mm(b[:], w[:, k * P:(k + 1) * P], hT[:, k, :], start=(k == 0), stop=(k == KD - 1))
                            used = True
                        elif i < UK0:
                            t = i - UQ0
                            pe.wait_ge(s["lat_done"], QL)
                            w = slot(SLOT_AT[("proj", i)])
                            for k in range(QL):
                                o = (t % 2) * QL * P + k * P
                                last = mm(b[:], w[:, o:o + P], lat[:, k, :], start=(k == 0), stop=(k == QL - 1))
                            used = t % 2 == 1
                        elif i < UV0:
                            t = i - UK0
                            pe.wait_ge(s["lat_done"], QL + KVL)
                            w = slot(SLOT_AT[("proj", i)])
                            for k in range(KVL):
                                o = (t % 4) * KVL * P + k * P
                                last = mm(b[:], w[:, o:o + P], lat[:, QL + k, :], start=(k == 0), stop=(k == KVL - 1))
                            used = t % 4 == 3
                        else:
                            half, c = divmod(i - UV0, CH)
                            w = slot(SLOT_AT[("proj", i)])
                            for k in range(KVL):
                                last = mm(b[:], lat[:, QL + k, c * P:(c + 1) * P], w[:, k * 512:(k + 1) * 512],
                                          start=(k == 0), stop=(k == KVL - 1))
                            used = c == CH - 1
                        last.then_inc(s["proj_mm"], 1)
                        if used:
                            pe.wait_ge(s["proj_mm"], i + 1)
                            pe.sem_inc(s["slot_used"], 1)

                    def ada(t):
                        if t == 0:
                            pe.wait_ge(s["soft_a"], 1)
                        w = slot(SLOT_AT[("ada", t)])
                        for k in range(KD):
                            last = mm(bank[7][:, 2 * t:2 * t + 2], w[:, k * P:(k + 1) * P], cond[:, k, :],
                                      start=(k == 0), stop=(k == KD - 1))
                        last.then_inc(s["ada_mm"], 1)
                        pe.wait_ge(s["ada_mm"], t + 1)
                        pe.sem_inc(s["slot_used"], 1)

                    def decay():
                        pe.wait_ge(s["soft_v"], 13)
                        mm(bank[2][:, 0:16], tri, g16, start=True, stop=True).then_inc(s["decay_mm"], 1)
                        for c in range(CH):
                            for h in range(GH):
                                last = mm(bank4[3 + c][:, h, :], g16[:, c * 4 + h:c * 4 + h + 1].to_broadcast([P, P]), tri,
                                          start=True, stop=True)
                            last.then_inc(s["decay_mm"], 1)

                    def l2sum(g):
                        pe.wait_ge(s["square_done"], 4 * (g + 1))
                        pe.wait_ge(s["decay_v"], 1)
                        if g:
                            pe.wait_ge(s["l2_sqrt"], g)
                        for h in range(GH):
                            for c in range(CH):
                                o = 32 + g * 16 + c * 4 + h
                                last = mm(bank[2][:, o:o + 1], mixed[:, 4 + 4 * g + h, c * P:(c + 1) * P], one,
                                          start=True, stop=True)
                        last.then_inc(s["l2_sum"], 1)

                    def l2row(g):
                        pe.wait_ge(s["l2_rec"], g + 1)
                        if g == 0:
                            pe.wait_ge(s["decay_v"], 34)
                            pe.wait_ge(s["decay_a"], 4)
                        else:
                            pe.wait_ge(s["l2_done"], 4)
                        for c in range(CH):
                            for h in range(GH):
                                last = row_of(bank4[3 + c][:, h, :], rn[:, g * 16 + c * 4 + h:g * 16 + c * 4 + h + 1])
                            last.then_inc(s["l2_row"], 1)

                    def prep(c):
                        pe.wait_ge(s["l2_done"], CH + c + 1)
                        if c == 0:
                            pe.wait_ge(s["l2_done"], 2 * CH)
                            pe.wait_ge(s["silu_done"], 12)
                        else:
                            pe.wait_ge(s["prep_v"], 11 * (c - 1) + 8)
                        for h in range(GH):
                            last = mm(bank4[2][:, h, :], kT[:, c, h, :], kT[:, c, h, :], start=True, stop=True)
                        last.then_inc(s["prep_mm"], 1)
                        for h in range(GH):
                            last = mm(bank4[3][:, h, :], kT[:, c, h, :], qT[:, c, h, :], start=True, stop=True)
                        last.then_inc(s["prep_mm"], 1)
                        for h in range(GH):
                            last = nc.tensor.transpose(bank4[4][:, h, :], kT[:, c, h, :], ident)
                        last.then_inc(s["prep_mm"], 1)
                        for h in range(GH):
                            last = nc.tensor.transpose(bank4[5][:, h, :], vT[:, c, h, :], ident)
                        last.then_inc(s["prep_mm"], 1)

                    def first(c):
                        pe.wait_ge(s["prep_v"], 11 * c + 4)
                        if c >= 1:
                            pe.wait_ge(s["inv_v"], 2 * c)
                        for h in range(GH):
                            last = nc.tensor.transpose(bank4[6][:, h, :], nA[:, c, h, :], ident)
                        last.then_inc(s["first_mm"], 1)

                    def u(li, pair):
                        for c in (2 * pair, 2 * pair + 1):
                            n = 4 * (li - 1) + c
                            pe.wait_ge(s["inv_v"], inv_after(li - 1, CH - 1 if li == 1 else c))
                            if n >= 2:
                                pe.wait_ge(s["u_sb"], n - 1)
                            for h in range(GH):
                                last = mm(bank4[2 + c % 2][:, h, :], nA[:, c, h, :], Y[:, c, h, :], start=True, stop=True)
                            last.then_inc(s["u_mm"], 1)

                    def x_(li, pair):
                        for c in (2 * pair, 2 * pair + 1):
                            n = 4 * (li - 1) + c
                            pe.wait_ge(s["u_sb"], n + 1)
                            if c >= 2:
                                pe.wait_ge(s["inv_v"], inv_after(li, c - 2))
                            else:
                                pe.wait_ge(s["inv_v"], inv_after(li - 1, CH - 1 if li == 1 else c + 2))
                            if n == 1:
                                pe.wait_ge(s["ada_v"], 1)
                            for h in range(GH):
                                last = mm(bank4[4 + 2 * (c % 2)][:, h, :], X[:, c, h, :], U[:, c, h, :], start=True, stop=True)
                            last.then_inc(s["x_mm"], 1)
                            if li < LEVELS:
                                for h in range(GH):
                                    last = mm(bank4[5 + 2 * (c % 2)][:, h, :], U[:, c, h, :], X[:, c, h, :],
                                              start=True, stop=True)
                                last.then_inc(s["x_mm"], 1)

                    def wn(c):
                        pe.wait_ge(s["inv_v"], inv_after(LEVELS, c))
                        if c >= 2:
                            pe.wait_ge(s["wn_sb"], c - 1)
                        else:
                            pe.wait_ge(s["u_sb"], 4 * LEVELS)
                        for h in range(GH):
                            last = mm(bank4[2 + c % 2][:, h, :], kT[:, c, h, :], Y[:, c, h, :], start=True, stop=True)
                        last.then_inc(s["wn_mm"], 1)

                    def value(c):
                        pe.wait_ge(s["inv_v"], inv_after(LEVELS, CH - 1))
                        if c:
                            pe.wait_ge(s["wn_sb"], c + 1)
                            pe.wait_ge(s["state_v"], 4 * c)
                        for h in range(GH):
                            last = mm(bank4[4][:, h, :], Y[:, c, h, :], vT[:, c, h, :], start=True, stop=(c == 0))
                            if c:
                                last = mm(bank4[4][:, h, :], X[:, c, h, :], Sst[:, h, :], start=False, stop=True)
                        last.then_inc(s["vn_mm"], 1)

                    def state(c):
                        pe.wait_ge(s["vn_sb"], c + 1)
                        if c:
                            pe.wait_ge(s["on_v"], c)
                        for h in range(GH):
                            if c:
                                mm(bank4[5][:, h, :], qT[:, c, h, :], Sst[:, h, :], start=True, stop=False)
                            last = mm(bank4[5][:, h, :], at[:, c, h, :], vnew[:, h, :], start=(c == 0), stop=True)
                        last.then_inc(s["state_mm"], 1)
                        if c < CH - 1:
                            for h in range(GH):
                                last = mm(bank4[6][:, h, :], kdec[:, c, h, :], vnew[:, h, :], start=True, stop=True)
                            last.then_inc(s["state_mm"], 1)

                    def gdnout(c):
                        pe.wait_ge(s["on_v"], c + 1)
                        if c:
                            pe.wait_ge(s["gdn_done"], c)
                        for h in range(GH):
                            last = nc.tensor.transpose(bank4[7][:, h, :], on[:, h, :], ident)
                        last.then_inc(s["ot_mm"], 1)

                    def latsum():
                        pe.wait_ge(s["on_v"], CH)
                        for k in range(QL + KVL):
                            pe.wait_ge(s["lat_sq"], k + 1)
                            for c in range(CH):
                                last = mm(bank[5][:, k * 4 + c:k * 4 + c + 1], sqlat[:, k, c * P:(c + 1) * P], one,
                                          start=True, stop=True)
                        last.then_inc(s["lat_sum"], 1)

                    def latrow():
                        pe.wait_ge(s["lat_rec"], 1)
                        pe.wait_ge(s["gdn_done"], CH)
                        for g in range(2):
                            for c in range(CH):
                                last = row_of(bank[6 + g][:, c * P:(c + 1) * P], lrr[:, g * 4 + c:g * 4 + c + 1])
                            last.then_inc(s["lat_row"], 1)

                    def lrugate(j):
                        if j == 0:
                            pe.wait_ge(s["conv_step"], 64)
                            pe.wait_ge(s["vn_sb"], CH)
                        else:
                            pe.wait_ge(s["lru_sig"], 2 * j)
                        for g in range(2):
                            mm(bank[3 + g][:], wlru[:, j, g, :], lruu[:, j, :], start=True, stop=True).then_inc(s["lru_mm"], 1)

                    def rope(j):
                        pe.wait_ge(s["evict_a"], evict_n(rope_src(j)))
                        if ROPE_AT[j] >= 1:
                            pe.wait_ge(s["rope_v"], 3 * ROPE_AT[j] - 1)
                        else:
                            pe.wait_ge(s["lat_done"], QL + KVL)
                        src = kpe[:] if j == 4 else qpe[:, j, :]
                        mm(bank[7][:], CST[:, K_PERM:K_PERM + P], src, start=True, stop=True).then_inc(s["rope_mm"], 1)

                    def scores(n):
                        h, q = ATT[n]
                        nk = (q + 1) * P
                        b = bank[2 + n % 2]
                        if n == 0:
                            pe.wait_ge(s["evict_a"], evict_n(NSTREAM - 1))
                            pe.wait_ge(s["rope_v"], 15)
                            pe.wait_ge(s["lru_sig"], 8)
                        if n >= 2:
                            pe.wait_ge(s["exp_a"], n - 1)
                        pr = (h % 2) * 64
                        mm(b[:, 0:nk], qn[:, h, q * P:(q + 1) * P], kn[:, h, 0:nk], start=True, stop=False)
                        mm(b[:, 0:nk], qpe[pr:pr + 64, h // 2, q * P:(q + 1) * P], kpe[pr:pr + 64, 0:nk],
                           start=False, stop=False)
                        mm(b[:, q * P:nk], bf[:, 0, :], bf[:, 1, :], start=False, stop=True).then_inc(s["s_mm"], 1)

                    def turn(n):
                        h, q = ATT[n]
                        pe.wait_ge(s["soft2_v"], 2 * (n + 1))
                        if n >= 2:
                            wait_pt(pe, n - 2)
                        for k in range(q + 1):
                            last = nc.tensor.transpose(bank4[4 + n % 2][:, k, :], Pr[:, n % 3, k * P:(k + 1) * P], ident)
                        last.then_inc(s["t_mm"], 1)

                    def pv(h):
                        wait_pt(pe, 4 * h + 3)
                        wait_pt(pe, 4 * h + 2)
                        if h >= 2:
                            pe.wait_ge(s["mla_done"], h - 1)
                        b = bank[6 + h % 2]
                        for k in range(CH):
                            last = mm(b[:, k * P:], vtok[:, k, h * P:(h + 1) * P], PT[:, h % 2, k, k * P:],
                                      start=(k == 0), stop=(k == CH - 1))
                        last.then_inc(s["pv_mm"], 1)

                    def out(o):
                        if o >= 2:
                            pe.wait_ge(s["x_done"], o - 1)
                        if o == 0:
                            pe.wait_ge(s["mla_done"], MH)
                            pe.wait_ge(s["gdn_done"], CH)
                            pe.wait_ge(s["lru_v"], 24)
                        for half in range(2):
                            w = slot(SLOT_OUT + 2 * o + half)
                            for k in range(8):
                                last = mm(bank[o % 2][:], w[:, k * P:(k + 1) * P], mixed[:, half * 8 + k, :],
                                          start=(half == 0 and k == 0), stop=(half == 1 and k == 7))
                            last.then_inc(s["out_mm"], 1)
                            pe.wait_ge(s["out_mm"], 2 * o + half + 1)
                            pe.sem_inc(s["slot_used"], 1)

                    do = {"norm": norm, "gates": gates, "proj": proj, "decay": decay, "l2sum": l2sum, "l2row": l2row,
                          "ada": ada, "prep": prep, "first": first, "u": u, "x": x_, "wn": wn, "value": value, "state": state,
                          "gdnout": gdnout, "latsum": latsum, "latrow": latrow, "lrugate": lrugate, "rope": rope}
                    for name, *args in PLAN:
                        if name in do:
                            do[name](*args)
                    for n in range(len(ATT) + 3):
                        if n < len(ATT):
                            scores(n)
                        if 2 <= n < len(ATT) + 2:
                            turn(n - 2)
                        if n >= 3 and ATT[n - 3][1] == 3:
                            pv(ATT[n - 3][0])
                    for o in range(KD):
                        out(o)

                @block.scalar
                def _(act):
                    af = nc.scalar.activation

                    def norm():
                        for k in range(KD):
                            if k % 2 == 0:
                                continue
                            if k == 1:
                                act.wait_ge(s["small_in"], 48)
                            act.wait_ge(s["squared"], k)
                            af(hT[:, k, :], xT[:, k, :], ACT.Square).then_inc(s["squared"], 1)
                        act.wait_ge(s["norm_sqrt"], 1)
                        af(hs, hs, ACT.Sqrt, bias=epsc, scale=1.0 / D).then_inc(s["norm_sqrt"], 1)

                    def gates():
                        act.wait_ge(s["soft_v"], 1)
                        gb = bank[7][:, 64:96].rearrange("p (c n) -> p c n", c=CH)
                        af(eb.rearrange("p (c n) -> p c n", c=CH), gb[:, :, 0:4], ACT.Exp, scale=-1.0).then_inc(s["soft_a"], 1)
                        af(ealog, col[:, C_ALOG:C_ALOG + 4], ACT.Exp).then_inc(s["soft_a"], 1)
                        act.wait_ge(s["soft_v"], 3)
                        af(e1, az, ACT.Exp, scale=-1.0).then_inc(s["soft_a"], 1)
                        act.wait_ge(s["soft_v"], 4)
                        af(ln1, w1, ACT.Ln).then_inc(s["soft_a"], 1)

                    def decay():
                        for c in range(CH):
                            act.wait_ge(s["decay_mm"], 2 + c)
                            af(X[:, c], bank4[3 + c], ACT.Exp).then_inc(s["decay_a"], 1)
                        act.wait_ge(s["decay_v"], 6)
                        af(egl, gl, ACT.Exp).then_inc(s["decay_a"], 1)
                        af(egc, gcc, ACT.Exp).then_inc(s["decay_a"], 1)
                        af(ekd, kdx, ACT.Exp).then_inc(s["decay_a"], 1)
                        for c in range(CH):
                            act.wait_ge(s["decay_v"], 6 + 8 * c + 8)
                            if c >= 0:
                                pass
                            af(nA[:, c], nA[:, c], ACT.Exp, scale=-1.0).then_inc(s["decay_a"], 1)
                            af(at[:, c], at[:, c], ACT.Exp).then_inc(s["decay_a"], 1)

                    def proj(i):
                        b = bank[i % 2]
                        if i < GZ0:
                            act.wait_ge(s["conv_step"], 4 * (i + 1))
                            h = i % 4
                            dst = (kT, qT, vT)[i // 4][:, :, h, :]
                            af(dst, conv[:, i % 2, :].rearrange("p (c t) -> p c t", c=CH), ACT.Silu).then_inc(s["silu_done"], 1)
                            if i < V0:
                                act.wait_ge(s["silu_done"], i + 1)
                                af(mixed[:, 4 + i, :].rearrange("p (c t) -> p c t", c=CH), dst, ACT.Square
                                   ).then_inc(s["square_done"], 1)
                            return
                        if on_dve(i) and i < NPROJ:
                            return
                        act.wait_ge(s["proj_mm"], i + 1)
                        if GZ0 <= i < LX0:
                            af(mixed[:, i - GZ0, :], b[:], ACT.Silu).then_inc(s["evict_a"], 1)
                        elif LZ0 <= i < MQ0:
                            af(mixed[:, 12 + i - LZ0, :], b[:], ACT.Silu).then_inc(s["evict_a"], 1)
                        elif MQ0 <= i < MKR:
                            af(lat[:, i - MQ0, :], b[:], ACT.Copy).then_inc(s["evict_a"], 1)
                        elif i == MKR:
                            af(kpe[:], b[:], ACT.Copy).then_inc(s["evict_a"], 1)
                        elif i < NPROJ:
                            if i == MZ0:
                                act.wait_ge(s["l2_sum"], 2)
                            af(mixed[:, 4 + i - MZ0, :], b[:], ACT.Silu).then_inc(s["evict_a"], 1)
                        else:
                            if i == UQ0:
                                act.wait_ge(s["lru_v"], 24)
                                act.wait_ge(s["lat_sum"], 1)
                            if i < UQ0 + 8:
                                dst = qn[:, i - UQ0, :]
                            elif i < UK0:
                                dst = qpe[:, i - UQ0 - 8, :]
                            elif i < UV0:
                                dst = kn[:, i - UK0, :]
                            else:
                                half, c = divmod(i - UV0, CH)
                                dst = vtok[:, c, half * 512:(half + 1) * 512]
                            af(dst, b[:], ACT.Copy).then_inc(s["evict_a"], 1)

                    def l2sum(g):
                        act.wait_ge(s["l2_sum"], g + 1)
                        af(nrm[:, g * 16:g * 16 + 16], bank[2][:, 32 + g * 16:48 + g * 16], ACT.Sqrt, bias=epsc
                           ).then_inc(s["l2_sqrt"], 1)

                    def u(li, pair):
                        for c in (2 * pair, 2 * pair + 1):
                            n = 4 * (li - 1) + c
                            act.wait_ge(s["u_mm"], n + 1)
                            if li > 1:
                                act.wait_ge(s["x_mm"], x_mm_after(li - 1, c))
                            af(U[:, c], bank4[2 + c % 2], ACT.Copy).then_inc(s["u_sb"], 1)

                    def wn(c):
                        act.wait_ge(s["wn_mm"], c + 1)
                        af(X[:, c], bank4[2 + c % 2], ACT.Copy).then_inc(s["wn_sb"], 1)

                    def value(c):
                        act.wait_ge(s["vn_mm"], c + 1)
                        if c:
                            act.wait_ge(s["state_mm"], 2 * c)
                        af(vnew, bank4[4], ACT.Copy).then_inc(s["vn_sb"], 1)

                    def state(c):
                        act.wait_ge(s["state_mm"], 2 * c + 1)
                        for h in range(GH):
                            if 4 * c + h:
                                act.wait_ge(s["osq_a"], 4 * c + h)
                            af(scrS[:], bank4[5][:, h, :], ACT.Square, accum_out=ss[:, 4 * c + h:4 * c + h + 1]
                               ).then_inc(s["osq_a"], 1)

                    def latsum():
                        for k in range(QL + KVL):
                            act.wait_ge(s["evict_a"], evict_n(MQ0 + k))
                            if k == 0:
                                act.wait_ge(s["state_mm"], 7)
                            af(sqlat[:, k, :], lat[:, k, :], ACT.Square).then_inc(s["lat_sq"], 1)
                        act.wait_ge(s["lat_sqrt"], 2)
                        af(ls, ls, ACT.Sqrt, bias=epsc).then_inc(s["lat_sqrt"], 1)

                    def lrugate(j):
                        for g in range(2):
                            act.wait_ge(s["lru_mm"], 2 * j + g + 1)
                            cb = (C_BR, C_BI)[g] + j
                            if j == 0 and g == 0:
                                act.wait_ge(s["state_mm"], 7)
                            af((lr, li_)[g][:, j, :], bank[3 + g][:], ACT.Sigmoid, bias=col[:, cb:cb + 1]
                               ).then_inc(s["lru_sig"], 1)

                    def lruscan():
                        for j in range(LW):
                            act.wait_ge(s["lru_sig"], 2 * j + 1)
                            af(la[:, j, :], lr[:, j, :], ACT.Exp, scale=cpar[:, j:j + 1]).then_inc(s["lru_a"], 1)
                            act.wait_ge(s["lru_sig"], 8)
                            af(lr[:, j, :], lr[:, j, :], ACT.Tanh, scale=npar[:, j:j + 1]).then_inc(s["lru_a"], 1)
                        for j in range(LW):
                            act.wait_ge(s["lru_v"], 3 * (j + 1))
                            af(lm[:, j, :], lm[:, j, :], ACT.Sqrt).then_inc(s["lru_a"], 1)

                    do = {"norm": norm, "gates": gates, "proj": proj, "decay": decay, "l2sum": l2sum, "u": u, "wn": wn,
                          "value": value, "state": state, "latsum": latsum, "lrugate": lrugate, "lruscan": lruscan}
                    for name, *args in PLAN:
                        if name in do:
                            do[name](*args)
                    sc = float((128 + 64) ** -0.5)
                    for n in range(len(ATT) + 2):
                        if n < len(ATT):
                            h, q = ATT[n]
                            nk = (q + 1) * P
                            act.wait_ge(s["max_v"], 2 * (n + 1))
                            if n >= 3:
                                act.wait_ge(s["t_mm"], n - 2)
                            af(Pr[:, n % 3, 0:nk], bank[2 + n % 2][:, 0:nk], ACT.Exp, bias=mx[:, n % 4:n % 4 + 1], scale=sc,
                               accum_out=lsum[:, n % 4:n % 4 + 1]).then_inc(s["exp_a"], 1)
                        m = n - 2
                        if m >= 0 and PT_ON_ACT[m]:
                            h, q = ATT[m]
                            act.wait_ge(s["t_mm"], m + 1)
                            if h >= 2:
                                act.wait_ge(s["pv_mm"], h - 1)
                            af(pt_dst(m), bank4[4 + m % 2][:, 0:q + 1, :], ACT.Copy).then_inc(s["pt_a"], 1)

                @block.vector
                def _(dve):
                    v = nc.vector
                    n_of = {}

                    def step(name, ins, wait=False):
                        n_of[name] = n_of.get(name, 0) + 1
                        ins.then_inc(s[name], 1)
                        if wait:
                            dve.wait_ge(s[name], n_of[name])

                    def norm():
                        for k in range(0, KD, 2):
                            if k:
                                dve.wait_ge(s["squared"], k)
                            else:
                                dve.wait_ge(s["small_in"], 48)
                            v.tensor_tensor(hT[:, k, :], xT[:, k, :], xT[:, k, :], ALU.mult).then_inc(s["squared"], 1)
                        dve.wait_ge(s["norm_sum"], 1)
                        v.tensor_reduce(hs, bank[7][:, 0:32].rearrange("p (c k) -> p c k", c=CH), AX, ALU.add
                                        ).then_inc(s["norm_sqrt"], 1)
                        dve.wait_ge(s["norm_sqrt"], 2)
                        v.reciprocal(hr, hs).then_inc(s["norm_rec"], 1)
                        dve.wait_ge(s["norm_row"], 1)
                        for k in range(KD):
                            v.scalar_tensor_tensor(hT[:, k, :], xT[:, k, :], col[:, C_GAIN + k:C_GAIN + k + 1], bank[2][:],
                                                   ALU.mult, ALU.mult).then_inc(s["h_ready"], 1)

                    def gates():
                        dve.wait_ge(s["gates_mm"], 1)
                        gb = bank[7][:, 64:96].rearrange("p (c n) -> p c n", c=CH)
                        step("soft_v", v.tensor_tensor(z[:, 0:16].rearrange("p (c n) -> p c n", c=CH), gb[:, :, 4:8],
                                                       col[:, C_DT:C_DT + 4].unsqueeze(1).to_broadcast([P, CH, 4]), ALU.add))
                        step("soft_v", v.tensor_scalar(z[:, 16:20], col[:, C_AP:C_AP + 4], -1.0, None, ALU.mult), True)
                        step("soft_v", v.scalar_tensor_tensor(az, z, -1.0, z, ALU.mult, ALU.max))
                        dve.wait_ge(s["soft_a"], 3)
                        step("soft_v", v.tensor_scalar(w1, e1, 1.0, None, ALU.add), True)
                        step("soft_v", v.tensor_scalar(d1, w1, -1.0, None, ALU.add), True)
                        step("soft_v", v.tensor_scalar(i0, d1, 0.0, None, ALU.is_equal), True)
                        step("soft_v", v.tensor_tensor(d1, d1, i0, ALU.add), True)
                        step("soft_v", v.reciprocal(r1, d1), True)
                        dve.wait_ge(s["soft_a"], 4)
                        step("soft_v", v.tensor_tensor(sp, ln1, i0, ALU.add), True)
                        step("soft_v", v.tensor_tensor(sp, sp, e1, ALU.mult), True)
                        step("soft_v", v.tensor_tensor(sp, sp, r1, ALU.mult), True)
                        step("soft_v", v.scalar_tensor_tensor(sp, z, 0.0, sp, ALU.max, ALU.add), True)
                        step("soft_v", v.scalar_tensor_tensor(
                            g16.rearrange("p (c n) -> p c n", c=CH), sp[:, 0:16].rearrange("p (c n) -> p c n", c=CH), -1.0,
                            ealog.unsqueeze(1).to_broadcast([P, CH, 4]), ALU.mult, ALU.mult))
                        step("soft_v", v.tensor_scalar(cpar, sp[:, 16:20], -8.0, None, ALU.mult))
                        step("soft_v", v.tensor_scalar(npar, sp[:, 16:20], 8.0, None, ALU.mult))
                        step("soft_v", v.tensor_scalar(eb, eb, 1.0, None, ALU.add), True)
                        step("soft_v", v.reciprocal(beta, eb), True)
                        step("soft_v", v.tensor_scalar(nbeta, beta, -1.0, None, ALU.mult))

                    def decay():
                        dve.wait_ge(s["decay_mm"], 1)
                        step("decay_v", v.tensor_copy(gcc, bank[2][:, 0:16]))
                        for c in range(CH):
                            dve.wait_ge(s["decay_a"], 1 + c)
                            step("decay_v", v.tensor_copy(gl[:, 4 * c:4 * c + 4], bank4[3 + c][:, :, P - 1]), c == CH - 1)
                        step("decay_v", v.tensor_tensor(kdx, gl, gcc, ALU.subtract))
                        for c in range(CH):
                            for h in range(GH):
                                g = gcc[:, 4 * c + h:4 * c + h + 1]
                                step("decay_v", v.scalar_tensor_tensor(nA[:, c, h, :], bank4[3 + c][:, h, :], g,
                                                                       CST[:, K_BIG:K_BIG + P], ALU.subtract, ALU.add))
                                step("decay_v", v.scalar_tensor_tensor(at[:, c, h, :], bank4[3 + c][:, h, :], g,
                                                                       CST[:, K_BIGT:K_BIGT + P], ALU.subtract, ALU.add))
                        dve.wait_ge(s["decay_a"], 7)
                        dve.wait_ge(s["soft_v"], 18)
                        step("decay_v", v.tensor_tensor(nbe, nbeta, egc, ALU.mult), True)

                    def proj(i):
                        if not on_dve(i) or i >= NPROJ:
                            return
                        b = bank[i % 2]
                        m = count_before(i, True)
                        dve.wait_ge(s["proj_mm"], i + 1)
                        if i < GZ0:
                            if i >= 2:
                                dve.wait_ge(s["silu_done"], i - 1)
                            dst = conv[:, i % 2, :]
                            w = C_CONV + 4 * i
                            bias = None
                        else:
                            j = i - LX0
                            dst = lruu[:, j, :]
                            w = C_LCONV + 4 * j
                            bias = col[:, C_LB + j:C_LB + j + 1]
                        if bias is None:
                            v.tensor_scalar(dst, b[:], col[:, w + 3:w + 4], None, ALU.mult).then_inc(s["conv_step"], 1)
                        else:
                            v.tensor_scalar(dst, b[:], col[:, w + 3:w + 4], bias, ALU.mult, ALU.add).then_inc(s["conv_step"], 1)
                        for t in range(1, 4):
                            dve.wait_ge(s["conv_step"], 4 * m + t)
                            v.scalar_tensor_tensor(dst[:, t:], b[:, 0:S - t], col[:, w + 3 - t:w + 4 - t], dst[:, t:],
                                                   ALU.mult, ALU.add).then_inc(s["conv_step"], 1)

                    def l2sum(g):
                        dve.wait_ge(s["l2_sqrt"], g + 1)
                        if g == 0:
                            v.reciprocal(rn[:, 0:16], nrm[:, 0:16]).then_inc(s["l2_rec"], 1)
                        else:
                            step("soft_v", v.reciprocal(nrm[:, 16:32], nrm[:, 16:32]), True)
                            v.tensor_scalar(rn[:, 16:32], nrm[:, 16:32], float(P) ** -0.5, None, ALU.mult
                                            ).then_inc(s["l2_rec"], 1)

                    def l2row(g):
                        for c in range(CH):
                            dve.wait_ge(s["l2_row"], 4 * g + c + 1)
                            t = (kT, qT)[g]
                            v.tensor_tensor(t[:, c], t[:, c], bank4[3 + c], ALU.mult).then_inc(s["l2_done"], 1)

                    def bc(colv, c):
                        return colv[:, 4 * c:4 * c + 4].unsqueeze(2).to_broadcast([P, GH, P])

                    def prep(c):
                        dve.wait_ge(s["prep_mm"], 4 * c + 1)
                        dve.wait_ge(s["decay_a"], 15)
                        for h in range(GH):
                            step("prep_v", v.scalar_tensor_tensor(nA[:, c, h, :], bank4[2][:, h, :],
                                                                  nbeta[:, 4 * c + h:4 * c + h + 1], nA[:, c, h, :],
                                                                  ALU.mult, ALU.mult))
                        dve.wait_ge(s["prep_mm"], 4 * c + 2)
                        step("prep_v", v.tensor_tensor(at[:, c], bank4[3], at[:, c], ALU.mult))
                        dve.wait_ge(s["prep_mm"], 4 * c + 3)
                        step("prep_v", v.tensor_tensor(kT[:, c], bank4[4], bc(nbe, c), ALU.mult))
                        step("prep_v", v.tensor_tensor(kdec[:, c], bank4[4], bc(ekd, c), ALU.mult))
                        dve.wait_ge(s["prep_mm"], 4 * c + 4)
                        step("prep_v", v.tensor_tensor(vT[:, c], bank4[5], bc(beta, c), ALU.mult))
                        step("prep_v", v.tensor_tensor(qT[:, c], qT[:, c], X[:, c], ALU.mult), True)
                        idb = ident.unsqueeze(1).to_broadcast([P, GH, P])
                        step("prep_v", v.tensor_copy(X[:, c], idb))
                        step("prep_v", v.tensor_copy(Y[:, c], idb), True)

                    def mask(i):
                        return mk[:, i, :].unsqueeze(1).to_broadcast([P, GH, P])

                    def first(c):
                        step("inv_v", v.copy_predicated(X[:, c], mask(0), nA[:, c]))
                        dve.wait_ge(s["first_mm"], c + 1)
                        step("inv_v", v.copy_predicated(Y[:, c], mask(1), bank4[6]), True)

                    def x_(li, pair):
                        for c in (2 * pair, 2 * pair + 1):
                            done = x_mm_after(li, c)
                            dve.wait_ge(s["x_mm"], done if li == LEVELS else done - 1)
                            step("inv_v", v.copy_predicated(Y[:, c], mask(2 * li + 1), bank4[4 + 2 * (c % 2)]))
                            if li < LEVELS:
                                dve.wait_ge(s["x_mm"], done)
                                step("inv_v", v.copy_predicated(X[:, c], mask(2 * li), bank4[5 + 2 * (c % 2)]))
                        dve.wait_ge(s["inv_v"], n_of["inv_v"])

                    def adaout():
                        dve.wait_ge(s["ada_mm"], ADA_LAYER)
                        v.tensor_copy(mod[:, bass.ds(layer * ADA_LAYER, ADA_LAYER), :],
                                      bank[7][:, 0:2 * ADA_LAYER].rearrange("p (t n) -> p t n", n=2)).then_inc(s["ada_v"], 1)

                    def state(c):
                        dve.wait_ge(s["osq_a"], 4 * c + 4)
                        v.tensor_scalar(ss[:, 4 * c:4 * c + 4], ss[:, 4 * c:4 * c + 4], 1.0 / P, EPS, ALU.mult, ALU.add
                                        ).then_inc(s["osum_v"], 1)
                        if c < CH - 1:
                            dve.wait_ge(s["state_mm"], 2 * c + 2)
                            for h in range(GH):
                                if c == 0:
                                    step("state_v", v.tensor_copy(Sst[:, h, :], bank4[6][:, h, :]))
                                else:
                                    step("state_v", v.scalar_tensor_tensor(Sst[:, h, :], Sst[:, h, :],
                                                                           egl[:, 4 * c + h:4 * c + h + 1],
                                                                           bank4[6][:, h, :], ALU.mult, ALU.add))
                            dve.wait_ge(s["state_v"], n_of["state_v"])
                        dve.wait_ge(s["opow_p"], c + 1)
                        if c:
                            dve.wait_ge(s["ot_mm"], c)
                        v.tensor_tensor(on, bank4[5], bc(rs, c), ALU.mult).then_inc(s["on_v"], 1)

                    def gdnout(c):
                        dve.wait_ge(s["ot_mm"], c + 1)
                        if c == 0:
                            dve.wait_ge(s["evict_a"], evict_n(LX0 - 1))
                        m4 = mixed[:, 0:4, c * P:(c + 1) * P]
                        v.scalar_tensor_tensor(m4, bank4[7], col[:, C_ON:C_ON + 1], m4, ALU.mult, ALU.mult
                                               ).then_inc(s["gdn_done"], 1)

                    def latsum():
                        dve.wait_ge(s["lat_sum"], 1)
                        b = bank[5][:, 0:20].rearrange("p (k c) -> p c k", c=CH)
                        v.tensor_reduce(ls[:, 0:4], b[:, :, 0:3], AX, ALU.add).then_inc(s["lat_sum"], 1)
                        v.tensor_reduce(ls[:, 4:8], b[:, :, 3:5], AX, ALU.add).then_inc(s["lat_sum"], 1)
                        dve.wait_ge(s["lat_sum"], 3)
                        v.tensor_scalar(ls[:, 0:4], ls[:, 0:4], 1.0 / (QL * P), None, ALU.mult).then_inc(s["lat_sqrt"], 1)
                        v.tensor_scalar(ls[:, 4:8], ls[:, 4:8], 1.0 / (KVL * P), None, ALU.mult).then_inc(s["lat_sqrt"], 1)
                        dve.wait_ge(s["lat_sqrt"], 3)
                        v.reciprocal(lrr, ls).then_inc(s["lat_rec"], 1)

                    def latrow():
                        for k in range(QL + KVL):
                            g = k // QL
                            dve.wait_ge(s["lat_row"], g + 1)
                            c = C_QN + k if g == 0 else C_KVN + k - QL
                            v.scalar_tensor_tensor(lat[:, k, :], lat[:, k, :], col[:, c:c + 1], bank[6 + g][:], ALU.mult,
                                                   ALU.mult).then_inc(s["lat_done"], 1)

                    def lruscan():
                        for j in range(LW):
                            dve.wait_ge(s["lru_a"], 2 * j + 2)
                            step("lru_v", v.tensor_tensor(lm[:, j, :], la[:, j, :], la[:, j, :], ALU.mult), True)
                            step("lru_v", v.scalar_tensor_tensor(lm[:, j, :], lm[:, j, :], 1.0, lr[:, j, :], ALU.add, ALU.mult))
                            step("lru_v", v.tensor_tensor(li_[:, j, :], li_[:, j, :], lruu[:, j, :], ALU.mult), True)
                        for j in range(LW):
                            dve.wait_ge(s["lru_a"], 8 + j + 1)
                            step("lru_v", v.tensor_tensor(li_[:, j, :], li_[:, j, :], lm[:, j, :], ALU.mult), True)
                            step("lru_v", v.tensor_tensor_scan(lruu[:, j, :], la[:, j, :], li_[:, j, :], 0.0, ALU.mult,
                                                               ALU.add), True)
                            if j == 0:
                                dve.wait_ge(s["evict_a"], evict_n(MQ0 - 1))
                            step("lru_v", v.tensor_tensor(mixed[:, 12 + j, :], mixed[:, 12 + j, :], lruu[:, j, :], ALU.mult))
                        dve.wait_ge(s["lru_v"], n_of["lru_v"])

                    def rope(j):
                        t = kpe[:] if j == 4 else qpe[:, j, :]
                        dve.wait_ge(s["rope_mm"], ROPE_AT[j] + 1)
                        step("rope_v", v.tensor_tensor(t, t, CST[:, K_COS:K_COS + S], ALU.mult))
                        step("rope_v", v.tensor_tensor(ropet[:, 0, :], bank[7][:], CST[:, K_SIN:K_SIN + S], ALU.mult), True)
                        step("rope_v", v.tensor_tensor(t, t, ropet[:, 0, :], ALU.add), True)

                    do = {"norm": norm, "gates": gates, "proj": proj, "decay": decay, "l2sum": l2sum, "l2row": l2row,
                          "adaout": adaout, "prep": prep, "first": first, "x": x_, "state": state, "gdnout": gdnout, "latsum": latsum,
                          "latrow": latrow, "lruscan": lruscan, "rope": rope}
                    for name, *args in PLAN:
                        if name in do:
                            do[name](*args)
                    sc = float((128 + 64) ** -0.5)
                    for n in range(len(ATT) + 3):
                        if n < len(ATT):
                            h, q = ATT[n]
                            nk = (q + 1) * P
                            dve.wait_ge(s["s_mm"], n + 1)
                            mc = mx[:, n % 4:n % 4 + 1]
                            if n >= 4:
                                dve.wait_ge(s["exp_a"], n - 3)
                            step("max_v", v.tensor_reduce(mc, bank[2 + n % 2][:, 0:nk], AX, ALU.max), True)
                            step("max_v", v.tensor_scalar(mc, mc, -sc, None, ALU.mult))
                        m = n - 1
                        if 0 <= m < len(ATT):
                            nk = (ATT[m][1] + 1) * P
                            dve.wait_ge(s["exp_a"], m + 1)
                            step("soft2_v", v.reciprocal(rl[:, m % 4:m % 4 + 1], lsum[:, m % 4:m % 4 + 1]), True)
                            step("soft2_v", v.tensor_scalar(Pr[:, m % 3, 0:nk], Pr[:, m % 3, 0:nk], rl[:, m % 4:m % 4 + 1],
                                                            None, ALU.mult))
                        m = n - 2
                        if 0 <= m < len(ATT) and not PT_ON_ACT[m]:
                            h, q = ATT[m]
                            dve.wait_ge(s["t_mm"], m + 1)
                            if h >= 2:
                                dve.wait_ge(s["pv_mm"], h - 1)
                            step("pt_v", v.tensor_copy(pt_dst(m), bank4[4 + m % 2][:, 0:q + 1, :]))
                        if n >= 3 and ATT[n - 3][1] == 3:
                            h = ATT[n - 3][0]
                            dve.wait_ge(s["pv_mm"], h + 1)
                            if h == 0:
                                dve.wait_ge(s["evict_a"], evict_n(NPROJ - 1))
                            v.tensor_tensor(mixed[:, 4 + h, :], mixed[:, 4 + h, :], bank[6 + h % 2][:], ALU.mult
                                            ).then_inc(s["mla_done"], 1)
                    for o in range(KD):
                        dve.wait_ge(s["out_mm"], 2 * (o + 1))
                        v.tensor_tensor(xT[:, o, :], xT[:, o, :], bank[o % 2][:], ALU.add).then_inc(s["x_done"], 1)
                    dve.wait_ge(s["x_done"], KD)

                @block.gpsimd
                def _(pool):
                    for c in range(CH):
                        pool.wait_ge(s["osum_v"], c + 1)
                        nc.gpsimd.tensor_tensor(rs[:, 4 * c:4 * c + 4], ss[:, 4 * c:4 * c + 4],
                                                CST[:, K_MHALF:K_MHALF + 4], ALU.pow).then_inc(s["opow_p"], 1)

            nc.all_engine_barrier()
            with nc.Block() as block:
                @block.gpsimd
                def _(pool):
                    for one_sem in allsems:
                        pool.sem_clear(one_sem)
            nc.all_engine_barrier()


NC_ = 256
NT = NC_ + S
KT = NT // P
AH = 4
GD = 768
LAM0 = 0.8 - 0.6 * math.exp(-0.3 * 0)
NE = 64
TOPK = 8
DE = 256
EW = KD * 2 * DE
EW2 = 2 * D
MAXB = 96

DK0, DQ0, RK0, RQ0, RG0, DV0, RV0, WO0, SW1, SW3, SW2, NSLOT2 = 0, 4, 8, 10, 12, 16, 20, 24, 32, 34, 36, 40
RING2 = 4

B_FN, B_N1, B_N2, B_FN2, B_ADA, B_DN, B_RN, B_DEC, B_LAM, NCOL2 = (0, 8, 16, 24, 32, 80, 81, 82, 90, 90 + 256)

Z_PERM, Z_COS, Z_SIN, Z_DF, Z_MF, Z_DB, Z_MB, Z_CF, Z_CB, NCONST2 = (
    0, 128, 640, 1152, 2048, 2944, 3840, 4736, 5376, 6016)
FX, FC = 896, 640

R_IOTA, R_TRIS, R_ONES, R_BASE, R_J, R_TRIL, R_BIAS, NROUTE = 0, 128, 256, 384, 388, 389, 453, 453 + 64
FAR = 8192.0


def proj2_units():
    units = []
    for slot in range(DK0, DV0):
        units.append((slot, NC_, S))
        if slot < DQ0 or RK0 <= slot < RQ0:
            units.append((slot, 0, NC_))
    return units


UNITS = proj2_units()


def norm_helpers(nc, s, bank, epsc, one, ident, hs, hr, width):
    mm = nc.tensor.matmul

    def pe_part(pe, n, sq, chunks, row):
        for k in range(KD):
            pe.wait_ge(s["squared"], KD * n + k + 1)
            for c in range(chunks):
                last = mm(bank[7][:, c * 8 + k:c * 8 + k + 1], sq(k)[:, c * P:(c + 1) * P], one, start=True, stop=True)
        last.then_inc(s["norm_sum"], 1)
        pe.wait_ge(s["norm_rec"], n + 1)
        for c in range(chunks):
            last = mm(bank[row][:, c * P:(c + 1) * P], hr[:, c:c + 1].to_broadcast([P, P]), ident, start=True, stop=True)
        last.then_inc(s["norm_row"], 1)

    def act_part(act, n, src, sq, chunks):
        for k in range(1, KD, 2):
            act.wait_ge(s["squared"], KD * n + k)
            nc.scalar.activation(sq(k), src(k), ACT.Square).then_inc(s["squared"], 1)
        act.wait_ge(s["norm_sqrt"], 2 * n + 1)
        nc.scalar.activation(hs[:, 0:chunks], hs[:, 0:chunks], ACT.Sqrt, bias=epsc, scale=1.0 / width
                             ).then_inc(s["norm_sqrt"], 1)

    def dve_part(dve, n, src, sq, chunks):
        for k in range(0, KD, 2):
            if n or k:
                dve.wait_ge(s["squared"], KD * n + k)
            nc.vector.tensor_tensor(sq(k), src(k), src(k), ALU.mult).then_inc(s["squared"], 1)
        dve.wait_ge(s["norm_sum"], n + 1)
        nc.vector.tensor_reduce(hs[:, 0:chunks], bank[7][:, 0:8 * chunks].rearrange("p (c k) -> p c k", c=chunks), AX,
                                ALU.add).then_inc(s["norm_sqrt"], 1)
        dve.wait_ge(s["norm_sqrt"], 2 * n + 2)
        nc.vector.reciprocal(hr[:, 0:chunks], hs[:, 0:chunks]).then_inc(s["norm_rec"], 1)
        dve.wait_ge(s["norm_row"], n + 1)

    return pe_part, act_part, dve_part


def second_mixer(nc, stream2, ctx_in, cols2, const2, xT, CST, mod, hT, h2rows):
    ctx = ExitStack()
    with ctx:
        def sb(name, shape, dt=F32):
            return ctx.enter_context(nc.sbuf_tensor(name, shape, dt))

        def sem(name):
            return ctx.enter_context(nc.semaphore(name))

        ps = ctx.enter_context(nc.psum_tensor("ps2", [P, 8, 512], F32))
        bank = [ps[:, i, :] for i in range(8)]
        bank4 = [b.rearrange("p (h t) -> p h t", h=4) for b in bank]

        h2T = hT[:, :, NC_:NT]
        mixed = sb("mixed2", [P, 2 * AH, S])
        ring = sb("ring2", [P, RING2, SLOT])
        col = sb("col2", [P, NCOL2])
        rot = sb("rot2", [P, 1152])
        dk = sb("dk", [P, 4, NT])
        dq = sb("dq", [P, 4, S])
        dv = sb("dv", [P, KT, 512])
        rk = sb("rk", [P, 2, NT])
        rq = sb("rq", [P, 2, S])
        rv = sb("rv", [P, KT, 512])
        Fx = sb("Fx", [P, AH, FX])
        Fc = sb("Fc", [P, AH, FC])
        arena = sb("arena2", [P, 6144])
        tmp = sb("tmp2", [P, 2, FX])
        dist = arena[:, 0:NCONST2 - 1152]
        ctxT = dv[:].rearrange("p c n -> p (c n)")[:, 0:KD * NC_].rearrange("p (k t) -> p k t", k=KD)
        Pm = arena[:, 0:2 * GD].rearrange("p (m t) -> p m t", m=2)
        Pn = arena[:, 2 * GD:4 * GD].rearrange("p (m t) -> p m t", m=2)
        aT = arena[:, 4 * GD:4 * GD + KT * 512].rearrange("p (k t) -> p k t", k=KT)
        sr = arena[:, 0:1024].rearrange("p (b t) -> p b t", b=2)
        ropet = tmp[:, 0, 0:512]
        sm = sb("sm2", [P, 512])

        def small(at, n):
            return sm[:, at:at + n]

        hs, hr = small(0, 4), small(4, 4)
        gx, gc, g2n = small(8, 8), small(16, 8), small(24, 8)
        z, az, e1, w1, ln1, d1, i0, r1, sp = (small(32 + 8 * i, 8) for i in range(9))
        lg = small(104, 8)
        lamp = small(112, 2)
        nlam = small(114, 1)
        dn = small(115, 1)
        mx = small(116, 4)
        lsum = small(120, 4)
        rl = small(124, 4)
        ssn, rnn = small(128, 32), small(160, 32)
        lprod = small(192, 128)

        ident = CST[:, K_ID:K_ID + P]
        one = CST[:, K_ONE:K_ONE + 1]
        epsc = CST[:, K_EPS:K_EPS + 1]
        ZO = 1152

        s = {n: sem("b_" + n) for n in (
            "small_in ctx_in squared norm_sum norm_sqrt norm_rec norm_row x_ready mods h_scaled h_ready soft_v soft_a "
            "table_v table_a fc_v proj_mm evict_a evict_v dv_mm rope_mm rope_v s_mm max_v exp_a mix_v t_mm at_a pv_mm "
            "att_v ret_mm ret_v rv_mm sq_a hsum_mm hsum_a hsum_v hrow_mm head_v out_mm x_done turn_mm turn_v turn_a rows_out "
            "slot_used").split()}
        w_ready = [sem(f"b_w_ready{r}") for r in range(RING2)]

        pe_norm, act_norm, dve_norm = norm_helpers(nc, s, bank, epsc, one, ident, hs, hr, D)
        XT = lambda k: xT[:, k, :]
        XS = lambda k: hT[:, k, NC_:NT]
        CS = lambda k: hT[:, k, 0:NC_]
        CX = lambda k: ctxT[:, k, :]
        ITEMS = [(h, q) for h in range(AH) for q in range(CH)]
        RET = [(h, k) for h in range(AH) for k in range(KT)]
        ROPES = [("k", t) for t in range(4)] + [("q", t) for t in range(4)] + [("rk", t) for t in range(2)] + [
            ("rq", t) for t in range(2)]

        def rope_tile(n):
            kind, t = ROPES[n]
            src, first = {"k": (dk, NC_), "q": (dq, 0), "rk": (rk, NC_), "rq": (rq, 0)}[kind]
            return src[:, t, first:first + S]

        def rope_unit(n):
            kind, t = ROPES[n]
            slot = {"k": DK0, "q": DQ0, "rk": RK0, "rq": RQ0}[kind] + t
            return next(u for u, (sl, a, _) in enumerate(UNITS) if sl == slot and a == NC_)

        UP = len(UNITS)
        DVU, RVU = UP, UP + KT

        def rope(pe, n):
            wait_evicted(pe, rope_unit(n))
            if n:
                pe.wait_ge(s["rope_v"], 3 * n - 1)
            nc.tensor.matmul(bank[2], rot[:, 0:P], rope_tile(n), start=True, stop=True).then_inc(s["rope_mm"], 1)

        V_UNITS = 0

        def wait_evicted(eng, u):
            eng.wait_ge(s["evict_a"], u + 1)

        def pbuf(n):
            return Pm if n % 2 == 0 else Pn

        def ret_out(dve, step, v, h):
            dve.wait_ge(s["rv_mm"], KT * (h + 1))
            step("att_v", v.tensor_copy(dq[:, h, :], bank[4 + h % 2]))

        with nc.Block() as block:
            @block.sync
            def _(sp_):
                sp_.dma_start(col[:], cols2).then_inc(s["small_in"], 16)
                sp_.dma_start(ctxT.rearrange("p k t -> p (k t)"), ctx_in).then_inc(s["ctx_in"], 16)
                sp_.dma_start(rot[:], const2[:, 0:1152]).then_inc(s["small_in"], 16)
                sp_.dma_start(dist, const2[:, 1152:NCONST2]).then_inc(s["small_in"], 16)
                for r in range(RING2):
                    sp_.dma_start(ring[:, r, :], stream2[r]).then_inc(w_ready[r], 16)
                n_mixer = SW1
                with sp_.Fori(1, n_mixer // RING2) as i:
                    for r in range(RING2):
                        sp_.wait_ge(s["slot_used"], i * RING2 + (r + 1 - RING2))
                        sp_.dma_start(ring[:, r, :], stream2[bass.ds(i * RING2 + r, 1)].rearrange("a p n -> p (a n)")
                                      ).then_inc(w_ready[r], 16)
                for c in range(CH):
                    sp_.wait_ge(s["turn_v"], c + 1)
                    sp_.wait_ge(s["turn_a"], c + 1)
                    sp_.dma_start(h2rows[c * P:(c + 1) * P, :], mixed[:, 2 * c:2 * c + 2, :].rearrange("p a n -> p (a n)")
                                  ).then_inc(s["rows_out"], 16)
                sp_.wait_ge(s["rows_out"], 16 * CH)

            @block.tensor
            def _(pe):
                mm = nc.tensor.matmul
                held = []

                def slot(j):
                    pe.wait_ge(w_ready[j % RING2], 16 * (j // RING2 + 1))
                    return ring[:, j % RING2, :]

                def release(n_mm, name):
                    pe.wait_ge(s[name], n_mm)
                    pe.sem_inc(s["slot_used"], 1)

                pe_norm(pe, 0, XS, CH, 2)
                pe_norm(pe, 1, CS, NC_ // P, 3)
                pe_norm(pe, 2, XS, CH, 4)
                pe.wait_ge(s["h_ready"], 2 * KD)
                for u, (sl, a, n) in enumerate(UNITS):
                    if u >= 2:
                        wait_evicted(pe, u - 2)
                    w = slot(sl)
                    for k in range(KD):
                        last = mm(bank[u % 2][:, 0:n], w[:, k * P:(k + 1) * P], hT[:, k, a:a + n], start=(k == 0),
                                  stop=(k == KD - 1))
                    last.then_inc(s["proj_mm"], 1)
                    if u + 1 == UP or UNITS[u + 1][0] != sl:
                        release(u + 1, "proj_mm")
                    for n_r in range(len(ROPES)):
                        if rope_unit(n_r) == u - 1:
                            rope(pe, n_r)
                for n_r in range(len(ROPES)):
                    if rope_unit(n_r) >= UP - 1:
                        rope(pe, n_r)
                for g in range(2):
                    for j in range(4):
                        w = slot((DV0, RV0)[g] + j)
                        for t in range(KT):
                            if j == 0:
                                if g:
                                    pe.wait_ge(s["evict_v"], V_UNITS + t + 1)
                                elif t == 0:
                                    pe.wait_ge(s["rope_v"], 3 * len(ROPES))
                            for kk in range(2):
                                k = 2 * j + kk
                                last = mm(bank[2 + t], hT[:, k, t * P:(t + 1) * P], w[:, kk * 512:(kk + 1) * 512],
                                          start=(k == 0), stop=(k == KD - 1))
                            last.then_inc(s["dv_mm"], 1)
                        release(g * 24 + j * 6 + 6, "dv_mm")

                def scores(n):
                    h, q = ITEMS[n]
                    if n == 0:
                        pe.wait_ge(s["evict_v"], V_UNITS + 2 * KT)
                        wait_evicted(pe, UP - 1)
                        wait_evicted(pe, UP - 2)
                    for m in range(2):
                        if n:
                            pe.wait_ge(s["exp_a"], 2 * (n - 1) + m + 1)
                        r = slice(64 * m, 64 * m + 64)
                        mm(bank[2 + 2 * m][:, 0:512], dq[r, h, q * P:(q + 1) * P], dk[r, h, 0:512], start=True, stop=True)
                        mm(bank[3 + 2 * m][:, 0:256], dq[r, h, q * P:(q + 1) * P], dk[r, h, 512:768], start=True, stop=True
                           ).then_inc(s["s_mm"], 1)

                def turn(n):
                    pe.wait_ge(s["mix_v"], 4 * (n + 1))
                    if n:
                        pe.wait_ge(s["at_a"], 2 * n)
                    for k in range(KT):
                        last = nc.tensor.transpose(bank4[6 + k // 4][:, k % 4, :], pbuf(n)[:, 0, k * P:(k + 1) * P], ident)
                        if k == 3 or k == KT - 1:
                            last.then_inc(s["t_mm"], 1)

                def pv(h):
                    pe.wait_ge(s["at_a"], 8 * (h + 1))
                    if h >= 2:
                        pe.wait_ge(s["att_v"], h - 1)
                    for k in range(KT):
                        last = mm(bank[h % 2], dv[:, k, h * P:(h + 1) * P], aT[:, k, :], start=(k == 0), stop=(k == KT - 1))
                    last.then_inc(s["pv_mm"], 1)

                for n in range(len(ITEMS) + 2):
                    if n < len(ITEMS):
                        scores(n)
                    if 1 <= n <= len(ITEMS):
                        turn(n - 1)
                        if ITEMS[n - 1][1] == CH - 1:
                            pv(ITEMS[n - 1][0])
                for n in range(len(RET) + 1):
                    if n < len(RET):
                        h, k = RET[n]
                        if n == 0:
                            pe.wait_ge(s["exp_a"], 2 * len(ITEMS))
                        if n >= 2:
                            pe.wait_ge(s["ret_v"], n - 1)
                        r = slice(64 * (h % 2), 64 * (h % 2) + 64)
                        mm(bank[2 + n % 2], rk[r, h // 2, k * P:(k + 1) * P], rq[r, h // 2, :], start=True, stop=True
                           ).then_inc(s["ret_mm"], 1)
                    if n:
                        h, k = RET[n - 1]
                        pe.wait_ge(s["ret_v"], n)
                        if k == 0 and h >= 2:
                            pe.wait_ge(s["att_v"], AH + h - 1)
                        if k == 0 and h < 2:
                            pe.wait_ge(s["exp_a"], 2 * len(ITEMS))
                        mm(bank[4 + h % 2], rv[:, k, h * P:(h + 1) * P], sr[:, (n - 1) % 2, :], start=(k == 0),
                           stop=(k == KT - 1)).then_inc(s["rv_mm"], 1)
                pe.wait_ge(s["at_a"], 2 * len(ITEMS))
                for h in range(2 * AH):
                    pe.wait_ge(s["sq_a"], h + 1)
                    for c in range(CH):
                        last = mm(bank[7][:, 4 * h + c:4 * h + c + 1], hT[:, h, c * P:(c + 1) * P], one, start=True, stop=True)
                last.then_inc(s["hsum_mm"], 1)
                pe.wait_ge(s["hsum_v"], 1)
                for h in range(2 * AH):
                    if h >= 2:
                        pe.wait_ge(s["head_v"], h - 1 if h - 2 < AH else AH + 2 * (h - 2 - AH) + 1)
                    else:
                        pe.wait_ge(s["att_v"], 2 * AH)
                    for c in range(CH):
                        last = mm(bank[2 + h % 2][:, c * P:(c + 1) * P], rnn[:, 4 * h + c:4 * h + c + 1].to_broadcast([P, P]),
                                  ident, start=True, stop=True)
                    last.then_inc(s["hrow_mm"], 1)
                for o in range(KD):
                    if o >= 2:
                        pe.wait_ge(s["x_done"], o - 1)
                    w = slot(WO0 + o)
                    for k in range(KD):
                        if o == 0:
                            pe.wait_ge(s["head_v"], k + 1 if k < AH else AH + 2 * (k - AH + 1))
                        last = mm(bank[o % 2], w[:, k * P:(k + 1) * P], mixed[:, k, :], start=(k == 0), stop=(k == KD - 1))
                    last.then_inc(s["out_mm"], 1)
                    release(o + 1, "out_mm")
                pe_norm(pe, 3, XS, CH, 5)
                for c in range(CH):
                    pe.wait_ge(s["h_ready"], 3 * KD)
                    if c:
                        pe.wait_ge(s["turn_v"], c)
                        pe.wait_ge(s["turn_a"], c)
                    for k in range(KD):
                        last = nc.tensor.transpose(bank4[2 + k // 4][:, k % 4, :], h2T[:, k, c * P:(c + 1) * P], ident)
                        if k % 4 == 3:
                            last.then_inc(s["turn_mm"], 1)

            @block.scalar
            def _(act):
                af = nc.scalar.activation
                act.wait_ge(s["small_in"], 48)
                act_norm(act, 0, XT, XS, CH)
                act_norm(act, 1, CX, CS, NC_ // P)
                act_norm(act, 2, XT, XS, CH)
                for k in range(KD):
                    act.wait_ge(s["h_scaled"], k + 1)
                    act.wait_ge(s["mods"], 4)
                    af(CS(k), CS(k), ACT.Identity, bias=mod[:, k, 1:2]).then_inc(s["h_ready"], 1)
                for k in range(KD):
                    act.wait_ge(s["h_scaled"], KD + k + 1)
                    af(XS(k), XS(k), ACT.Identity, bias=mod[:, k, 0:1]).then_inc(s["h_ready"], 1)
                act.wait_ge(s["soft_v"], 2)
                af(e1, az, ACT.Exp, scale=-1.0).then_inc(s["soft_a"], 1)
                act.wait_ge(s["soft_v"], 3)
                af(ln1, w1, ACT.Ln).then_inc(s["soft_a"], 1)
                act.wait_ge(s["soft_v"], 15)
                af(lamp, lamp, ACT.Exp).then_inc(s["soft_a"], 1)

                def evict(u):
                    sl, a, n = UNITS[u]
                    act.wait_ge(s["proj_mm"], u + 1)
                    src = bank[u % 2][:, 0:n]
                    if sl < DQ0:
                        af(dk[:, sl - DK0, a:a + n], src, ACT.Copy).then_inc(s["evict_a"], 1)
                    elif sl < RK0:
                        af(dq[:, sl - DQ0, :], src, ACT.Copy).then_inc(s["evict_a"], 1)
                    elif sl < RQ0:
                        af(rk[:, sl - RK0, a:a + n], src, ACT.Copy).then_inc(s["evict_a"], 1)
                    elif sl < RG0:
                        af(rq[:, sl - RQ0, :], src, ACT.Copy).then_inc(s["evict_a"], 1)
                    else:
                        af(mixed[:, AH + sl - RG0, :], src, ACT.Silu).then_inc(s["evict_a"], 1)

                for u in range(UP):
                    evict(u)
                for h in range(AH):
                    for d in range(2):
                        i = 2 * h + d
                        act.wait_ge(s["table_v"], 3 * h + d + 1)
                        af(tmp[:, d, :], tmp[:, d, :], ACT.Exp).then_inc(s["table_a"], 1)
                    act.wait_ge(s["table_v"], 3 * (h + 1))
                    for d in range(2):
                        af((tmp[:, 0, 0:FC], tmp[:, 1, 0:FC])[d], dist[:, (Z_CF, Z_CB)[d] - ZO:(Z_CF, Z_CB)[d] - ZO + FC],
                           ACT.Exp, scale=lg[:, 4 * d + h:4 * d + h + 1]).then_inc(s["table_a"], 1)
                for n in range(len(ITEMS) + 1):
                    if n < len(ITEMS):
                        for m in range(2):
                            act.wait_ge(s["max_v"], 4 * n + 2 * m + 2)
                            if n >= 2:
                                act.wait_ge(s["t_mm"], 2 * (n - 1))
                            af(pbuf(n)[:, m, :], ps[:, 2 + 2 * m:4 + 2 * m, :].rearrange("p b t -> p (b t)")[:, 0:GD], ACT.Exp,
                               bias=mx[:, 2 * (n % 2) + m:2 * (n % 2) + m + 1], scale=0.125,
                               accum_out=lsum[:, 2 * (n % 2) + m:2 * (n % 2) + m + 1]).then_inc(s["exp_a"], 1)
                    if n:
                        h, q = ITEMS[n - 1]
                        for half in range(2):
                            act.wait_ge(s["t_mm"], 2 * (n - 1) + half + 1)
                            if h and q == 0 and half == 0:
                                act.wait_ge(s["pv_mm"], h)
                            kk = slice(0, 4) if half == 0 else slice(4, KT)
                            m = 4 if half == 0 else KT - 4
                            af(aT[:, kk, q * P:(q + 1) * P], bank4[6 + half][:, 0:m, :], ACT.Copy).then_inc(s["at_a"], 1)
                for h in range(2 * AH):
                    act.wait_ge(s["att_v"], h + 1)
                    src = mixed[:, h, :] if h < AH else dq[:, h - AH, :]
                    af(hT[:, h, 0:S], src, ACT.Square).then_inc(s["sq_a"], 1)
                act.wait_ge(s["hsum_mm"], 1)
                af(ssn, bank[7][:, 0:32], ACT.Sqrt, bias=epsc, scale=1.0 / P).then_inc(s["hsum_a"], 1)
                act_norm(act, 3, XT, XS, CH)
                for k in range(KD):
                    act.wait_ge(s["h_scaled"], 2 * KD + k + 1)
                    af(h2T[:, k, :], h2T[:, k, :], ACT.Identity, bias=mod[:, 24 + k, 0:1]).then_inc(s["h_ready"], 1)
                for c in range(CH):
                    act.wait_ge(s["turn_mm"], 2 * c + 2)
                    af(mixed[:, 2 * c + 1, :], bank[3], ACT.Copy).then_inc(s["turn_a"], 1)

            @block.vector
            def _(dve):
                v = nc.vector
                n_of = {}

                def step(name, ins, wait=False):
                    n_of[name] = n_of.get(name, 0) + 1
                    ins.then_inc(s[name], 1)
                    if wait:
                        dve.wait_ge(s[name], n_of[name])

                dve.wait_ge(s["small_in"], 48)
                dve_norm(dve, 0, XT, XS, CH)
                for k in range(KD):
                    step("x_ready", v.scalar_tensor_tensor(XT(k), XT(k), col[:, B_FN + k:B_FN + k + 1], bank[2], ALU.mult,
                                                           ALU.mult), k == KD - 1)
                dve.wait_ge(s["ctx_in"], 16)
                dve_norm(dve, 1, CX, CS, NC_ // P)
                for j in range(2):
                    step("mods", v.tensor_tensor(mod[:, :, j], mod[:, :, j], col[:, B_ADA:B_ADA + NADA], ALU.add), j == 1)
                step("mods", v.scalar_tensor_tensor(gx, mod[:, 8:16, 0], 1.0, col[:, B_N1:B_N1 + 8], ALU.add, ALU.mult))
                step("mods", v.scalar_tensor_tensor(gc, mod[:, 8:16, 1], 1.0, col[:, B_N1:B_N1 + 8], ALU.add, ALU.mult))
                step("mods", v.scalar_tensor_tensor(g2n, mod[:, 32:40, 0], 1.0, col[:, B_N2:B_N2 + 8], ALU.add, ALU.mult), True)
                for k in range(KD):
                    step("h_scaled", v.scalar_tensor_tensor(CS(k), CX(k), gc[:, k:k + 1], bank[3][:, 0:NC_], ALU.mult, ALU.mult))
                dve_norm(dve, 2, XT, XS, CH)
                for k in range(KD):
                    step("h_scaled", v.scalar_tensor_tensor(XS(k), XT(k), gx[:, k:k + 1], bank[4], ALU.mult, ALU.mult))
                step("soft_v", v.tensor_scalar(z, col[:, B_DEC:B_DEC + 8], -1.0, None, ALU.mult), True)
                step("soft_v", v.scalar_tensor_tensor(az, z, -1.0, z, ALU.mult, ALU.max))
                dve.wait_ge(s["soft_a"], 1)
                step("soft_v", v.tensor_scalar(w1, e1, 1.0, None, ALU.add), True)
                step("soft_v", v.tensor_scalar(d1, w1, -1.0, None, ALU.add), True)
                step("soft_v", v.tensor_scalar(i0, d1, 0.0, None, ALU.is_equal), True)
                step("soft_v", v.tensor_tensor(d1, d1, i0, ALU.add), True)
                step("soft_v", v.reciprocal(r1, d1), True)
                dve.wait_ge(s["soft_a"], 2)
                step("soft_v", v.tensor_tensor(sp, ln1, i0, ALU.add), True)
                step("soft_v", v.tensor_tensor(sp, sp, e1, ALU.mult), True)
                step("soft_v", v.tensor_tensor(sp, sp, r1, ALU.mult), True)
                step("soft_v", v.scalar_tensor_tensor(sp, z, 0.0, sp, ALU.max, ALU.add), True)
                step("soft_v", v.tensor_scalar(lg, sp, -1.0, None, ALU.mult))
                lp = col[:, B_LAM:B_LAM + 256].rearrange("p (a b n) -> p a b n", a=2, b=2)
                step("soft_v", v.tensor_tensor(lprod.rearrange("p (a n) -> p a n", a=2), lp[:, :, 0, :], lp[:, :, 1, :],
                                               ALU.mult), True)
                step("soft_v", v.tensor_reduce(lamp, lprod.rearrange("p (a n) -> p a n", a=2), AX, ALU.add))
                step("soft_v", v.tensor_scalar(dn, col[:, B_DN:B_DN + 1], 1 - LAM0, None, ALU.mult))
                dve.wait_ge(s["soft_a"], 3)
                step("soft_v", v.tensor_tensor(nlam, lamp[:, 1:2], lamp[:, 0:1], ALU.subtract), True)
                step("soft_v", v.tensor_scalar(nlam, nlam, -LAM0, None, ALU.add), True)

                def rope_v(n):
                    t = rope_tile(n)
                    dve.wait_ge(s["rope_mm"], n + 1)
                    step("rope_v", v.tensor_tensor(t, t, rot[:, 128:640], ALU.mult))
                    step("rope_v", v.tensor_tensor(ropet, bank[2], rot[:, 640:1152], ALU.mult), True)
                    step("rope_v", v.tensor_tensor(t, t, ropet, ALU.add), True)

                for n in range(len(ROPES)):
                    rope_v(n)
                for h in range(AH):
                    for d in range(2):
                        a, m = (Z_DF, Z_DB)[d] - ZO, (Z_MF, Z_MB)[d] - ZO
                        step("table_v", v.scalar_tensor_tensor(tmp[:, d, :], dist[:, a:a + FX], lg[:, 4 * d + h:4 * d + h + 1],
                                                               dist[:, m:m + FX], ALU.mult, ALU.add))
                    dve.wait_ge(s["table_a"], 4 * h + 2)
                    step("table_v", v.tensor_tensor(Fx[:, h, :], tmp[:, 0, :], tmp[:, 1, :], ALU.add))
                    dve.wait_ge(s["table_a"], 4 * h + 4)
                    step("fc_v", v.tensor_tensor(Fc[:, h, :], tmp[:, 0, 0:FC], tmp[:, 1, 0:FC], ALU.add), True)
                for g in range(2):
                    dst = (dv, rv)[g]
                    for t in range(KT):
                        dve.wait_ge(s["dv_mm"], g * 24 + 18 + t + 1)
                        step("evict_v", v.tensor_copy(dst[:, t, :], bank[2 + t]), t == KT - 1)
                for n in range(len(ITEMS) + 2):
                    if n < len(ITEMS):
                        for m in range(2):
                            c = 2 * (n % 2) + m
                            dve.wait_ge(s["s_mm"], 2 * n + m + 1)
                            step("max_v", v.tensor_reduce(mx[:, c:c + 1],
                                                          ps[:, 2 + 2 * m:4 + 2 * m, :].rearrange("p b t -> p (b t)")[:, 0:GD],
                                                          AX, ALU.max), True)
                            step("max_v", v.tensor_scalar(mx[:, c:c + 1], mx[:, c:c + 1], -0.125, None, ALU.mult))
                    if 1 <= n <= len(ITEMS):
                        m = n - 1
                        c = 2 * (m % 2)
                        b = pbuf(m)
                        dve.wait_ge(s["exp_a"], 2 * m + 2)
                        step("mix_v", v.reciprocal(rl[:, c:c + 2], lsum[:, c:c + 2]), True)
                        step("mix_v", v.tensor_tensor(rl[:, c + 1:c + 2], rl[:, c + 1:c + 2], nlam, ALU.mult), True)
                        step("mix_v", v.tensor_scalar(b[:, 1, :], b[:, 1, :], rl[:, c + 1:c + 2], None, ALU.mult), True)
                        step("mix_v", v.scalar_tensor_tensor(b[:, 0, :], b[:, 0, :], rl[:, c:c + 1], b[:, 1, :], ALU.mult,
                                                             ALU.add))
                    if n >= 2 and ITEMS[n - 2][1] == CH - 1 or n == len(ITEMS) + 1:
                        h = ITEMS[n - 2][0]
                        dve.wait_ge(s["pv_mm"], h + 1)
                        step("att_v", v.tensor_copy(mixed[:, h, :], bank[h % 2]))
                for n in range(len(RET)):
                    h, k = RET[n]
                    dve.wait_ge(s["ret_mm"], n + 1)
                    if n >= 2:
                        dve.wait_ge(s["rv_mm"], n - 1)
                    if n == 0:
                        dve.wait_ge(s["t_mm"], 2 * len(ITEMS))
                    w = Fc[:, h, P - k * P:P - k * P + S] if k < 2 else Fx[:, h, 384 - (k - 2) * P:384 - (k - 2) * P + S]
                    step("ret_v", v.scalar_tensor_tensor(sr[:, n % 2, :], bank[2 + n % 2], 0.125, w, ALU.mult, ALU.mult))
                    if n >= 1 and RET[n - 1][1] == KT - 1:
                        ret_out(dve, step, v, RET[n - 1][0])
                ret_out(dve, step, v, AH - 1)
                dve.wait_ge(s["hsum_a"], 1)
                step("hsum_v", v.reciprocal(rnn, ssn))
                for h in range(2 * AH):
                    dve.wait_ge(s["hrow_mm"], h + 1)
                    if h < AH:
                        step("head_v", v.scalar_tensor_tensor(mixed[:, h, :], mixed[:, h, :], dn, bank[2 + h % 2], ALU.mult,
                                                              ALU.mult))
                    else:
                        step("head_v", v.scalar_tensor_tensor(dq[:, h - AH, :], dq[:, h - AH, :], col[:, B_RN:B_RN + 1],
                                                              bank[2 + h % 2], ALU.mult, ALU.mult), True)
                        step("head_v", v.tensor_tensor(mixed[:, h, :], mixed[:, h, :], dq[:, h - AH, :], ALU.mult))
                for o in range(KD):
                    dve.wait_ge(s["out_mm"], o + 1)
                    step("x_done", v.scalar_tensor_tensor(xT[:, o, :], bank[o % 2], mod[:, 16 + o, 0:1], xT[:, o, :], ALU.mult,
                                                          ALU.add), o == KD - 1)
                dve.wait_ge(s["hrow_mm"], 8)
                dve_norm(dve, 3, XT, XS, CH)
                for k in range(KD):
                    step("h_scaled", v.scalar_tensor_tensor(h2T[:, k, :], XT(k), g2n[:, k:k + 1], bank[5], ALU.mult, ALU.mult))
                for c in range(CH):
                    dve.wait_ge(s["turn_mm"], 2 * c + 1)
                    step("turn_v", v.tensor_copy(mixed[:, 2 * c, :], bank[2]))

        nc.all_engine_barrier()
        with nc.Block() as block:
            @block.gpsimd
            def _(pool):
                for one_sem in list(s.values()) + w_ready:
                    pool.sem_clear(one_sem)
        nc.all_engine_barrier()


def experts(nc, stream2, route, router_w, cols2, up_w, down_w, xT, CST, mod, hT, h2rows, rows, out):
    ctx = ExitStack()
    with ctx:
        def sb(name, shape, dt=F32):
            return ctx.enter_context(nc.sbuf_tensor(name, shape, dt))

        def sem(name):
            return ctx.enter_context(nc.semaphore("c_" + name))

        ps = ctx.enter_context(nc.psum_tensor("ps3", [P, 8, 512], F32))
        bank = [ps[:, i, :] for i in range(8)]
        bank4 = [b.rearrange("p (h t) -> p h t", h=4) for b in bank]
        h2T = hT[:, :, NC_:NT]

        wup = sb("wup", [P, 2, EW])
        wdn = sb("wdn", [P, 2, EW2])
        shw = wup[:].rearrange("p a (b n) -> p (a b) n", n=SLOT)
        ytb = sb("ytb", [P, TOPK * D])
        rw = sb("router", [P, KD * NE])
        rc = sb("rc", [P, NROUTE])
        fn = sb("fn", [P, 8])
        scores, sel, selm, work, msk = (sb(n, [P, CH, NE]) for n in ("scores", "sel", "selm", "work", "msk"))
        m8 = sb("m8", [P, CH * 8, 8])
        cmp = sb("cmp", [P, CH * 64])
        cmp2 = sb("cmp2", [P, CH * 64])
        kidx = sb("kidx", [P, CH, NE])
        wts = sb("wts", [P, CH, NE])
        tab = sb("tab", [P, NE, CH, 3])
        s64 = sb("s64", [P, 4, NE])
        gsc = sb("gsc", [P, 32])
        rank = sb("rank", [P, 32])
        gneg = sb("gneg", [P, 32])
        top = sb("top", [P, CH, 8])
        wsum = sb("wsum", [P, 4])
        ej = sb("ej", [P, 1])
        erow = sb("erow", [1, P], I32)
        npair = sb("npair", [1, 2], I32)
        cur = sb("cur", [P, 2, CH, 3])
        hot = sb("hot", [P, 2, CH, P])
        iota = sb("iota", [P, P])
        dsti = sb("dsti", [P, 2], I32)
        toki = sb("toki", [P, 2], I32)
        sdst = sb("sdst", [P, 2], I32)
        wsl = sb("wsl", [P, 2])
        xb = sb("xb", [P, 2, D])
        xbT = sb("xbT", [P, 2, KD, P])
        sil = sb("sil", [P, 2, DE])
        g = sb("g", [P, 2, DE])
        gT = sb("gT", [P, 2, 2, P])
        y = sb("y", [P, 2, D])
        gs = sb("gs", [P, 2, S])
        hs, hr = sb("hs3", [P, 4]), sb("hr3", [P, 4])

        ident = CST[:, K_ID:K_ID + P]
        one = CST[:, K_ONE:K_ONE + 1]
        epsc = CST[:, K_EPS:K_EPS + 1]
        ones = rc[:, R_ONES:R_ONES + P]

        s = {n: sem(n) for n in (
            "may_gather may_scatter small_in shared_in logit_mm sig_a route_v pos_mm row_mm shup_mm shsil_a shg_v shdn_mm shx_v xb_v "
            "cpy_v cur_v hot_v info_mm idx_v xt_mm xt_a xt_v up_mm sil_a g_v gt_mm gt_a dn_mm y_a y_v "
            "acc_v acc_mm accx_v squared norm_sum norm_sqrt norm_rec norm_row fin_v out_done").split()}
        gather_in = [sem(f"gather_in{b}") for b in range(2)]
        scatter_out = [sem(f"scatter_out{b}") for b in range(2)]
        wup_in = [sem(f"wup_in{b}") for b in range(2)]
        wdn_in = [sem(f"wdn_in{b}") for b in range(2)]
        rows_in = [sem(f"rows_in{b}") for b in range(2)]
        N_MASK, N_EXPERT, N_ROUTE = 53, 74, 81

        def yt(c):
            return ytb if c % 2 else wup[:].rearrange("p a n -> p (a n)")

        pe_norm, act_norm, dve_norm = norm_helpers(nc, s, bank, epsc, one, ident, hs, hr, D)
        XT = lambda k: xT[:, k, :]
        XS = lambda k: h2T[:, k, :]

        with nc.Block() as block:
            @block.sync
            def _(sp):
                sp.dma_start(rc[:], route).then_inc(s["small_in"], 16)
                sp.dma_start(rw[:], router_w).then_inc(s["small_in"], 16)
                sp.dma_start(fn[:], cols2[:, B_FN2:B_FN2 + 8]).then_inc(s["small_in"], 16)
                for j in range(6):
                    sp.dma_start(shw[:, j, :], stream2[SW1 + j]).then_inc(s["shared_in"], 16)

                sp.wait_ge(s["route_v"], N_ROUTE)
                n = nc.sync.value_load(npair[0:1, 0:1], min_val=15, max_val=MAXB // 2 - 1) + 1
                sp.wait_ge(s["shup_mm"], 4)
                sp.wait_ge(s["shdn_mm"], KD)
                for b in range(2):
                    e = nc.sync.value_load(erow[0:1, b:b + 1], min_val=0, max_val=NE - 1)
                    sp.dma_start(wup[:, b, :], up_w[bass.ds(e, 1)].rearrange("a p n -> p (a n)")).then_inc(wup_in[b], 16)
                    sp.dma_start(wdn[:, b, :], down_w[bass.ds(e, 1)].rearrange("a p n -> p (a n)")).then_inc(wdn_in[b], 16)
                with sp.Fori(1, n) as i:
                    for b in range(2):
                        e = nc.sync.value_load(erow[0:1, bass.ds(i * 2 + b, 1)], min_val=0, max_val=NE - 1)
                        sp.wait_ge(s["up_mm"], i * 2 + (b - 1))
                        sp.dma_start(wup[:, b, :], up_w[bass.ds(e, 1)].rearrange("a p n -> p (a n)")).then_inc(wup_in[b], 16)
                        sp.wait_ge(s["dn_mm"], i * 4 + 2 * (b - 1))
                        sp.dma_start(wdn[:, b, :], down_w[bass.ds(e, 1)].rearrange("a p n -> p (a n)")).then_inc(wdn_in[b], 16)
                for b in range(2):
                    sp.wait_ge(scatter_out[b], n * 16)
                for c in range(CH):
                    if c >= 2:
                        sp.wait_ge(s["acc_mm"], KD * (c - 1))
                    sp.dma_start(yt(c)[:], rows[c * P * TOPK:(c + 1) * P * TOPK, :].rearrange("(p k) n -> p (k n)", k=TOPK)
                                 ).then_inc(rows_in[c % 2], 16)
                sp.wait_ge(s["fin_v"], KD)
                sp.dma_start(out.rearrange("p (k n) -> p k n", k=KD), h2T).then_inc(s["out_done"], 16)
                sp.wait_ge(s["out_done"], 16)

            def load_pairs(eng):
                eng.wait_ge(s["route_v"], N_ROUTE)
                last_i = eng.value_load(npair[0:1, 0:1], min_val=15, max_val=MAXB // 2 - 1)
                return last_i, last_i + 1

            @block.tensor
            def _(pe):
                mm = nc.tensor.matmul

                for c in range(CH):
                    if c == 0:
                        pe.wait_ge(s["small_in"], 48)
                    for k in range(KD):
                        last = mm(bank[0][:, c * NE:(c + 1) * NE], h2T[:, k, c * P:(c + 1) * P],
                                  rw[:, k * NE:(k + 1) * NE], start=(k == 0), stop=(k == KD - 1))
                last.then_inc(s["logit_mm"], 1)
                pe.wait_ge(s["shared_in"], 96)
                for t in range(4):
                    for k in range(KD):
                        last = mm(bank[1 + t], shw[:, t, k * P:(k + 1) * P], h2T[:, k, :], start=(k == 0), stop=(k == KD - 1))
                    last.then_inc(s["shup_mm"], 1)
                pe.wait_ge(s["route_v"], N_MASK)
                for c in range(CH):
                    mm(bank[7][:, c * NE:(c + 1) * NE], rc[:, R_TRIS:R_TRIS + P], msk[:, c, :], start=True, stop=(c == 0))
                    for c2 in range(c):
                        mm(bank[7][:, c * NE:(c + 1) * NE], ones, msk[:, c2, :], start=False, stop=(c2 == c - 1))
                for c in range(CH):
                    last = mm(bank[7][:, 256:256 + NE], ones, msk[:, c, :], start=(c == 0), stop=(c == CH - 1))
                last.then_inc(s["pos_mm"], 1)
                for o in range(KD):
                    if o == 0:
                        pe.wait_ge(s["shg_v"], 2)
                    if o >= 2:
                        pe.wait_ge(s["shx_v"], o - 1)
                    if o == 1:
                        pe.wait_ge(s["route_v"], N_EXPERT)
                        mm(bank[0][0:1, 0:P], ej[:], ident, start=True, stop=True).then_inc(s["row_mm"], 1)
                    for k in range(2):
                        w = shw[:, 4 + o // 4, (o % 4) * 256 + k * P:(o % 4) * 256 + (k + 1) * P]
                        last = mm(bank[5 + o % 2], w, gs[:, k, :], start=(k == 0), stop=(k == 1))
                    last.then_inc(s["shdn_mm"], 1)

                def info(i, u):
                    b = u % 2
                    pe.wait_ge(s["hot_v"], i * 10 + (5 * u + 4))
                    if type(i) is not int or i * 2 + u > 0:
                        pe.wait_ge(s["idx_v"], i * 6 + 3 * u)
                    for c in range(CH):
                        last = mm(bank[0][:, 0:2], hot[:, b, c, :], cur[:, b, c, 1:3], start=(c == 0), stop=(c == CH - 1))
                    last.then_inc(s["info_mm"], 1)

                def turn(i, u):
                    b = u % 2
                    pe.wait_ge(gather_in[b], i * 16 + 16 * (u // 2 + 1))
                    if type(i) is not int or i * 2 + u > 0:
                        pe.wait_ge(s["xt_a"], i * 2 + u)
                        pe.wait_ge(s["xt_v"], i * 2 + u)
                    for k in range(KD):
                        last = nc.tensor.transpose(bank4[1 + k // 4][:, k % 4, :], xb[:, b, k * P:(k + 1) * P], ident)
                        if k % 4 == 3:
                            last.then_inc(s["xt_mm"], 1)

                def up(i, u):
                    b = u % 2
                    pe.wait_ge(s["xt_a"], i * 2 + (u + 1))
                    pe.wait_ge(s["xt_v"], i * 2 + (u + 1))
                    pe.wait_ge(wup_in[b], i * 16 + 16 * (u // 2 + 1))
                    if type(i) is not int or i * 2 + u >= 2:
                        pe.wait_ge(s["g_v"], i * 2 + (u - 1))
                    for k in range(KD):
                        last = mm(bank[3 + b], xbT[:, b, k, :], wup[:, b, k * 512:(k + 1) * 512], start=(k == 0),
                                  stop=(k == KD - 1))
                    last.then_inc(s["up_mm"], 1)

                def turn_g(i, u):
                    b = u % 2
                    pe.wait_ge(s["g_v"], i * 2 + (u + 1))
                    if type(i) is not int or i * 2 + u > 0:
                        pe.wait_ge(s["gt_a"], i * 2 + u)
                    for k in range(2):
                        last = nc.tensor.transpose(bank4[5][:, k, :], g[:, b, k * P:(k + 1) * P], ident)
                    last.then_inc(s["gt_mm"], 1)

                def down(i, u):
                    b = u % 2
                    pe.wait_ge(s["gt_a"], i * 2 + (u + 1))
                    pe.wait_ge(wdn_in[b], i * 16 + 16 * (u // 2 + 1))
                    if type(i) is not int or i * 2 + u > 0:
                        pe.wait_ge(s["y_a"], i * 2 + u)
                        pe.wait_ge(s["y_v"], i * 2 + u)
                    for half in range(2):
                        for k in range(2):
                            last = mm(bank[6 + half], gT[:, b, k, :], wdn[:, b, k * D + half * 512:k * D + half * 512 + 512],
                                      start=(k == 0), stop=(k == 1))
                        last.then_inc(s["dn_mm"], 1)

                last_i, n = load_pairs(nc.tensor)
                pe.wait_ge(s["shg_v"], 2)
                pe.wait_ge(s["shx_v"], KD)
                info(0, 0)
                info(0, 1)
                turn(0, 0)
                up(0, 0)
                info(0, 2)
                turn(0, 1)
                with pe.Fori(0, last_i) as i:
                    for u in (1, 2):
                        up(i, u)
                        turn_g(i, u - 1)
                        info(i, u + 2)
                        turn(i, u + 1)
                        down(i, u - 1)
                up(last_i, 1)
                turn_g(last_i, 0)
                down(last_i, 0)
                turn_g(last_i, 1)
                down(last_i, 1)

                for c in range(CH):
                    pe.wait_ge(s["acc_v"], c + 1)
                    if c == 0:
                        pe.wait_ge(s["xt_a"], n * 2)
                        pe.wait_ge(s["xt_v"], n * 2)
                    else:
                        pe.wait_ge(s["accx_v"], KD * c)
                    for k in range(KD):
                        for m in range(4):
                            last = mm(bank4[1 + k // 4][:, k % 4, :], yt(c)[:, m * D + k * P:m * D + (k + 1) * P], ident,
                                      start=(m == 0), stop=(m == 3))
                        last.then_inc(s["acc_mm"], 1)
                pe_norm(pe, 0, XS, CH, 3)

            @block.scalar
            def _(act):
                af = nc.scalar.activation
                act.wait_ge(s["logit_mm"], 1)
                af(scores[:].rearrange("p c e -> p (c e)"), bank[0][:, 0:CH * NE], ACT.Sigmoid).then_inc(s["sig_a"], 1)
                for t in range(2):
                    act.wait_ge(s["shup_mm"], t + 1)
                    af(gs[:, t, :], bank[1 + t], ACT.Silu).then_inc(s["shsil_a"], 1)
                last_i, n = load_pairs(nc.scalar)

                def xt(i, u):
                    b = u % 2
                    act.wait_ge(s["xt_mm"], i * 4 + (2 * u + 1))
                    if type(i) is not int or i * 2 + u >= 2:
                        act.wait_ge(s["up_mm"], i * 2 + (u - 1))
                    af(xbT[:, b, 0:4, :], bank4[1], ACT.Copy).then_inc(s["xt_a"], 1)

                def silu(i, u):
                    b = u % 2
                    act.wait_ge(s["up_mm"], i * 2 + (u + 1))
                    if type(i) is not int or i * 2 + u >= 2:
                        act.wait_ge(s["g_v"], i * 2 + (u - 1))
                    af(sil[:, b, :], bank[3 + b][:, 0:DE], ACT.Silu).then_inc(s["sil_a"], 1)

                def gt(i, u):
                    b = u % 2
                    act.wait_ge(s["gt_mm"], i * 2 + (u + 1))
                    af(gT[:, b, :, :], bank4[5][:, 0:2, :], ACT.Copy).then_inc(s["gt_a"], 1)

                def yev(i, u):
                    b = u % 2
                    act.wait_ge(s["dn_mm"], i * 4 + (2 * u + 1))
                    if type(i) is not int or i * 2 + u >= 2:
                        act.wait_ge(scatter_out[b], i * 16 + 16 * (u // 2))
                    af(y[:, b, 0:512], bank[6], ACT.Copy).then_inc(s["y_a"], 1)

                xt(0, 0)
                silu(0, 0)
                xt(0, 1)
                with act.Fori(0, last_i) as i:
                    for u in (1, 2):
                        gt(i, u - 1)
                        silu(i, u)
                        xt(i, u + 1)
                        yev(i, u - 1)
                gt(last_i, 0)
                silu(last_i, 1)
                yev(last_i, 0)
                gt(last_i, 1)
                yev(last_i, 1)
                act_norm(act, 0, XT, XS, CH)

            @block.gpsimd
            def _(pool):
                last_i, n = load_pairs(nc.gpsimd)

                def gather(i, u):
                    b = u % 2
                    pool.wait_ge(s["idx_v"], i * 6 + 3 * (u + 1))
                    if type(i) is not int or i * 2 + u >= 2:
                        pool.wait_ge(s["xt_mm"], i * 4 + 2 * (u - 1))
                    pool.sem_inc(s["may_gather"], 1)
                    nc.gpsimd.indirect_dma_start(out=xb[:, b, :], out_offset=None, in_=h2rows,
                                                 in_offset=bass.IndirectOffsetOnAxis(ap=toki[:, b:b + 1], axis=0),
                                                 bounds_check=S - 1, oob_is_err=False).then_inc(gather_in[b], 16)

                def scatter(i, u):
                    b = u % 2
                    pool.wait_ge(s["y_a"], i * 2 + (u + 1))
                    pool.wait_ge(s["y_v"], i * 2 + (u + 1))
                    pool.wait_ge(s["cpy_v"], i * 2 + (u + 1))
                    pool.sem_inc(s["may_scatter"], 1)
                    nc.gpsimd.indirect_dma_start(out=rows, out_offset=bass.IndirectOffsetOnAxis(ap=sdst[:, b:b + 1], axis=0),
                                                 in_=y[:, b, :], in_offset=None,
                                                 bounds_check=S * TOPK - 1, oob_is_err=False).then_inc(scatter_out[b], 16)

                pool.wait_ge(s["xb_v"], 1)
                gather(0, 0)
                gather(0, 1)
                gather(0, 2)
                with pool.Fori(0, last_i) as i:
                    for u in (1, 2):
                        gather(i, u + 2)
                        scatter(i, u - 1)
                scatter(last_i, 0)
                scatter(last_i, 1)
                pool.wait_ge(gather_in[0], n * 16 + 16)

            @block.vector
            def _(dve):
                v = nc.vector
                n_of = {}

                def step(name, ins, wait=False):
                    n_of[name] = n_of.get(name, 0) + 1
                    ins.then_inc(s[name], 1)
                    if wait:
                        dve.wait_ge(s[name], n_of[name])

                R = lambda ins, wait=True: step("route_v", ins, wait)
                bias = rc[:, R_BIAS:R_BIAS + NE].unsqueeze(1).to_broadcast([P, CH, NE])
                step("xb_v", v.memset(xb[:], 0.0), True)
                dve.wait_ge(s["small_in"], 48)
                dve.wait_ge(s["sig_a"], 1)
                R(v.tensor_copy(iota[:], rc[:, R_IOTA:R_IOTA + P]), False)
                R(v.tensor_tensor(sel[:], scores[:], bias, ALU.add))
                for c in range(CH):
                    for q in range(8):
                        R(v.max(m8[:, 8 * c + q, :], sel[:, c, 8 * q:8 * q + 8]), c == CH - 1 and q == 7)
                R(v.tensor_tensor(gsc[:], m8[:, :, 0], m8[:, :, 1], ALU.add))
                g3 = gsc[:].rearrange("p (c q) -> p c q", c=CH)
                c3 = cmp[:].rearrange("p (c q r) -> p c q r", c=CH, q=8)
                c4 = cmp2[:].rearrange("p (c q r) -> p c q r", c=CH, q=8)
                other = g3.unsqueeze(2).to_broadcast([P, CH, 8, 8])
                own = g3.unsqueeze(3).to_broadcast([P, CH, 8, 8])
                tril = rc[:, R_TRIL:R_TRIL + 64].unsqueeze(1).to_broadcast([P, CH, 64])
                R(v.tensor_tensor(c3, other, own, ALU.is_gt), False)
                R(v.tensor_tensor(c4, other, own, ALU.is_equal))
                R(v.tensor_tensor(cmp2[:].rearrange("p (c n) -> p c n", c=CH), cmp2[:].rearrange("p (c n) -> p c n", c=CH),
                                  tril, ALU.mult))
                R(v.tensor_tensor(cmp[:], cmp[:], cmp2[:], ALU.add))
                R(v.tensor_reduce(rank[:], cmp[:].rearrange("p (q r) -> p q r", r=8), AX, ALU.add))
                R(v.tensor_scalar(rank[:], rank[:], 3.5, None, ALU.is_lt))
                R(v.tensor_scalar(gneg[:], rank[:], -1.0, 1e30, ALU.add, ALU.mult), False)
                sel8 = sel[:].rearrange("p c (q r) -> p (c q) r", r=8)
                selm8 = selm[:].rearrange("p c (q r) -> p (c q) r", r=8)
                R(v.tensor_tensor(selm8, sel8, rank[:].unsqueeze(2).to_broadcast([P, 32, 8]), ALU.mult))
                R(v.tensor_tensor(selm8, selm8, gneg[:].unsqueeze(2).to_broadcast([P, 32, 8]), ALU.add))
                for c in range(CH):
                    R(v.max(top[:, c, :], selm[:, c, :]), c == CH - 1)
                for c in range(CH):
                    R(v.match_replace(work[:, c, :], top[:, c, :], selm[:, c, :], -3e30), c == CH - 1)
                R(v.tensor_scalar(msk[:], work[:], -2e30, None, ALU.is_lt))
                assert n_of["route_v"] == N_MASK, n_of["route_v"]
                R(v.tensor_tensor(wts[:], scores[:], msk[:], ALU.mult))
                R(v.tensor_reduce(wsum[:], wts[:], AX, ALU.add))
                R(v.reciprocal(wsum[:], wsum[:]))
                R(v.tensor_scalar(wsum[:], wsum[:], 2.5, None, ALU.mult))
                R(v.tensor_tensor(tab[:, :, :, 2].rearrange("p e c -> p c e"), wts[:],
                                  wsum[:].unsqueeze(2).to_broadcast([P, CH, NE]), ALU.mult), False)
                for c in range(CH):
                    R(v.tensor_tensor_scan(kidx[:, c, :], ones[:, 0:NE], msk[:, c, :], 0.0, ALU.mult, ALU.add), c == CH - 1)
                R(v.tensor_tensor(kidx[:], kidx[:], msk[:], ALU.subtract))
                R(v.tensor_tensor(tab[:, :, :, 1].rearrange("p e c -> p c e"), kidx[:],
                                  rc[:, R_BASE:R_BASE + 4].unsqueeze(2).to_broadcast([P, CH, NE]), ALU.add), False)
                dve.wait_ge(s["pos_mm"], 1)
                cnt, nb, end, base = (s64[:, q, :] for q in range(4))
                R(v.tensor_copy(cnt, bank[7][:, 256:256 + NE]))
                R(v.tensor_scalar(nb, cnt, 0.5, None, ALU.is_gt))
                for q in range(1, 4):
                    R(v.scalar_tensor_tensor(nb, cnt, q * P + 0.5, nb, ALU.is_gt, ALU.add))
                R(v.tensor_tensor_scan(end, ones[:, 0:NE], nb, 0.0, ALU.mult, ALU.add))
                R(v.tensor_tensor(base, end, nb, ALU.subtract), False)
                R(v.tensor_scalar(cmp[:, 0:NE], end, rc[:, R_J:R_J + 1], None, ALU.is_le))
                R(v.tensor_reduce(ej[:], cmp[:, 0:NE], AX, ALU.add))
                R(v.tensor_scalar(ej[:], ej[:], NE - 1.0, None, ALU.min))
                assert n_of["route_v"] == N_EXPERT, n_of["route_v"]
                R(v.tensor_scalar(base, base, float(P), None, ALU.mult))
                R(v.tensor_tensor(kidx[:], bank[7][:, 0:CH * NE].rearrange("p (c e) -> p c e", c=CH),
                                  base.unsqueeze(1).to_broadcast([P, CH, NE]), ALU.add))
                R(v.scalar_tensor_tensor(kidx[:], kidx[:], 1.0, msk[:], ALU.add, ALU.mult))
                R(v.tensor_scalar(tab[:, :, :, 0].rearrange("p e c -> p c e"), kidx[:], -1.0, None, ALU.add))
                for t in range(2):
                    dve.wait_ge(s["shsil_a"], t + 1)
                    dve.wait_ge(s["shup_mm"], 3 + t)
                    step("shg_v", v.tensor_tensor(gs[:, t, :], gs[:, t, :], bank[3 + t], ALU.mult))
                dve.wait_ge(s["row_mm"], 1)
                R(v.tensor_copy(erow[:], bank[0][0:1, 0:P]), False)
                R(v.tensor_scalar(npair[0:1, 0:1], end[0:1, NE - 1:NE], -1.0, None, ALU.add))
                R(v.tensor_scalar(npair[0:1, 0:1], npair[0:1, 0:1], 1, None, ALU.arith_shift_right))
                assert n_of["route_v"] == N_ROUTE, n_of["route_v"]
                for o in range(KD):
                    dve.wait_ge(s["shdn_mm"], o + 1)
                    step("shx_v", v.scalar_tensor_tensor(xT[:, o, :], bank[5 + o % 2], mod[:, 40 + o, 0:1], xT[:, o, :],
                                                         ALU.mult, ALU.add), o == KD - 1)
                last_i, n = load_pairs(nc.vector)

                def hot_of(i, u):
                    b = u % 2
                    later = type(i) is not int or i * 2 + u >= 2
                    j = i * 2 + u
                    e = nc.vector.value_load(erow[0:1, bass.ds(j, 1)] if type(i) is not int else erow[0:1, j:j + 1],
                                             min_val=0, max_val=NE - 1)
                    if later:
                        dve.wait_ge(s["info_mm"], i * 2 + (u - 1))
                    v.tensor_copy(cur[:, b, :, :].unsqueeze(1), tab[:, bass.ds(e, 1), :, :]).then_inc(s["cur_v"], 1)
                    dve.wait_ge(s["cur_v"], i * 2 + (u + 1))
                    for c in range(CH):
                        v.tensor_scalar(hot[:, b, c, :], iota[:], cur[:, b, c, 0:1], None, ALU.is_equal).then_inc(s["hot_v"], 1)
                    v.tensor_scalar(iota[:], iota[:], float(P), None, ALU.add).then_inc(s["hot_v"], 1)
                    dve.wait_ge(s["hot_v"], i * 10 + 5 * (u + 1))

                def index(i, u):
                    b = u % 2
                    dve.wait_ge(s["info_mm"], i * 2 + (u + 1))
                    if type(i) is not int or i * 2 + u >= 2:
                        dve.wait_ge(gather_in[b], i * 16 + 16 * (u // 2))
                        dve.wait_ge(s["cpy_v"], i * 2 + (u - 1))
                        dve.wait_ge(s["g_v"], i * 2 + (u - 1))
                    v.tensor_scalar(dsti[:, b:b + 1], bank[0][:, 0:1], FAR, None, ALU.add).then_inc(s["idx_v"], 1)
                    v.tensor_copy(wsl[:, b:b + 1], bank[0][:, 1:2]).then_inc(s["idx_v"], 1)
                    dve.wait_ge(s["idx_v"], i * 6 + (3 * u + 1))
                    v.tensor_scalar(toki[:, b:b + 1], dsti[:, b:b + 1], 3, None, ALU.arith_shift_right).then_inc(s["idx_v"], 1)
                    dve.wait_ge(s["idx_v"], i * 6 + 3 * (u + 1))

                def xt(i, u):
                    b = u % 2
                    dve.wait_ge(s["xt_mm"], i * 4 + 2 * (u + 1))
                    if type(i) is not int or i * 2 + u >= 2:
                        dve.wait_ge(s["up_mm"], i * 2 + (u - 1))
                    v.tensor_copy(xbT[:, b, 4:8, :], bank4[2]).then_inc(s["xt_v"], 1)

                def gate(i, u):
                    b = u % 2
                    dve.wait_ge(s["sil_a"], i * 2 + (u + 1))
                    if type(i) is not int or i * 2 + u >= 2:
                        dve.wait_ge(s["gt_mm"], i * 2 + (u - 1))
                        dve.wait_ge(scatter_out[b], i * 16 + 16 * (u // 2))
                    v.tensor_copy(sdst[:, b:b + 1], dsti[:, b:b + 1]).then_inc(s["cpy_v"], 1)
                    v.scalar_tensor_tensor(g[:, b, :], bank[3 + b][:, DE:2 * DE], wsl[:, b:b + 1], sil[:, b, :], ALU.mult,
                                           ALU.mult).then_inc(s["g_v"], 1)

                def yev(i, u):
                    b = u % 2
                    dve.wait_ge(s["dn_mm"], i * 4 + 2 * (u + 1))
                    if type(i) is not int or i * 2 + u >= 2:
                        dve.wait_ge(scatter_out[b], i * 16 + 16 * (u // 2))
                    v.tensor_copy(y[:, b, 512:1024], bank[7]).then_inc(s["y_v"], 1)

                hot_of(0, 0)
                index(0, 0)
                hot_of(0, 1)
                index(0, 1)
                xt(0, 0)
                hot_of(0, 2)
                gate(0, 0)
                index(0, 2)
                xt(0, 1)
                with dve.Fori(0, last_i) as i:
                    for u in (1, 2):
                        hot_of(i, u + 2)
                        gate(i, u)
                        index(i, u + 2)
                        xt(i, u + 1)
                        yev(i, u - 1)
                gate(last_i, 1)
                yev(last_i, 0)
                yev(last_i, 1)

                for c in range(CH):
                    dve.wait_ge(rows_in[c % 2], 16 * (c // 2 + 1))
                    t = yt(c)
                    step("acc_v", v.tensor_tensor(t[:, 0:4 * D], t[:, 0:4 * D], t[:, 4 * D:8 * D], ALU.add))
                    for k in range(KD):
                        if k % 4 == 0:
                            dve.wait_ge(s["acc_mm"], KD * c + k + 4)
                        step("accx_v", v.scalar_tensor_tensor(xT[:, k, c * P:(c + 1) * P], bank4[1 + k // 4][:, k % 4, :],
                                                              mod[:, 40 + k, 0:1], xT[:, k, c * P:(c + 1) * P], ALU.mult,
                                                              ALU.add), c == CH - 1 and k == KD - 1)
                dve_norm(dve, 0, XT, XS, CH)
                for k in range(KD):
                    step("fin_v", v.scalar_tensor_tensor(h2T[:, k, :], XT(k), fn[:, k:k + 1], bank[3], ALU.mult, ALU.mult))

        nc.all_engine_barrier()


def tiled(w, cols):
    part = w[:, cols]
    n = part.shape[0] // P
    return np.ascontiguousarray(part.reshape(n, P, -1).transpose(1, 0, 2)).reshape(P, -1)


def span(a, n=P):
    return list(range(a, a + n))


def first_stream(i, l):
    w_in, w_uq, w_ukv, w_out = (i[n][l] for n in ("w_in", "mla_w_uq", "mla_w_ukv", "w_out"))
    slots = []
    at = {"q": 0, "k": 512, "v": 1024, "gz": 1544, "mq": 2056, "mkv": 2440, "mkr": 2696, "mz": 2760, "lx": 3784, "lz": 4296}
    for name, n in (("k", 4), ("q", 4), ("v", 4), ("gz", 4), ("lx", 4), ("lz", 4), ("mq", 3), ("mkv", 2)):
        slots += [tiled(w_in, span(at[name] + P * t)) for t in range(n)]
    slots.append(tiled(w_in, span(at["mkr"], 64) * 2))
    slots += [tiled(w_in, span(at["mz"] + P * t)) for t in range(8)]
    uq = [tiled(w_uq, span(192 * h)) for h in range(8)]
    uq += [tiled(w_uq, span(384 * j + 128, 64) + span(384 * j + 320, 64)) for j in range(4)]
    for t in range(6):
        slots.append(np.concatenate([uq[2 * t], uq[2 * t + 1], np.zeros((P, SLOT - 768), w_uq.dtype)], axis=1))
    uk = [tiled(w_ukv, span(256 * h)) for h in range(8)]
    slots += [np.concatenate(uk[4 * t:4 * t + 4], axis=1) for t in range(2)]
    for half in range(2):
        slots.append(tiled(w_ukv, sum((span(256 * (4 * half + h) + 128) for h in range(4)), [])))
    for o in range(8):
        for half in range(2):
            slots.append(tiled(w_out[1024 * half:1024 * half + 1024], span(P * o)))
    ada = [tiled(i["ada_w_2"][0], span(P * t)) for t in range(l * ADA_LAYER, (l + 1) * ADA_LAYER)]
    own = iter(slots)
    ordered = []
    for st in PLAN:
        if st[0] == "ada":
            ordered.append(ada[st[1]])
        elif st[0] == "proj" and SLOT_AT[st] == len(ordered):
            ordered.append(next(own))
    ordered += list(own)
    return np.stack(ordered)


def first_columns(i, l):
    def tiles(v):
        return np.asarray(v).reshape(-1, P).T

    def taps(w):
        return np.asarray(w).T.reshape(-1, P, 4).transpose(1, 0, 2).reshape(P, -1)

    cw = i["gdn_conv_w"][l]
    parts = [tiles(i["norm_gain"][l]), taps(np.concatenate([cw[:, 512:1024], cw[:, 0:512], cw[:, 1024:]], axis=1)),
             taps(i["lru_conv_w"][l]), tiles(i["lru_conv_b"][l]), tiles(i["lru_b_r"][l]), tiles(i["lru_b_i"][l]),
             tiles(i["lru_a_param"][l]), tiles(i["mla_q_norm"][l]), tiles(i["mla_kv_norm"][l]), tiles(i["gdn_out_norm"][l]),
             np.broadcast_to(i["gdn_a_log"][l], (P, 4)), np.broadcast_to(i["gdn_dt_bias"][l], (P, 4))]
    return np.concatenate(parts, axis=1)


def lru_blocks(i, l):
    out = np.zeros((P, LW, 2, P), np.float32)
    for g, name in enumerate(("lru_w_r", "lru_w_i")):
        w = i[name][l]
        for j in range(LW):
            for b in range(2):
                out[64 * b:64 * b + 64, j, g, 64 * b:64 * b + 64] = w[2 * j + b]
    return out.reshape(P, -1)


def constants():
    f = np.float32
    c = np.zeros((P, NCONST), f)
    r = np.arange(P)
    c[:, K_ID:K_ID + P] = np.eye(P)
    c[:, K_TRI:K_TRI + P] = r[:, None] <= r[None, :]
    c[:, K_BIG:K_BIG + P] = np.where(r[None, :] >= r[:, None], f(1e30), f(0))
    c[:, K_BIGT:K_BIGT + P] = np.where(r[None, :] < r[:, None], f(-1e30), f(0))
    perm = np.zeros((P, P), f)
    for m in range(P):
        if m % 64 < 32:
            perm[m + 32, m] = -1
        else:
            perm[m - 32, m] = 1
    c[:, K_PERM:K_PERM + P] = perm
    inv = (f(1) / (f(10000.0) ** (np.arange(0, 64, 2, dtype=f) / f(64)))).astype(f)
    ang = np.arange(S, dtype=f)[:, None] * inv[None, :]
    ang = np.concatenate([ang, ang, ang, ang], axis=1)
    c[:, K_COS:K_COS + S] = np.cos(ang).T
    c[:, K_SIN:K_SIN + S] = np.sin(ang).T
    c[:, K_ONE] = 1
    c[:, K_EPS] = EPS
    c[:, K_MHALF:] = -0.5
    masks = np.zeros((P, 2 * (LEVELS + 1) + 2, P), f)
    for li in range(LEVELS + 1):
        b = 1 << li
        m = (r[:, None] // (2 * b) == r[None, :] // (2 * b)) & (r[:, None] % (2 * b) >= b) & (r[None, :] % (2 * b) < b)
        masks[:, 2 * li], masks[:, 2 * li + 1] = m, m.T
    masks[:, -2] = np.eye(P)
    masks[:, -1] = np.where(r[None, :] > r[:, None], f(-1e30), f(0))
    return c, masks.reshape(P, -1)


def second_stream(i):
    w, wo, s1, s3, s2 = (i[n][0] for n in ("w_in_2", "w_out_2", "shared_w1_2", "shared_w3_2", "shared_w2_2"))
    slots = [tiled(w, span(512 + P * t)) for t in range(4)]
    slots += [tiled(w, span(P * t)) for t in range(4)]
    slots += [tiled(w, span(1792 + P * t)) for t in range(2)]
    slots += [tiled(w, span(1536 + P * t)) for t in range(2)]
    slots += [tiled(w, span(2560 + P * t)) for t in range(4)]
    for at in (1024, 2048):
        slots += [tiled(w[256 * j:256 * j + 256], span(at, 512)) for j in range(4)]
    slots += [tiled(wo, span(P * t)) for t in range(8)]
    for sw in (s1, s3):
        slots += [tiled(sw, span(P * t)) for t in range(2)]
    slots += [np.concatenate([tiled(s2, span(P * (4 * g + t))) for t in range(4)], axis=1) for g in range(2)]
    slots += [np.zeros_like(slots[0])] * 2
    return np.stack(slots)


def second_columns(i):
    def tiles(v):
        return np.asarray(v).reshape(-1, P).T

    lam = np.concatenate([i[n][0] for n in ("lambda_q1_2", "lambda_k1_2", "lambda_q2_2", "lambda_k2_2")])
    dec = np.concatenate([i["ret_decay_fwd_2"][0], i["ret_decay_bwd_2"][0]])
    parts = [tiles(i["final_norm"]), tiles(i["norm1_g_2"][0]), tiles(i["norm2_g_2"][0]), tiles(i["final_norm_g_2"]),
             tiles(i["ada_b_2"][0]), tiles(i["dattn_norm_g_2"][0]), tiles(i["ret_norm_g_2"][0]),
             np.broadcast_to(dec, (P, 8)), np.broadcast_to(lam, (P, 256))]
    return np.concatenate(parts, axis=1)


def expert_weights(i):
    w1, w3, w2 = (i[n][0] for n in ("exp_w1_2", "exp_w3_2", "exp_w2_2"))
    up = np.concatenate([w1, w3], axis=2).reshape(NE, KD, P, 2 * DE).transpose(0, 2, 1, 3).reshape(NE, P, EW)
    down = w2.reshape(NE, 2, P, D).transpose(0, 2, 1, 3).reshape(NE, P, EW2)
    return np.ascontiguousarray(up), np.ascontiguousarray(down)


def constants2():
    f = np.float32
    r = np.arange(P)
    c = np.zeros((P, NCONST2), f)
    for m in range(P):
        if m % 32 < 16:
            c[m + 16, Z_PERM + m] = -1
        else:
            c[m - 16, Z_PERM + m] = 1
    inv = (f(10000.0) ** (-np.arange(16, dtype=f) / f(16))).astype(f)
    t = np.arange(S)
    rows, colsn = (t // 64).astype(f), (t % 64).astype(f)
    ang = np.stack([rows[:, None] * inv, colsn[:, None] * inv], axis=1)
    ang = np.repeat(ang[:, :, None, :], 2, axis=2).reshape(S, 64)
    ang = np.concatenate([ang, ang], axis=1)
    c[:, Z_COS:Z_COS + S] = np.cos(ang).T
    c[:, Z_SIN:Z_SIN + S] = np.sin(ang).T
    d = np.arange(FX)[None, :] - 384 - r[:, None]
    c[:, Z_DF:Z_DF + FX] = np.maximum(d, 0)
    c[:, Z_MF:Z_MF + FX] = np.where(d < 0, f(-1e30), f(0))
    c[:, Z_DB:Z_DB + FX] = np.maximum(-d, 0)
    c[:, Z_MB:Z_MB + FX] = np.where(d > 0, f(-1e30), f(0))
    d = np.arange(FC)[None, :] - P - r[:, None]
    c[:, Z_CF:Z_CF + FC] = NC_ + d
    c[:, Z_CB:Z_CB + FC] = S - d
    return c


def routing_constants(i):
    f = np.float32
    r = np.arange(P)
    c = np.zeros((P, NROUTE), f)
    c[:, R_IOTA:R_IOTA + P] = r[None, :]
    c[:, R_TRIS:R_TRIS + P] = r[:, None] < r[None, :]
    c[:, R_ONES:R_ONES + P] = 1
    c[:, R_BASE:R_BASE + 4] = 8 * (128 * np.arange(4)[None, :] + r[:, None]) - FAR
    c[:, R_J] = r
    g = np.arange(8)
    c[:, R_TRIL:R_TRIL + 64] = (g[None, :] < g[:, None]).reshape(1, 64)
    c[:, R_BIAS:R_BIAS + 64] = np.broadcast_to(i["router_bias_2"][0], (P, NE))
    return c


def build(nc, x, ctx_in, cond_in, stream, cols, gates_w, lru_w, const, masks, stream2, cols2, const2, route, router_w,
          up_w, down_w, out):
    h2rows = nc.dram_tensor("h2rows", [S, D], F32, kind="Internal").ap()
    rows = nc.dram_tensor("expert_rows", [S * TOPK, D], F32, kind="Internal").ap()
    with ExitStack() as outer:
        xT = outer.enter_context(nc.sbuf_tensor("xT", [P, KD, S], F32))
        CST = outer.enter_context(nc.sbuf_tensor("CST", [P, NCONST], F32))
        mod = outer.enter_context(nc.sbuf_tensor("mod", [P, NADA, 2], F32))
        start_in = outer.enter_context(nc.semaphore("start_in"))
        with ExitStack() as first:
            cond = first.enter_context(nc.sbuf_tensor("cond", [P, KD, 2], F32))
            cond_raw = first.enter_context(nc.sbuf_tensor("cond_raw", [P, KD, 2], F32))
            mk = first.enter_context(nc.sbuf_tensor("mk", [P, 2 * (LEVELS + 1), P], U8))
            bf = first.enter_context(nc.sbuf_tensor("bf", [P, 2, P], BF16))
            staged = first.enter_context(ExitStack())
            masks_in = staged.enter_context(nc.sbuf_tensor("masks_in", [P, 2 * (LEVELS + 1) + 2, P], F32))
            with nc.Block() as block:
                @block.sync
                def _(sp):
                    sp.dma_start(cond_raw[:].rearrange("p k n -> p (k n)"), cond_in).then_inc(start_in, 16)
                    sp.dma_start(xT[:].rearrange("p k n -> p (k n)"), x).then_inc(start_in, 16)
                    sp.dma_start(CST[:], const).then_inc(start_in, 16)
                    sp.dma_start(masks_in[:].rearrange("p j n -> p (j n)"), masks).then_inc(start_in, 16)
                    sp.wait_ge(start_in, 64)

                @block.scalar
                def _(act):
                    act.wait_ge(start_in, 64)
                    nc.scalar.activation(cond[:], cond_raw[:], ACT.Silu)

                @block.vector
                def _(dve):
                    dve.wait_ge(start_in, 64)
                    nc.vector.tensor_copy(mk[:], masks_in[:, 0:2 * (LEVELS + 1), :])
                    nc.vector.tensor_copy(bf[:], masks_in[:, 2 * (LEVELS + 1):, :])
            nc.all_engine_barrier()
            staged.close()
            first_block(nc, stream, cols, gates_w, lru_w, mk, bf, xT, CST, cond, mod)
        hT = outer.enter_context(nc.sbuf_tensor("hT2", [P, KD, NT], F32))
        second_mixer(nc, stream2, ctx_in, cols2, const2, xT, CST, mod, hT, h2rows)
        experts(nc, stream2, route, router_w, cols2, up_w, down_w, xT, CST, mod, hT, h2rows, rows, out)


def by_channels(a):
    return np.ascontiguousarray(a.T.reshape(KD, P, -1).transpose(1, 0, 2)).reshape(P, -1)


def kernel(**inputs):
    import concourse.bacc as bacc
    from concourse.bass_utils import run_bass_kernel_spmd

    i = {name: np.asarray(value) for name, value in inputs.items()}
    const, masks = constants()
    up, down = expert_weights(i)
    arrays = {
        "x": by_channels(i["x"][0]),
        "ctx": by_channels(i["ctx_2"][0]),
        "cond": np.stack([i["c_2"][0].reshape(KD, P), i["c_ctx_2"].reshape(KD, P)]).transpose(2, 1, 0).reshape(P, -1),
        "stream": np.concatenate([first_stream(i, l) for l in range(L)]),
        "cols": np.stack([first_columns(i, l) for l in range(L)]),
        "gates_w": np.stack([tiled(i["w_in"][l], span(1536, 8)) for l in range(L)]),
        "lru_w": np.stack([lru_blocks(i, l) for l in range(L)]),
        "const": const,
        "masks": masks,
        "stream2": second_stream(i),
        "cols2": second_columns(i),
        "const2": constants2(),
        "route": routing_constants(i),
        "router_w": tiled(i["router_w_2"][0], span(0, NE)),
        "expert_up": up,
        "expert_down": down,
    }
    arrays = {f"in_{name}": np.ascontiguousarray(a) for name, a in arrays.items()}
    nc = bacc.Bacc("TRN2", target_bir_lowering=False, num_devices=1)
    args = [nc.dram_tensor(name, a.shape, mybir.dt.from_np(a.dtype), kind="ExternalInput").ap() for name, a in arrays.items()]
    out = nc.dram_tensor("out", [P, KD * S], F32, kind="ExternalOutput").ap()
    build(nc, *args, out)
    got = run_bass_kernel_spmd(nc, [arrays], core_ids=[0]).results[0]["out"]
    return np.ascontiguousarray(got.reshape(P, KD, S).transpose(2, 1, 0).reshape(1, S, D))
```

```python
import math
from contextlib import ExitStack

import numpy as np

import concourse.bass as bass
from concourse import mybir


P = 128
S = 512
D = 1024
KD = D // P
L = 2
CH = S // P
GH = 4
MH = 8
QL, KVL = 3, 2
LW = 4
NMIX = 16
RING = 4
SLOT = 1024
EPS = 1e-6

F32 = mybir.dt.float32
F32R = mybir.dt.float32r
BF16 = mybir.dt.bfloat16
U8 = mybir.dt.uint8
I32 = mybir.dt.int32
U32 = mybir.dt.uint32
ALU = mybir.AluOpType
ACT = mybir.ActivationFunctionType
AX = mybir.AxisListType.X

K0, Q0, V0, GZ0, LX0, LZ0, MQ0, MKV0, MKR, MZ0, NPROJ = 0, 4, 8, 12, 16, 20, 24, 27, 29, 30, 38
UQ0, UK0, UV0, NSTREAM = 38, 50, 58, 66
NADA = 48
ADA_LAYER = NADA // L
LEVELS = 6

C_GAIN, C_CONV, C_LCONV, C_LB, C_BR, C_BI, C_AP, C_QN, C_KVN, C_ON, C_ALOG, C_DT, NCOL = (
    0, 8, 56, 72, 76, 80, 84, 88, 91, 93, 94, 98, 102)

K_ID, K_TRI, K_BIG, K_BIGT, K_PERM, K_COS, K_SIN, K_ONE, K_EPS, K_MHALF, NCONST = (
    0, 128, 256, 384, 512, 640, 1152, 1664, 1665, 1666, 1666 + 16)


def slots_of(plan):
    at, n = {}, 0
    for st in plan:
        if st[0] == "ada":
            at[st] = n
            n += 1
        elif st[0] == "proj":
            i = st[1]
            if i < UQ0:
                at[st] = n
                n += 1
            else:
                group, first = (2, UQ0) if i < UK0 else (4, UK0) if i < UV0 else (CH, UV0)
                if (i - first) % group == 0:
                    n += 1
                at[st] = n - 1
    return at, n


def layer_plan():
    rest = iter(range(NPROJ))
    plan = [("norm",), ("proj", next(rest)), ("gates",), ("ada", 0)]

    def fill(n=1):
        plan.extend(("proj", next(rest)) for _ in range(n))

    fill()
    plan.append(("decay",))
    fill(2)
    plan.append(("l2sum", 0))
    fill()
    plan.append(("l2row", 0))
    fill(3)
    plan.append(("l2sum", 1))
    fill()
    plan.append(("l2row", 1))
    fill(4)
    for c in range(CH):
        plan.append(("prep", c))
        fill()
        plan.append(("first", c))
    for li in range(1, LEVELS + 1):
        plan += [("u", li, 0), ("u", li, 1)]
        fill()
        plan += [("x", li, 0), ("x", li, 1)]
    plan += [("wn", c) for c in range(CH)]
    for c in range(CH):
        plan.append(("value", c))
        fill()
        plan.append(("state", c))
        fill()
        plan.append(("gdnout", c))
    plan.append(("latsum",))
    plan.append(("lrugate", 0))
    plan.append(("lrugate", 1))
    fill()
    plan += [("latrow",), ("lrugate", 2), ("lrugate", 3)]
    plan += [("proj", i) for i in rest]
    spread, ada = [], iter(range(1, ADA_LAYER))
    for n, st in enumerate(plan):
        spread.append(st)
        if n >= 3 and st[0] in ("proj", "l2sum", "l2row", "prep", "decay") and not ("u", 1, 0) in spread:
            t = next(ada, None)
            if t is not None:
                spread.append(("ada", t))
    assert next(ada, None) is None
    spread.insert(spread.index(("u", 1, 0)), ("adaout",))
    plan = spread
    scan = iter([("lrudecay", j) for j in range(LW)] + [("lruscan", j) for j in range(LW)])
    for t in range(UQ0, UQ0 + 12):
        plan += [st for st in (next(scan, None),) if st]
        plan.append(("proj", t))
    plan.append(("rope", 4))
    for t in range(UK0, NSTREAM):
        plan.append(("proj", t))
        if t - UK0 < 4:
            plan.append(("rope", t - UK0))
    return plan


PLAN = layer_plan()
SLOT_AT, SLOT_OUT = slots_of(PLAN)
NSLOT = SLOT_OUT + 2 * KD
SPLIT_ORDER = list(range(4)) + list(range(12, 16)) + list(range(4, 12))
SPLIT_AT = {t: n for n, t in enumerate(SPLIT_ORDER)}
assert NSLOT % RING == 0


def on_dve(i):
    return i < GZ0 or LX0 <= i < LZ0


def count_before(i, dve):
    return sum(1 for t in range(i) if on_dve(t) == dve)


def first_block(nc, stream, cols, gates_w, lru_w, mk, bf, xT, CST, cond, mod):
    ctx = ExitStack()
    with ctx:
        def sb(name, shape, dt=F32):
            return ctx.enter_context(nc.sbuf_tensor(name, shape, dt))

        def sem(name):
            return ctx.enter_context(nc.semaphore(name))

        bank = [ctx.enter_context(nc.psum_tensor(f"bank{i}", [P, 512], F32)) for i in range(8)]
        bank4 = [b[:].rearrange("p (h t) -> p h t", h=4) for b in bank]

        def over(name, shape, offset):
            return nc.alloc_sbuf_tensor_at(name, shape, F32R, offset=offset)

        hT_at = nc.sbuf_base
        hT = sb("hT", [P, KD, S])
        mixed_at = nc.sbuf_base
        mixed = sb("mixed", [P, NMIX, S])
        lat = sb("lat", [P, QL + KVL, S])
        kpe = sb("kpe", [P, S])
        ring = sb("ring", [P, RING, SLOT])
        col = sb("col", [P, NCOL])
        wgate = sb("wgate", [P, KD, 8])
        wlru = sb("wlru", [P, LW, 2, P])
        arena_at = nc.sbuf_base
        arena = sb("arena", [P, 21 * 1024])
        lruu = sb("lruu", [P, LW, S])

        def part(at, n):
            return arena[:, at * 512:(at + n) * 512]

        def chunked(at):
            return part(at, 4).rearrange("p (c h t) -> p c h t", c=CH, h=GH)

        kT, qT, vT = chunked(0), chunked(4), chunked(8)
        nA, at, X, Y, kdec = chunked(12), chunked(16), chunked(20), chunked(24), chunked(28)
        U = chunked(32)
        conv = part(36, 2).rearrange("p (b t) -> p b t", b=2)
        Sst = part(38, 1).rearrange("p (h t) -> p h t", h=GH)
        vnew = part(39, 1).rearrange("p (h t) -> p h t", h=GH)
        on = part(40, 1).rearrange("p (h t) -> p h t", h=GH)
        scr = part(41, 1)
        lr = part(12, 4).rearrange("p (j t) -> p j t", j=LW)
        li_ = part(16, 4).rearrange("p (j t) -> p j t", j=LW)
        la = part(20, 4).rearrange("p (j t) -> p j t", j=LW)
        lm = part(24, 4).rearrange("p (j t) -> p j t", j=LW)
        sqlat = part(4, 5).rearrange("p (j t) -> p j t", j=5)
        qn = part(0, 8).rearrange("p (h t) -> p h t", h=MH)
        kn = part(8, 8).rearrange("p (h t) -> p h t", h=MH)
        qpe = part(16, 4).rearrange("p (j t) -> p j t", j=4)
        vtok = part(20, 8).rearrange("p (c n) -> p c n", c=CH)
        PT = part(28, 8).rearrange("p (b k t) -> p b k t", b=2, k=4)
        Pr = part(36, 3).rearrange("p (b t) -> p b t", b=3)
        ropet = part(39, 2).rearrange("p (b t) -> p b t", b=2)

        low = over("mixed_low", [P, NMIX, S], mixed_at)
        high_h = over("mixed_high", [P, KD, S], hT_at)
        high_q = over("mixed_high_heads", [P, MH, S], arena_at)
        high = [high_h[:, t, :] if t < 4 else high_q[:, t - 4, :] if t < 12 else high_h[:, t - 8, :] for t in range(NMIX)]
        wsplit = over("wsplit", [P, 2, 2, SLOT], arena_at + 8 * 512 * 4)

        sm = sb("sm", [P, 512])

        def small(at, n):
            return sm[:, at:at + n]

        z, az, e1, w1, ln1, d1, i0, r1, sp = (small(20 * i, 20) for i in range(9))
        beta, nbeta, nbe, egc, ekd, gcc, gl, egl, kdx, g16, eb = (small(180 + 16 * i, 16) for i in range(11))
        ealog = small(356, 4)
        nrm = small(360, 32)
        rn = small(392, 32)
        ss = small(424, 16)
        rs = small(440, 16)
        cpar, npar = small(456, 4), small(460, 4)
        mx = small(464, 4)
        lsum = small(468, 4)
        rl = small(472, 4)
        hs = small(476, 4)
        hr = small(480, 4)
        ls = small(484, 8)
        lrr = small(492, 8)
        scrS = sb("scrS", [P, 128])

        ident = CST[:, K_ID:K_ID + P]
        tri = CST[:, K_TRI:K_TRI + P]
        one = CST[:, K_ONE:K_ONE + 1]
        epsc = CST[:, K_EPS:K_EPS + 1]

        s = {n: sem(n) for n in (
            "small_in squared norm_sum norm_sqrt norm_rec norm_row h_ready gates_mm soft_v soft_a "
            "decay_mm decay_v decay_a proj_mm conv_step silu_done evict_a square_done l2_sum l2_sqrt l2_rec "
            "l2_row l2_done prep_mm prep_v first_mm inv_v u_mm u_sb x_mm wn_mm wn_sb vn_mm vn_sb state_mm "
            "state_v osq_a osum_v opow_p on_v ot_mm gdn_done ada_mm ada_v lat_sq lat_sum lat_sqrt lat_rec lat_row lat_done "
            "lru_mm lru_sig lru_a lru_v rope_mm rope_v s_mm max_v exp_a soft2_v t_mm pt_v pt_a pv_mm mla_done out_mm x_done "
            "slot_used high_p low_p w_high w_low").split()}
        w_ready = [sem(f"w_ready{r}") for r in range(RING)]
        allsems = list(s.values()) + w_ready

        def proj_emptied(eng, i):
            if i < NPROJ and on_dve(i):
                eng.wait_ge(s["conv_step"], 4 * (count_before(i, True) + 1))
            elif i < GZ0:
                raise AssertionError
            else:
                eng.wait_ge(s["evict_a"], i - count_before(min(i, NPROJ), True) + 1)

        def inv_after(li, c):
            return (8 * li + 2 * (c + 1)) if li < LEVELS else 8 * LEVELS + c + 1

        def x_mm_after(li, c):
            return 8 * (li - 1) + 2 * (c + 1) if li < LEVELS else 8 * (LEVELS - 1) + c + 1

        ATT = [(h, q) for h in range(MH) for q in range(CH)]

        ROPE_AT = {a[0]: n for n, a in enumerate([st[1:] for st in PLAN if st[0] == "rope"])}

        def rope_src(j):
            return MKR if j == 4 else UQ0 + 8 + j

        def evict_n(i):
            return i - count_before(min(i, NPROJ), True) + 1

        PT_ON_ACT = [n % 4 == 3 for n in range(len(ATT))]

        def wait_pt(eng, n):
            done = sum(1 for m in range(n + 1) if PT_ON_ACT[m] == PT_ON_ACT[n])
            eng.wait_ge(s["pt_a"] if PT_ON_ACT[n] else s["pt_v"], done)

        def pt_dst(n):
            h, q = ATT[n]
            return PT[:, h % 2, 0:q + 1, q * P:(q + 1) * P]

        with nc.Fori(0, L) as layer:
            with nc.Block() as block:

                @block.sync
                def _(sp_):
                    sp_.dma_start(col[:], cols[bass.ds(layer, 1)].rearrange("a p n -> p (a n)")).then_inc(s["small_in"], 16)
                    sp_.dma_start(wgate[:].rearrange("p k n -> p (k n)"),
                                  gates_w[bass.ds(layer, 1)].rearrange("a p n -> p (a n)")).then_inc(s["small_in"], 16)
                    sp_.dma_start(wlru[:].rearrange("p j g n -> p (j g n)"),
                                  lru_w[bass.ds(layer, 1)].rearrange("a p n -> p (a n)")).then_inc(s["small_in"], 16)
                    for r in range(RING):
                        sp_.dma_start(ring[:, r, :], stream[bass.ds(layer * NSLOT + r, 1)].rearrange("a p n -> p (a n)")
                                      ).then_inc(w_ready[r], 16)
                    with sp_.Fori(1, NSLOT // RING) as i:
                        for r in range(RING):
                            sp_.wait_ge(s["slot_used"], i * RING + (r + 1 - RING))
                            sp_.dma_start(ring[:, r, :],
                                          stream[bass.ds(layer * NSLOT + i * RING + r, 1)].rearrange("a p n -> p (a n)")
                                          ).then_inc(w_ready[r], 16)

                @block.tensor
                def _(pe):
                    mm = nc.tensor.matmul

                    def slot(j):
                        pe.wait_ge(w_ready[j % RING], 16 * (j // RING + 1))
                        return ring[:, j % RING, :]

                    owed = []

                    def release(ins):
                        if owed:
                            owed.pop()
                            ins.then_inc(s["slot_used"], 1)

                    def row_of(dst, colv):
                        return mm(dst, colv.to_broadcast([P, P]), ident, start=True, stop=True)

                    def norm():
                        for k in range(KD):
                            pe.wait_ge(s["squared"], k + 1)
                            for c in range(CH):
                                last = mm(bank[7][:, c * 8 + k:c * 8 + k + 1], hT[:, k, c * P:(c + 1) * P], one,
                                          start=True, stop=True)
                        last.then_inc(s["norm_sum"], 1)
                        pe.wait_ge(s["norm_rec"], 1)
                        for c in range(CH):
                            last = row_of(bank[2][:, c * P:(c + 1) * P], hr[:, c:c + 1])
                        last.then_inc(s["norm_row"], 1)

                    def gates():
                        pe.wait_ge(s["small_in"], 48)
                        for c in range(CH):
                            for k in range(KD):
                                last = mm(bank[7][:, 64 + c * 8:64 + c * 8 + 8], hT[:, k, c * P:(c + 1) * P],
                                          wgate[:, k, :], start=(k == 0), stop=(k == KD - 1))
                        last.then_inc(s["gates_mm"], 1)

                    def proj(i):
                        b = bank[i % 2]
                        if i >= 2:
                            proj_emptied(pe, i - 2)
                        if i < NPROJ:
                            w = slot(SLOT_AT[("proj", i)])
                            for k in range(KD):
                                if i == 0:
                                    pe.wait_ge(s["h_ready"], k + 1)
                                last = mm(b[:], w[:, k * P:(k + 1) * P], hT[:, k, :], start=(k == 0), stop=(k == KD - 1))
                                if k == 0:
                                    release(last)
                            used = True
                        elif i < UK0:
                            t = i - UQ0
                            pe.wait_ge(s["lat_done"], QL)
                            w = slot(SLOT_AT[("proj", i)])
                            for k in range(QL):
                                o = (t % 2) * QL * P + k * P
                                last = mm(b[:], w[:, o:o + P], lat[:, k, :], start=(k == 0), stop=(k == QL - 1))
                                if k == 0:
                                    release(last)
                            used = t % 2 == 1
                        elif i < UV0:
                            t = i - UK0
                            pe.wait_ge(s["lat_done"], QL + KVL)
                            w = slot(SLOT_AT[("proj", i)])
                            for k in range(KVL):
                                o = (t % 4) * KVL * P + k * P
                                last = mm(b[:], w[:, o:o + P], lat[:, QL + k, :], start=(k == 0), stop=(k == KVL - 1))
                                if k == 0:
                                    release(last)
                            used = t % 4 == 3
                        else:
                            half, c = divmod(i - UV0, CH)
                            w = slot(SLOT_AT[("proj", i)])
                            for k in range(KVL):
                                last = mm(b[:], lat[:, QL + k, c * P:(c + 1) * P], w[:, k * 512:(k + 1) * 512],
                                          start=(k == 0), stop=(k == KVL - 1))
                                if k == 0:
                                    release(last)
                            used = c == CH - 1
                        last.then_inc(s["proj_mm"], 1)
                        if used:
                            owed.append(i)

                    def ada(t):
                        if t == 0:
                            pe.wait_ge(s["soft_a"], 1)
                        w = slot(SLOT_AT[("ada", t)])
                        for k in range(KD):
                            last = mm(bank[7][:, 2 * t:2 * t + 2], w[:, k * P:(k + 1) * P], cond[:, k, :],
                                      start=(k == 0), stop=(k == KD - 1))
                            if k == 0:
                                release(last)
                        last.then_inc(s["ada_mm"], 1)
                        owed.append(t)

                    def decay():
                        pe.wait_ge(s["soft_v"], 13)
                        mm(bank[2][:, 0:16], tri, g16, start=True, stop=True).then_inc(s["decay_mm"], 1)
                        for c in range(CH):
                            for h in range(GH):
                                last = mm(bank4[3 + c][:, h, :], g16[:, c * 4 + h:c * 4 + h + 1].to_broadcast([P, P]), tri,
                                          start=True, stop=True)
                            last.then_inc(s["decay_mm"], 1)

                    def l2sum(g):
                        pe.wait_ge(s["square_done"], 4 * (g + 1))
                        pe.wait_ge(s["decay_v"], 1)
                        if g:
                            pe.wait_ge(s["l2_sqrt"], g)
                        for h in range(GH):
                            for c in range(CH):
                                o = 32 + g * 16 + c * 4 + h
                                last = mm(bank[2][:, o:o + 1], mixed[:, 4 + 4 * g + h, c * P:(c + 1) * P], one,
                                          start=True, stop=True)
                        last.then_inc(s["l2_sum"], 1)

                    def l2row(g):
                        pe.wait_ge(s["l2_rec"], g + 1)
                        if g == 0:
                            pe.wait_ge(s["decay_v"], 34)
                            pe.wait_ge(s["decay_a"], 4)
                        else:
                            pe.wait_ge(s["l2_done"], 4)
                        for c in range(CH):
                            for h in range(GH):
                                last = row_of(bank4[3 + c][:, h, :], rn[:, g * 16 + c * 4 + h:g * 16 + c * 4 + h + 1])
                            last.then_inc(s["l2_row"], 1)

                    def prep(c):
                        pe.wait_ge(s["l2_done"], CH + c + 1)
                        if c == 0:
                            pe.wait_ge(s["l2_done"], 2 * CH)
                            pe.wait_ge(s["silu_done"], 12)
                        else:
                            pe.wait_ge(s["prep_v"], 11 * (c - 1) + 8)
                        for h in range(GH):
                            last = mm(bank4[2][:, h, :], kT[:, c, h, :], kT[:, c, h, :], start=True, stop=True)
                        last.then_inc(s["prep_mm"], 1)
                        for h in range(GH):
                            last = mm(bank4[3][:, h, :], kT[:, c, h, :], qT[:, c, h, :], start=True, stop=True)
                        last.then_inc(s["prep_mm"], 1)
                        for h in range(GH):
                            last = nc.tensor.transpose(bank4[4][:, h, :], kT[:, c, h, :], ident)
                        last.then_inc(s["prep_mm"], 1)
                        for h in range(GH):
                            last = nc.tensor.transpose(bank4[5][:, h, :], vT[:, c, h, :], ident)
                        last.then_inc(s["prep_mm"], 1)

                    def first(c):
                        pe.wait_ge(s["prep_v"], 11 * c + 4)
                        if c >= 1:
                            pe.wait_ge(s["inv_v"], 2 * c)
                        for h in range(GH):
                            last = nc.tensor.transpose(bank4[6][:, h, :], nA[:, c, h, :], ident)
                        last.then_inc(s["first_mm"], 1)

                    def u(li, pair):
                        for c in (2 * pair, 2 * pair + 1):
                            n = 4 * (li - 1) + c
                            pe.wait_ge(s["inv_v"], inv_after(li - 1, CH - 1 if li == 1 else c))
                            if n >= 2:
                                pe.wait_ge(s["u_sb"], n - 1)
                            for h in range(GH):
                                last = mm(bank4[2 + c % 2][:, h, :], nA[:, c, h, :], Y[:, c, h, :], start=True, stop=True)
                            last.then_inc(s["u_mm"], 1)

                    def x_(li, pair):
                        for c in (2 * pair, 2 * pair + 1):
                            n = 4 * (li - 1) + c
                            pe.wait_ge(s["u_sb"], n + 1)
                            if c >= 2:
                                pe.wait_ge(s["inv_v"], inv_after(li, c - 2))
                            else:
                                pe.wait_ge(s["inv_v"], inv_after(li - 1, CH - 1 if li == 1 else c + 2))
                            if n == 1:
                                pe.wait_ge(s["ada_v"], 1)
                            for h in range(GH):
                                last = mm(bank4[4 + 2 * (c % 2)][:, h, :], X[:, c, h, :], U[:, c, h, :], start=True, stop=True)
                            last.then_inc(s["x_mm"], 1)
                            if li < LEVELS:
                                for h in range(GH):
                                    last = mm(bank4[5 + 2 * (c % 2)][:, h, :], U[:, c, h, :], X[:, c, h, :],
                                              start=True, stop=True)
                                last.then_inc(s["x_mm"], 1)

                    def wn(c):
                        pe.wait_ge(s["inv_v"], inv_after(LEVELS, c))
                        if c >= 2:
                            pe.wait_ge(s["wn_sb"], c - 1)
                        else:
                            pe.wait_ge(s["u_sb"], 4 * LEVELS)
                        for h in range(GH):
                            last = mm(bank4[2 + c % 2][:, h, :], kT[:, c, h, :], Y[:, c, h, :], start=True, stop=True)
                        last.then_inc(s["wn_mm"], 1)

                    def value(c):
                        pe.wait_ge(s["inv_v"], inv_after(LEVELS, CH - 1))
                        if c:
                            pe.wait_ge(s["wn_sb"], c + 1)
                            pe.wait_ge(s["state_v"], 4 * c)
                        for h in range(GH):
                            last = mm(bank4[4][:, h, :], Y[:, c, h, :], vT[:, c, h, :], start=True, stop=(c == 0))
                            if c:
                                last = mm(bank4[4][:, h, :], X[:, c, h, :], Sst[:, h, :], start=False, stop=True)
                        last.then_inc(s["vn_mm"], 1)

                    def state(c):
                        pe.wait_ge(s["vn_sb"], c + 1)
                        if c:
                            pe.wait_ge(s["on_v"], c)
                        for h in range(GH):
                            if c:
                                mm(bank4[5][:, h, :], qT[:, c, h, :], Sst[:, h, :], start=True, stop=False)
                            last = mm(bank4[5][:, h, :], at[:, c, h, :], vnew[:, h, :], start=(c == 0), stop=True)
                        last.then_inc(s["state_mm"], 1)
                        if c < CH - 1:
                            for h in range(GH):
                                last = mm(bank4[6][:, h, :], kdec[:, c, h, :], vnew[:, h, :], start=True, stop=True)
                            last.then_inc(s["state_mm"], 1)

                    def gdnout(c):
                        pe.wait_ge(s["on_v"], c + 1)
                        if c:
                            pe.wait_ge(s["gdn_done"], c)
                        for h in range(GH):
                            last = nc.tensor.transpose(bank4[7][:, h, :], on[:, h, :], ident)
                        last.then_inc(s["ot_mm"], 1)

                    def latsum():
                        pe.wait_ge(s["on_v"], CH)
                        for k in range(QL + KVL):
                            pe.wait_ge(s["lat_sq"], k + 1)
                            for c in range(CH):
                                last = mm(bank[5][:, k * 4 + c:k * 4 + c + 1], sqlat[:, k, c * P:(c + 1) * P], one,
                                          start=True, stop=True)
                        last.then_inc(s["lat_sum"], 1)

                    def latrow():
                        pe.wait_ge(s["lat_rec"], 1)
                        pe.wait_ge(s["gdn_done"], CH)
                        for g in range(2):
                            for c in range(CH):
                                last = row_of(bank[6 + g][:, c * P:(c + 1) * P], lrr[:, g * 4 + c:g * 4 + c + 1])
                            last.then_inc(s["lat_row"], 1)

                    def lrugate(j):
                        if j == 0:
                            pe.wait_ge(s["conv_step"], 64)
                            pe.wait_ge(s["vn_sb"], CH)
                        else:
                            pe.wait_ge(s["lru_sig"], 2 * j)
                        for g in range(2):
                            mm(bank[3 + g][:], wlru[:, j, g, :], lruu[:, j, :], start=True, stop=True).then_inc(s["lru_mm"], 1)

                    def rope(j):
                        pe.wait_ge(s["evict_a"], evict_n(rope_src(j)))
                        if ROPE_AT[j] >= 1:
                            pe.wait_ge(s["rope_v"], 3 * ROPE_AT[j] - 1)
                        else:
                            pe.wait_ge(s["lat_done"], QL + KVL)
                        src = kpe[:] if j == 4 else qpe[:, j, :]
                        mm(bank[7][:], CST[:, K_PERM:K_PERM + P], src, start=True, stop=True).then_inc(s["rope_mm"], 1)

                    def scores(n):
                        h, q = ATT[n]
                        nk = (q + 1) * P
                        b = bank[2 + n % 2]
                        if n == 0:
                            pe.wait_ge(s["evict_a"], evict_n(NSTREAM - 1))
                            pe.wait_ge(s["rope_v"], 15)
                            pe.wait_ge(s["lru_sig"], 8)
                        if n >= 2:
                            pe.wait_ge(s["exp_a"], n - 1)
                        pr = (h % 2) * 64
                        release(mm(b[:, 0:nk], qn[:, h, q * P:(q + 1) * P], kn[:, h, 0:nk], start=True, stop=False))
                        mm(b[:, 0:nk], qpe[pr:pr + 64, h // 2, q * P:(q + 1) * P], kpe[pr:pr + 64, 0:nk],
                           start=False, stop=False)
                        mm(b[:, q * P:nk], bf[:, 0, :], bf[:, 1, :], start=False, stop=True).then_inc(s["s_mm"], 1)

                    def turn(n):
                        h, q = ATT[n]
                        pe.wait_ge(s["soft2_v"], 2 * (n + 1))
                        if n >= 2:
                            wait_pt(pe, n - 2)
                        for k in range(q + 1):
                            last = nc.tensor.transpose(bank4[4 + n % 2][:, k, :], Pr[:, n % 3, k * P:(k + 1) * P], ident)
                        last.then_inc(s["t_mm"], 1)

                    def pv(h):
                        wait_pt(pe, 4 * h + 3)
                        wait_pt(pe, 4 * h + 2)
                        if h >= 2:
                            pe.wait_ge(s["mla_done"], h - 1)
                        b = bank[6 + h % 2]
                        for k in range(CH):
                            last = mm(b[:, k * P:], vtok[:, k, h * P:(h + 1) * P], PT[:, h % 2, k, k * P:],
                                      start=(k == 0), stop=(k == CH - 1))
                        last.then_inc(s["pv_mm"], 1)

                    def out(o):
                        if o >= 2:
                            pe.wait_ge(s["x_done"], o - 1)
                        for half in range(2):
                            n = 2 * o + half
                            pe.wait_ge(s["w_low"], n + 1)
                            wh, wl = (wsplit[:, n % 2, i, :] for i in range(2))
                            for k in range(8):
                                t = half * 8 + k
                                if o == 0:
                                    pe.wait_ge(s["low_p"], SPLIT_AT[t] + 1)
                                mh, ml = high[t], low[:, t, :]
                                c = slice(k * P, (k + 1) * P)
                                ins = mm(bank[o % 2][:], wh[:, c], mh, start=(half == 0 and k == 0), stop=False)
                                if k == 0:
                                    ins.then_inc(s["slot_used"], 1)
                                mm(bank[o % 2][:], wh[:, c], ml, start=False, stop=False)
                                last = mm(bank[o % 2][:], wl[:, c], mh, start=False, stop=(half == 1 and k == 7))
                            last.then_inc(s["out_mm"], 1)

                    do = {"norm": norm, "gates": gates, "proj": proj, "decay": decay, "l2sum": l2sum, "l2row": l2row,
                          "ada": ada, "prep": prep, "first": first, "u": u, "x": x_, "wn": wn, "value": value, "state": state,
                          "gdnout": gdnout, "latsum": latsum, "latrow": latrow, "lrugate": lrugate, "rope": rope}
                    for name, *args in PLAN:
                        if name in do:
                            do[name](*args)
                    for n in range(len(ATT) + 3):
                        if n < len(ATT):
                            scores(n)
                        if 2 <= n < len(ATT) + 2:
                            turn(n - 2)
                        if n >= 3 and ATT[n - 3][1] == 3:
                            pv(ATT[n - 3][0])
                    for o in range(KD):
                        out(o)

                @block.scalar
                def _(act):
                    af = nc.scalar.activation

                    def norm():
                        for k in range(KD):
                            if k % 2 == 0:
                                continue
                            if k == 1:
                                act.wait_ge(s["small_in"], 48)
                            act.wait_ge(s["squared"], k)
                            af(hT[:, k, :], xT[:, k, :], ACT.Square).then_inc(s["squared"], 1)
                        act.wait_ge(s["norm_sqrt"], 1)
                        af(hs, hs, ACT.Sqrt, bias=epsc, scale=1.0 / D).then_inc(s["norm_sqrt"], 1)

                    def gates():
                        act.wait_ge(s["soft_v"], 1)
                        gb = bank[7][:, 64:96].rearrange("p (c n) -> p c n", c=CH)
                        af(eb.rearrange("p (c n) -> p c n", c=CH), gb[:, :, 0:4], ACT.Exp, scale=-1.0).then_inc(s["soft_a"], 1)
                        af(ealog, col[:, C_ALOG:C_ALOG + 4], ACT.Exp).then_inc(s["soft_a"], 1)
                        act.wait_ge(s["soft_v"], 3)
                        af(e1, az, ACT.Exp, scale=-1.0).then_inc(s["soft_a"], 1)
                        act.wait_ge(s["soft_v"], 4)
                        af(ln1, w1, ACT.Ln).then_inc(s["soft_a"], 1)

                    def decay():
                        for c in range(CH):
                            act.wait_ge(s["decay_mm"], 2 + c)
                            af(X[:, c], bank4[3 + c], ACT.Exp).then_inc(s["decay_a"], 1)
                        act.wait_ge(s["decay_v"], 6)
                        af(egl, gl, ACT.Exp).then_inc(s["decay_a"], 1)
                        af(egc, gcc, ACT.Exp).then_inc(s["decay_a"], 1)
                        af(ekd, kdx, ACT.Exp).then_inc(s["decay_a"], 1)
                        for c in range(CH):
                            act.wait_ge(s["decay_v"], 6 + 8 * c + 8)
                            af(nA[:, c], nA[:, c], ACT.Exp, scale=-1.0).then_inc(s["decay_a"], 1)
                            af(at[:, c], at[:, c], ACT.Exp).then_inc(s["decay_a"], 1)

                    def proj(i):
                        b = bank[i % 2]
                        if i < GZ0:
                            act.wait_ge(s["conv_step"], 4 * (i + 1))
                            h = i % 4
                            dst = (kT, qT, vT)[i // 4][:, :, h, :]
                            af(dst, conv[:, i % 2, :].rearrange("p (c t) -> p c t", c=CH), ACT.Silu).then_inc(s["silu_done"], 1)
                            if i < V0:
                                act.wait_ge(s["silu_done"], i + 1)
                                af(mixed[:, 4 + i, :].rearrange("p (c t) -> p c t", c=CH), dst, ACT.Square
                                   ).then_inc(s["square_done"], 1)
                            return
                        if on_dve(i) and i < NPROJ:
                            return
                        act.wait_ge(s["proj_mm"], i + 1)
                        if GZ0 <= i < LX0:
                            af(mixed[:, i - GZ0, :], b[:], ACT.Silu).then_inc(s["evict_a"], 1)
                        elif LZ0 <= i < MQ0:
                            af(mixed[:, 12 + i - LZ0, :], b[:], ACT.Silu).then_inc(s["evict_a"], 1)
                        elif MQ0 <= i < MKR:
                            af(lat[:, i - MQ0, :], b[:], ACT.Copy).then_inc(s["evict_a"], 1)
                        elif i == MKR:
                            af(kpe[:], b[:], ACT.Copy).then_inc(s["evict_a"], 1)
                        elif i < NPROJ:
                            if i == MZ0:
                                act.wait_ge(s["l2_sum"], 2)
                            af(mixed[:, 4 + i - MZ0, :], b[:], ACT.Silu).then_inc(s["evict_a"], 1)
                        else:
                            if i == UQ0:
                                act.wait_ge(s["lat_sum"], 1)
                            if i == UQ0 + 8:
                                act.wait_ge(s["lru_v"], 24)
                            if i < UQ0 + 8:
                                dst = qn[:, i - UQ0, :]
                            elif i < UK0:
                                dst = qpe[:, i - UQ0 - 8, :]
                            elif i < UV0:
                                dst = kn[:, i - UK0, :]
                            else:
                                half, c = divmod(i - UV0, CH)
                                dst = vtok[:, c, half * 512:(half + 1) * 512]
                            af(dst, b[:], ACT.Copy).then_inc(s["evict_a"], 1)

                    def l2sum(g):
                        act.wait_ge(s["l2_sum"], g + 1)
                        af(nrm[:, g * 16:g * 16 + 16], bank[2][:, 32 + g * 16:48 + g * 16], ACT.Sqrt, bias=epsc
                           ).then_inc(s["l2_sqrt"], 1)

                    def u(li, pair):
                        for c in (2 * pair, 2 * pair + 1):
                            n = 4 * (li - 1) + c
                            act.wait_ge(s["u_mm"], n + 1)
                            if li > 1:
                                act.wait_ge(s["x_mm"], x_mm_after(li - 1, c))
                            af(U[:, c], bank4[2 + c % 2], ACT.Copy).then_inc(s["u_sb"], 1)

                    def wn(c):
                        act.wait_ge(s["wn_mm"], c + 1)
                        af(X[:, c], bank4[2 + c % 2], ACT.Copy).then_inc(s["wn_sb"], 1)

                    def value(c):
                        act.wait_ge(s["vn_mm"], c + 1)
                        if c:
                            act.wait_ge(s["state_mm"], 2 * c)
                        af(vnew, bank4[4], ACT.Copy).then_inc(s["vn_sb"], 1)

                    def state(c):
                        act.wait_ge(s["state_mm"], 2 * c + 1)
                        for h in range(GH):
                            if 4 * c + h:
                                act.wait_ge(s["osq_a"], 4 * c + h)
                            af(scrS[:], bank4[5][:, h, :], ACT.Square, accum_out=ss[:, 4 * c + h:4 * c + h + 1]
                               ).then_inc(s["osq_a"], 1)

                    def latsum():
                        for k in range(QL + KVL):
                            act.wait_ge(s["evict_a"], evict_n(MQ0 + k))
                            if k == 0:
                                act.wait_ge(s["state_mm"], 7)
                            af(sqlat[:, k, :], lat[:, k, :], ACT.Square).then_inc(s["lat_sq"], 1)
                        act.wait_ge(s["lat_sqrt"], 2)
                        af(ls, ls, ACT.Sqrt, bias=epsc).then_inc(s["lat_sqrt"], 1)

                    def lrugate(j):
                        for g in range(2):
                            act.wait_ge(s["lru_mm"], 2 * j + g + 1)
                            cb = (C_BR, C_BI)[g] + j
                            if j == 0 and g == 0:
                                act.wait_ge(s["state_mm"], 7)
                            af((lr, li_)[g][:, j, :], bank[3 + g][:], ACT.Sigmoid, bias=col[:, cb:cb + 1]
                               ).then_inc(s["lru_sig"], 1)

                    def lrudecay(j):
                        act.wait_ge(s["lru_sig"], 2 * j + 1)
                        af(la[:, j, :], lr[:, j, :], ACT.Exp, scale=cpar[:, j:j + 1]).then_inc(s["lru_a"], 1)
                        act.wait_ge(s["lru_sig"], 8)
                        af(lr[:, j, :], lr[:, j, :], ACT.Tanh, scale=npar[:, j:j + 1]).then_inc(s["lru_a"], 1)

                    def lruscan(j):
                        act.wait_ge(s["lru_v"], 3 * (j + 1))
                        af(lm[:, j, :], lm[:, j, :], ACT.Sqrt).then_inc(s["lru_a"], 1)

                    do = {"norm": norm, "gates": gates, "proj": proj, "decay": decay, "l2sum": l2sum, "u": u, "wn": wn,
                          "value": value, "state": state, "latsum": latsum, "lrugate": lrugate, "lrudecay": lrudecay, "lruscan": lruscan}
                    for name, *args in PLAN:
                        if name in do:
                            do[name](*args)
                    sc = float((128 + 64) ** -0.5)
                    for n in range(len(ATT) + 2):
                        if n < len(ATT):
                            h, q = ATT[n]
                            nk = (q + 1) * P
                            act.wait_ge(s["max_v"], 2 * (n + 1))
                            if n >= 3:
                                act.wait_ge(s["t_mm"], n - 2)
                            af(Pr[:, n % 3, 0:nk], bank[2 + n % 2][:, 0:nk], ACT.Exp, bias=mx[:, n % 4:n % 4 + 1], scale=sc,
                               accum_out=lsum[:, n % 4:n % 4 + 1]).then_inc(s["exp_a"], 1)
                        m = n - 2
                        if m >= 0 and PT_ON_ACT[m]:
                            h, q = ATT[m]
                            act.wait_ge(s["t_mm"], m + 1)
                            if h >= 2:
                                act.wait_ge(s["pv_mm"], h - 1)
                            af(pt_dst(m), bank4[4 + m % 2][:, 0:q + 1, :], ACT.Copy).then_inc(s["pt_a"], 1)
                    for n in range(2 * KD):
                        j = SLOT_OUT + n
                        act.wait_ge(w_ready[j % RING], 16 * (j // RING + 1))
                        if n == 0:
                            act.wait_ge(s["s_mm"], len(ATT))
                        if n >= 2:
                            act.wait_ge(s["out_mm"], n - 1)
                        af(wsplit[:, n % 2, 0, :], ring[:, j % RING, :], ACT.Copy).then_inc(s["w_high"], 1)

                @block.vector
                def _(dve):
                    v = nc.vector
                    n_of = {}

                    def step(name, ins, wait=False):
                        n_of[name] = n_of.get(name, 0) + 1
                        ins.then_inc(s[name], 1)
                        if wait:
                            dve.wait_ge(s[name], n_of[name])

                    def norm():
                        for k in range(0, KD, 2):
                            if k:
                                dve.wait_ge(s["squared"], k)
                            else:
                                dve.wait_ge(s["small_in"], 48)
                            v.tensor_tensor(hT[:, k, :], xT[:, k, :], xT[:, k, :], ALU.mult).then_inc(s["squared"], 1)
                        dve.wait_ge(s["norm_sum"], 1)
                        v.tensor_reduce(hs, bank[7][:, 0:32].rearrange("p (c k) -> p c k", c=CH), AX, ALU.add
                                        ).then_inc(s["norm_sqrt"], 1)
                        dve.wait_ge(s["norm_sqrt"], 2)
                        v.reciprocal(hr, hs).then_inc(s["norm_rec"], 1)
                        dve.wait_ge(s["norm_row"], 1)
                        for k in range(KD):
                            v.scalar_tensor_tensor(hT[:, k, :], xT[:, k, :], col[:, C_GAIN + k:C_GAIN + k + 1], bank[2][:],
                                                   ALU.mult, ALU.mult).then_inc(s["h_ready"], 1)

                    def gates():
                        dve.wait_ge(s["gates_mm"], 1)
                        gb = bank[7][:, 64:96].rearrange("p (c n) -> p c n", c=CH)
                        step("soft_v", v.tensor_tensor(z[:, 0:16].rearrange("p (c n) -> p c n", c=CH), gb[:, :, 4:8],
                                                       col[:, C_DT:C_DT + 4].unsqueeze(1).to_broadcast([P, CH, 4]), ALU.add))
                        step("soft_v", v.tensor_scalar(z[:, 16:20], col[:, C_AP:C_AP + 4], -1.0, None, ALU.mult), True)
                        step("soft_v", v.scalar_tensor_tensor(az, z, -1.0, z, ALU.mult, ALU.max))
                        dve.wait_ge(s["soft_a"], 3)
                        step("soft_v", v.tensor_scalar(w1, e1, 1.0, None, ALU.add), True)
                        step("soft_v", v.tensor_scalar(d1, w1, -1.0, None, ALU.add), True)
                        step("soft_v", v.tensor_scalar(i0, d1, 0.0, None, ALU.is_equal), True)
                        step("soft_v", v.tensor_tensor(d1, d1, i0, ALU.add), True)
                        step("soft_v", v.reciprocal(r1, d1), True)
                        dve.wait_ge(s["soft_a"], 4)
                        step("soft_v", v.tensor_tensor(sp, ln1, i0, ALU.add), True)
                        step("soft_v", v.tensor_tensor(sp, sp, e1, ALU.mult), True)
                        step("soft_v", v.tensor_tensor(sp, sp, r1, ALU.mult), True)
                        step("soft_v", v.scalar_tensor_tensor(sp, z, 0.0, sp, ALU.max, ALU.add), True)
                        step("soft_v", v.scalar_tensor_tensor(
                            g16.rearrange("p (c n) -> p c n", c=CH), sp[:, 0:16].rearrange("p (c n) -> p c n", c=CH), -1.0,
                            ealog.unsqueeze(1).to_broadcast([P, CH, 4]), ALU.mult, ALU.mult))
                        step("soft_v", v.tensor_scalar(cpar, sp[:, 16:20], -8.0, None, ALU.mult))
                        step("soft_v", v.tensor_scalar(npar, sp[:, 16:20], 8.0, None, ALU.mult))
                        step("soft_v", v.tensor_scalar(eb, eb, 1.0, None, ALU.add), True)
                        step("soft_v", v.reciprocal(beta, eb), True)
                        step("soft_v", v.tensor_scalar(nbeta, beta, -1.0, None, ALU.mult))

                    def decay():
                        dve.wait_ge(s["decay_mm"], 1)
                        step("decay_v", v.tensor_copy(gcc, bank[2][:, 0:16]))
                        for c in range(CH):
                            dve.wait_ge(s["decay_a"], 1 + c)
                            step("decay_v", v.tensor_copy(gl[:, 4 * c:4 * c + 4], bank4[3 + c][:, :, P - 1]), c == CH - 1)
                        step("decay_v", v.tensor_tensor(kdx, gl, gcc, ALU.subtract))
                        for c in range(CH):
                            for h in range(GH):
                                g = gcc[:, 4 * c + h:4 * c + h + 1]
                                step("decay_v", v.scalar_tensor_tensor(nA[:, c, h, :], bank4[3 + c][:, h, :], g,
                                                                       CST[:, K_BIG:K_BIG + P], ALU.subtract, ALU.add))
                                step("decay_v", v.scalar_tensor_tensor(at[:, c, h, :], bank4[3 + c][:, h, :], g,
                                                                       CST[:, K_BIGT:K_BIGT + P], ALU.subtract, ALU.add))
                        dve.wait_ge(s["decay_a"], 7)
                        dve.wait_ge(s["soft_v"], 18)
                        step("decay_v", v.tensor_tensor(nbe, nbeta, egc, ALU.mult), True)

                    def proj(i):
                        if not on_dve(i) or i >= NPROJ:
                            return
                        b = bank[i % 2]
                        m = count_before(i, True)
                        dve.wait_ge(s["proj_mm"], i + 1)
                        if i < GZ0:
                            if i >= 2:
                                dve.wait_ge(s["silu_done"], i - 1)
                            dst = conv[:, i % 2, :]
                            w = C_CONV + 4 * i
                            bias = None
                        else:
                            j = i - LX0
                            dst = lruu[:, j, :]
                            w = C_LCONV + 4 * j
                            bias = col[:, C_LB + j:C_LB + j + 1]
                        if bias is None:
                            v.tensor_scalar(dst, b[:], col[:, w + 3:w + 4], None, ALU.mult).then_inc(s["conv_step"], 1)
                        else:
                            v.tensor_scalar(dst, b[:], col[:, w + 3:w + 4], bias, ALU.mult, ALU.add).then_inc(s["conv_step"], 1)
                        for t in range(1, 4):
                            dve.wait_ge(s["conv_step"], 4 * m + t)
                            v.scalar_tensor_tensor(dst[:, t:], b[:, 0:S - t], col[:, w + 3 - t:w + 4 - t], dst[:, t:],
                                                   ALU.mult, ALU.add).then_inc(s["conv_step"], 1)

                    def l2sum(g):
                        dve.wait_ge(s["l2_sqrt"], g + 1)
                        if g == 0:
                            v.reciprocal(rn[:, 0:16], nrm[:, 0:16]).then_inc(s["l2_rec"], 1)
                        else:
                            step("soft_v", v.reciprocal(nrm[:, 16:32], nrm[:, 16:32]), True)
                            v.tensor_scalar(rn[:, 16:32], nrm[:, 16:32], float(P) ** -0.5, None, ALU.mult
                                            ).then_inc(s["l2_rec"], 1)

                    def l2row(g):
                        for c in range(CH):
                            dve.wait_ge(s["l2_row"], 4 * g + c + 1)
                            t = (kT, qT)[g]
                            v.tensor_tensor(t[:, c], t[:, c], bank4[3 + c], ALU.mult).then_inc(s["l2_done"], 1)

                    def bc(colv, c):
                        return colv[:, 4 * c:4 * c + 4].unsqueeze(2).to_broadcast([P, GH, P])

                    def prep(c):
                        dve.wait_ge(s["prep_mm"], 4 * c + 1)
                        dve.wait_ge(s["decay_a"], 15)
                        for h in range(GH):
                            step("prep_v", v.scalar_tensor_tensor(nA[:, c, h, :], bank4[2][:, h, :],
                                                                  nbeta[:, 4 * c + h:4 * c + h + 1], nA[:, c, h, :],
                                                                  ALU.mult, ALU.mult))
                        dve.wait_ge(s["prep_mm"], 4 * c + 2)
                        step("prep_v", v.tensor_tensor(at[:, c], bank4[3], at[:, c], ALU.mult))
                        dve.wait_ge(s["prep_mm"], 4 * c + 3)
                        step("prep_v", v.tensor_tensor(kT[:, c], bank4[4], bc(nbe, c), ALU.mult))
                        step("prep_v", v.tensor_tensor(kdec[:, c], bank4[4], bc(ekd, c), ALU.mult))
                        dve.wait_ge(s["prep_mm"], 4 * c + 4)
                        step("prep_v", v.tensor_tensor(vT[:, c], bank4[5], bc(beta, c), ALU.mult))
                        step("prep_v", v.tensor_tensor(qT[:, c], qT[:, c], X[:, c], ALU.mult), True)
                        idb = ident.unsqueeze(1).to_broadcast([P, GH, P])
                        step("prep_v", v.tensor_copy(X[:, c], idb))
                        step("prep_v", v.tensor_copy(Y[:, c], idb), True)

                    def mask(i):
                        return mk[:, i, :].unsqueeze(1).to_broadcast([P, GH, P])

                    def first(c):
                        step("inv_v", v.copy_predicated(X[:, c], mask(0), nA[:, c]))
                        dve.wait_ge(s["first_mm"], c + 1)
                        step("inv_v", v.copy_predicated(Y[:, c], mask(1), bank4[6]), True)

                    def x_(li, pair):
                        for c in (2 * pair, 2 * pair + 1):
                            done = x_mm_after(li, c)
                            dve.wait_ge(s["x_mm"], done if li == LEVELS else done - 1)
                            step("inv_v", v.copy_predicated(Y[:, c], mask(2 * li + 1), bank4[4 + 2 * (c % 2)]))
                            if li < LEVELS:
                                dve.wait_ge(s["x_mm"], done)
                                step("inv_v", v.copy_predicated(X[:, c], mask(2 * li), bank4[5 + 2 * (c % 2)]))
                        dve.wait_ge(s["inv_v"], n_of["inv_v"])

                    def adaout():
                        dve.wait_ge(s["ada_mm"], ADA_LAYER)
                        v.tensor_copy(mod[:, bass.ds(layer * ADA_LAYER, ADA_LAYER), :],
                                      bank[7][:, 0:2 * ADA_LAYER].rearrange("p (t n) -> p t n", n=2)).then_inc(s["ada_v"], 1)

                    def state(c):
                        dve.wait_ge(s["osq_a"], 4 * c + 4)
                        v.tensor_scalar(ss[:, 4 * c:4 * c + 4], ss[:, 4 * c:4 * c + 4], 1.0 / P, EPS, ALU.mult, ALU.add
                                        ).then_inc(s["osum_v"], 1)
                        if c < CH - 1:
                            dve.wait_ge(s["state_mm"], 2 * c + 2)
                            for h in range(GH):
                                if c == 0:
                                    step("state_v", v.tensor_copy(Sst[:, h, :], bank4[6][:, h, :]))
                                else:
                                    step("state_v", v.scalar_tensor_tensor(Sst[:, h, :], Sst[:, h, :],
                                                                           egl[:, 4 * c + h:4 * c + h + 1],
                                                                           bank4[6][:, h, :], ALU.mult, ALU.add))
                            dve.wait_ge(s["state_v"], n_of["state_v"])
                        dve.wait_ge(s["opow_p"], c + 1)
                        if c:
                            dve.wait_ge(s["ot_mm"], c)
                        v.tensor_tensor(on, bank4[5], bc(rs, c), ALU.mult).then_inc(s["on_v"], 1)

                    def gdnout(c):
                        dve.wait_ge(s["ot_mm"], c + 1)
                        if c == 0:
                            dve.wait_ge(s["evict_a"], evict_n(LX0 - 1))
                        m4 = mixed[:, 0:4, c * P:(c + 1) * P]
                        v.scalar_tensor_tensor(m4, bank4[7], col[:, C_ON:C_ON + 1], m4, ALU.mult, ALU.mult
                                               ).then_inc(s["gdn_done"], 1)

                    def latsum():
                        dve.wait_ge(s["lat_sum"], 1)
                        b = bank[5][:, 0:20].rearrange("p (k c) -> p c k", c=CH)
                        v.tensor_reduce(ls[:, 0:4], b[:, :, 0:3], AX, ALU.add).then_inc(s["lat_sum"], 1)
                        v.tensor_reduce(ls[:, 4:8], b[:, :, 3:5], AX, ALU.add).then_inc(s["lat_sum"], 1)
                        dve.wait_ge(s["lat_sum"], 3)
                        v.tensor_scalar(ls[:, 0:4], ls[:, 0:4], 1.0 / (QL * P), None, ALU.mult).then_inc(s["lat_sqrt"], 1)
                        v.tensor_scalar(ls[:, 4:8], ls[:, 4:8], 1.0 / (KVL * P), None, ALU.mult).then_inc(s["lat_sqrt"], 1)
                        dve.wait_ge(s["lat_sqrt"], 3)
                        v.reciprocal(lrr, ls).then_inc(s["lat_rec"], 1)

                    def latrow():
                        for k in range(QL + KVL):
                            g = k // QL
                            dve.wait_ge(s["lat_row"], g + 1)
                            c = C_QN + k if g == 0 else C_KVN + k - QL
                            v.scalar_tensor_tensor(lat[:, k, :], lat[:, k, :], col[:, c:c + 1], bank[6 + g][:], ALU.mult,
                                                   ALU.mult).then_inc(s["lat_done"], 1)

                    def lrudecay(j):
                        dve.wait_ge(s["lru_a"], 2 * j + 2)
                        step("lru_v", v.tensor_tensor(lm[:, j, :], la[:, j, :], la[:, j, :], ALU.mult), True)
                        step("lru_v", v.scalar_tensor_tensor(lm[:, j, :], lm[:, j, :], 1.0, lr[:, j, :], ALU.add, ALU.mult))
                        step("lru_v", v.tensor_tensor(li_[:, j, :], li_[:, j, :], lruu[:, j, :], ALU.mult), True)

                    def lruscan(j):
                        dve.wait_ge(s["lru_a"], 8 + j + 1)
                        step("lru_v", v.tensor_tensor(li_[:, j, :], li_[:, j, :], lm[:, j, :], ALU.mult), True)
                        step("lru_v", v.tensor_tensor_scan(lruu[:, j, :], la[:, j, :], li_[:, j, :], 0.0, ALU.mult,
                                                           ALU.add), True)
                        if j == 0:
                            dve.wait_ge(s["evict_a"], evict_n(MQ0 - 1))
                        step("lru_v", v.tensor_tensor(mixed[:, 12 + j, :], mixed[:, 12 + j, :], lruu[:, j, :], ALU.mult), True)

                    def rope(j):
                        t = kpe[:] if j == 4 else qpe[:, j, :]
                        dve.wait_ge(s["rope_mm"], ROPE_AT[j] + 1)
                        step("rope_v", v.tensor_tensor(t, t, CST[:, K_COS:K_COS + S], ALU.mult))
                        step("rope_v", v.tensor_tensor(ropet[:, 0, :], bank[7][:], CST[:, K_SIN:K_SIN + S], ALU.mult), True)
                        step("rope_v", v.tensor_tensor(t, t, ropet[:, 0, :], ALU.add), True)

                    do = {"norm": norm, "gates": gates, "proj": proj, "decay": decay, "l2sum": l2sum, "l2row": l2row,
                          "adaout": adaout, "prep": prep, "first": first, "x": x_, "state": state, "gdnout": gdnout, "latsum": latsum,
                          "latrow": latrow, "lrudecay": lrudecay, "lruscan": lruscan, "rope": rope}
                    for name, *args in PLAN:
                        if name in do:
                            do[name](*args)
                    sc = float((128 + 64) ** -0.5)
                    for n in range(len(ATT) + 3):
                        if n < len(ATT):
                            h, q = ATT[n]
                            nk = (q + 1) * P
                            dve.wait_ge(s["s_mm"], n + 1)
                            mc = mx[:, n % 4:n % 4 + 1]
                            if n >= 4:
                                dve.wait_ge(s["exp_a"], n - 3)
                            step("max_v", v.tensor_reduce(mc, bank[2 + n % 2][:, 0:nk], AX, ALU.max), True)
                            step("max_v", v.tensor_scalar(mc, mc, -sc, None, ALU.mult))
                        m = n - 1
                        if 0 <= m < len(ATT):
                            nk = (ATT[m][1] + 1) * P
                            dve.wait_ge(s["exp_a"], m + 1)
                            step("soft2_v", v.reciprocal(rl[:, m % 4:m % 4 + 1], lsum[:, m % 4:m % 4 + 1]), True)
                            step("soft2_v", v.tensor_scalar(Pr[:, m % 3, 0:nk], Pr[:, m % 3, 0:nk], rl[:, m % 4:m % 4 + 1],
                                                            None, ALU.mult))
                        m = n - 2
                        if 0 <= m < len(ATT) and not PT_ON_ACT[m]:
                            h, q = ATT[m]
                            dve.wait_ge(s["t_mm"], m + 1)
                            if h >= 2:
                                dve.wait_ge(s["pv_mm"], h - 1)
                            step("pt_v", v.tensor_copy(pt_dst(m), bank4[4 + m % 2][:, 0:q + 1, :]))
                        if n >= 3 and ATT[n - 3][1] == 3:
                            h = ATT[n - 3][0]
                            dve.wait_ge(s["pv_mm"], h + 1)
                            if h == 0:
                                dve.wait_ge(s["evict_a"], evict_n(NPROJ - 1))
                            v.tensor_tensor(mixed[:, 4 + h, :], mixed[:, 4 + h, :], bank[6 + h % 2][:], ALU.mult
                                            ).then_inc(s["mla_done"], 1)
                    def split_low(n):
                        j = SLOT_OUT + n
                        dve.wait_ge(s["w_high"], n + 1)
                        if n >= 2:
                            dve.wait_ge(s["out_mm"], n - 1)
                        v.tensor_tensor(wsplit[:, n % 2, 1, :], ring[:, j % RING, :], wsplit[:, n % 2, 0, :].bitcast(F32),
                                        ALU.subtract).then_inc(s["w_low"], 1)

                    split_low(0)
                    split_low(1)
                    for o in range(KD):
                        if o + 1 < KD:
                            split_low(2 * o + 2)
                            split_low(2 * o + 3)
                        dve.wait_ge(s["out_mm"], 2 * (o + 1))
                        v.tensor_tensor(xT[:, o, :], xT[:, o, :], bank[o % 2][:], ALU.add).then_inc(s["x_done"], 1)
                    dve.wait_ge(s["x_done"], KD)

                @block.gpsimd
                def _(pool):
                    for c in range(CH):
                        pool.wait_ge(s["osum_v"], c + 1)
                        nc.gpsimd.tensor_tensor(rs[:, 4 * c:4 * c + 4], ss[:, 4 * c:4 * c + 4],
                                                CST[:, K_MHALF:K_MHALF + 4], ALU.pow).then_inc(s["opow_p"], 1)
                    for n, t in enumerate(SPLIT_ORDER):
                        if n == 0:
                            pool.wait_ge(s["evict_a"], evict_n(NPROJ - 1))
                            pool.wait_ge(s["gdn_done"], CH)
                            pool.wait_ge(s["lru_v"], 24)
                        if 4 <= t < 12:
                            pool.wait_ge(s["mla_done"], t - 3)
                        nc.gpsimd.tensor_copy(high[t], mixed[:, t, :]).then_inc(s["high_p"], 1)
                        pool.wait_ge(s["high_p"], n + 1)
                        nc.gpsimd.tensor_tensor(low[:, t, :], mixed[:, t, :], high[t].bitcast(F32), ALU.subtract
                                                ).then_inc(s["low_p"], 1)

            nc.all_engine_barrier()
            with nc.Block() as block:
                @block.gpsimd
                def _(pool):
                    for one_sem in allsems:
                        pool.sem_clear(one_sem)
            nc.all_engine_barrier()


NC_ = 256
NT = NC_ + S
KT = NT // P
AH = 4
GD = 768
LAM0 = 0.8 - 0.6 * math.exp(-0.3 * 0)
NE = 64
TOPK = 8
DE = 256
EW = KD * 2 * DE
EW2 = 2 * D
MINB = 32
UN = 4
MAXB = 96

DK0, DQ0, RK0, RQ0, RG0, DV0, RV0, WO0, SW1, SW3, SW2, NSLOT2 = 0, 4, 8, 10, 12, 16, 20, 24, 32, 34, 36, 40
RING2 = 4

B_FN, B_N1, B_N2, B_FN2, B_ADA, B_DN, B_RN, B_DEC, B_LAM, NCOL2 = (0, 8, 16, 24, 32, 80, 81, 82, 90, 90 + 256)

Z_PERM, Z_COS, Z_SIN, Z_DF, Z_MF, Z_DB, Z_MB, Z_CF, Z_CB, NCONST2 = (
    0, 128, 640, 1152, 2048, 2944, 3840, 4736, 5376, 6016)
FX, FC = 896, 640

R_IOTA, R_TRIS, R_ONES, R_BASE, R_J, R_TRIL, R_BIAS, NROUTE = 0, 128, 256, 384, 388, 389, 453, 453 + 64
FAR = 8192.0


def proj2_units():
    units = []
    for slot in range(DK0, DV0):
        units.append((slot, NC_, S))
        if slot < DQ0 or RK0 <= slot < RQ0:
            units.append((slot, 0, NC_))
    return units


UNITS = proj2_units()


def norm_helpers(nc, s, bank, epsc, one, ident, hs, hr, width):
    mm = nc.tensor.matmul

    def pe_part(pe, n, sq, chunks, row):
        for k in range(KD):
            pe.wait_ge(s["squared"], KD * n + k + 1)
            for c in range(chunks):
                last = mm(bank[7][:, c * 8 + k:c * 8 + k + 1], sq(k)[:, c * P:(c + 1) * P], one, start=True, stop=True)
        last.then_inc(s["norm_sum"], 1)
        pe.wait_ge(s["norm_rec"], n + 1)
        for c in range(chunks):
            last = mm(bank[row][:, c * P:(c + 1) * P], hr[:, c:c + 1].to_broadcast([P, P]), ident, start=True, stop=True)
        last.then_inc(s["norm_row"], 1)

    def act_part(act, n, src, sq, chunks):
        for k in range(1, KD, 2):
            act.wait_ge(s["squared"], KD * n + k)
            nc.scalar.activation(sq(k), src(k), ACT.Square).then_inc(s["squared"], 1)
        act.wait_ge(s["norm_sqrt"], 2 * n + 1)
        nc.scalar.activation(hs[:, 0:chunks], hs[:, 0:chunks], ACT.Sqrt, bias=epsc, scale=1.0 / width
                             ).then_inc(s["norm_sqrt"], 1)

    def dve_part(dve, n, src, sq, chunks):
        for k in range(0, KD, 2):
            if n or k:
                dve.wait_ge(s["squared"], KD * n + k)
            nc.vector.tensor_tensor(sq(k), src(k), src(k), ALU.mult).then_inc(s["squared"], 1)
        dve.wait_ge(s["norm_sum"], n + 1)
        nc.vector.tensor_reduce(hs[:, 0:chunks], bank[7][:, 0:8 * chunks].rearrange("p (c k) -> p c k", c=chunks), AX,
                                ALU.add).then_inc(s["norm_sqrt"], 1)
        dve.wait_ge(s["norm_sqrt"], 2 * n + 2)
        nc.vector.reciprocal(hr[:, 0:chunks], hs[:, 0:chunks]).then_inc(s["norm_rec"], 1)
        dve.wait_ge(s["norm_row"], n + 1)

    return pe_part, act_part, dve_part


def second_mixer(nc, stream2, ctx_in, cols2, const2, xT, CST, mod, hT, h2rows):
    ctx = ExitStack()
    with ctx:
        def sb(name, shape, dt=F32):
            return ctx.enter_context(nc.sbuf_tensor(name, shape, dt))

        def sem(name):
            return ctx.enter_context(nc.semaphore(name))

        ps = ctx.enter_context(nc.psum_tensor("ps2", [P, 8, 512], F32))
        bank = [ps[:, i, :] for i in range(8)]
        bank4 = [b.rearrange("p (h t) -> p h t", h=4) for b in bank]

        h2T = hT[:, :, NC_:NT]
        mixed = sb("mixed2", [P, 2 * AH, S])
        ring = sb("ring2", [P, RING2, SLOT])
        col = sb("col2", [P, NCOL2])
        rot = sb("rot2", [P, 1152])
        dk = sb("dk", [P, 4, NT])
        dq = sb("dq", [P, 4, S])
        dv = sb("dv", [P, KT, 512])
        rk = sb("rk", [P, 2, NT])
        rq = sb("rq", [P, 2, S])
        rv = sb("rv", [P, KT, 512])
        Fx = sb("Fx", [P, AH, FX])
        Fc = sb("Fc", [P, AH, FC])
        arena = sb("arena2", [P, 6144])
        tmp = sb("tmp2", [P, 2, FX])
        dist = arena[:, 0:NCONST2 - 1152]
        ctxT = dv[:].rearrange("p c n -> p (c n)")[:, 0:KD * NC_].rearrange("p (k t) -> p k t", k=KD)
        Pm = arena[:, 0:2 * GD].rearrange("p (m t) -> p m t", m=2)
        Pn = arena[:, 2 * GD:4 * GD].rearrange("p (m t) -> p m t", m=2)
        aT = arena[:, 4 * GD:4 * GD + KT * 512].rearrange("p (k t) -> p k t", k=KT)
        sr = arena[:, 0:1024].rearrange("p (b t) -> p b t", b=2)
        Po = tmp[:, :, 0:GD]
        ropet = tmp[:, 0, 0:512]
        sm = sb("sm2", [P, 512])

        def small(at, n):
            return sm[:, at:at + n]

        hs, hr = small(0, 4), small(4, 4)
        gx, gc, g2n = small(8, 8), small(16, 8), small(24, 8)
        z, az, e1, w1, ln1, d1, i0, r1, sp = (small(32 + 8 * i, 8) for i in range(9))
        lg = small(104, 8)
        lamp = small(112, 2)
        nlam = small(114, 1)
        dn = small(115, 1)
        mx, lsum, rl = small(320, 6), small(326, 6), small(332, 6)
        ssn, rnn = small(128, 32), small(160, 32)
        lprod = small(192, 128)

        ident = CST[:, K_ID:K_ID + P]
        one = CST[:, K_ONE:K_ONE + 1]
        epsc = CST[:, K_EPS:K_EPS + 1]
        ZO = 1152

        s = {n: sem("b_" + n) for n in (
            "small_in rot_in dist_in ctx_in squared norm_sum norm_sqrt norm_rec norm_row x_ready mods h_scaled h_ready soft_v soft_a "
            "table_v table_a fc_v proj_mm evict_a evict_v dv_mm rope_mm rope_v s_mm max_v exp_a mix_v t_mm at_a pv_mm "
            "att_v ret_mm ret_v rv_mm sq_a hsum_mm hsum_a hsum_v hrow_mm head_v out_mm x_done turn_mm turn_v turn_a rows_out "
            "slot_used").split()}
        w_ready = [sem(f"b_w_ready{r}") for r in range(RING2)]

        pe_norm, act_norm, dve_norm = norm_helpers(nc, s, bank, epsc, one, ident, hs, hr, D)
        XT = lambda k: xT[:, k, :]
        XS = lambda k: hT[:, k, NC_:NT]
        CS = lambda k: hT[:, k, 0:NC_]
        CX = lambda k: ctxT[:, k, :]
        ITEMS = [(h, q) for h in range(AH) for q in range(CH)]
        RET = [(h, k) for h in range(AH) for k in range(KT)]
        ROPES = [("k", t) for t in range(4)] + [("q", t) for t in range(4)] + [("rk", t) for t in range(2)] + [
            ("rq", t) for t in range(2)]

        def rope_tile(n):
            kind, t = ROPES[n]
            src, first = {"k": (dk, NC_), "q": (dq, 0), "rk": (rk, NC_), "rq": (rq, 0)}[kind]
            return src[:, t, first:first + S]

        def rope_unit(n):
            kind, t = ROPES[n]
            slot = {"k": DK0, "q": DQ0, "rk": RK0, "rq": RQ0}[kind] + t
            return next(u for u, (sl, a, _) in enumerate(UNITS) if sl == slot and a == NC_)

        UP = len(UNITS)
        DVU, RVU = UP, UP + KT

        def rope(pe, n):
            wait_evicted(pe, rope_unit(n))
            if n:
                pe.wait_ge(s["rope_v"], 3 * n - 1)
            else:
                pe.wait_ge(s["rot_in"], 16)
            nc.tensor.matmul(bank[2], rot[:, 0:P], rope_tile(n), start=True, stop=True).then_inc(s["rope_mm"], 1)


        def wait_evicted(eng, u):
            eng.wait_ge(s["evict_a"], u + 1)

        def pbuf(n):
            return (Pm, Pn, Po)[n % 3]

        def ret_out(dve, step, v, h):
            dve.wait_ge(s["rv_mm"], KT * (h + 1))
            step("att_v", v.tensor_copy(dq[:, h, :], bank[4 + h % 2]))

        with nc.Block() as block:
            @block.sync
            def _(sp_):
                sp_.dma_start(col[:], cols2).then_inc(s["small_in"], 16)
                sp_.dma_start(ctxT.rearrange("p k t -> p (k t)"), ctx_in).then_inc(s["ctx_in"], 16)
                sp_.dma_start(rot[:], const2[:, 0:1152]).then_inc(s["rot_in"], 16)
                for r in range(RING2):
                    sp_.dma_start(ring[:, r, :], stream2[r]).then_inc(w_ready[r], 16)
                sp_.dma_start(dist, const2[:, 1152:NCONST2]).then_inc(s["dist_in"], 16)
                n_mixer = SW1
                with sp_.Fori(1, n_mixer // RING2) as i:
                    for r in range(RING2):
                        sp_.wait_ge(s["slot_used"], i * RING2 + (r + 1 - RING2))
                        sp_.dma_start(ring[:, r, :], stream2[bass.ds(i * RING2 + r, 1)].rearrange("a p n -> p (a n)")
                                      ).then_inc(w_ready[r], 16)
                for c in range(CH):
                    sp_.wait_ge(s["turn_v"], c + 1)
                    sp_.wait_ge(s["turn_a"], c + 1)
                    sp_.dma_start(h2rows[c * P:(c + 1) * P, :], mixed[:, 2 * c:2 * c + 2, :].rearrange("p a n -> p (a n)")
                                  ).then_inc(s["rows_out"], 16)
                sp_.wait_ge(s["rows_out"], 16 * CH)

            @block.tensor
            def _(pe):
                mm = nc.tensor.matmul
                held = []

                def slot(j):
                    pe.wait_ge(w_ready[j % RING2], 16 * (j // RING2 + 1))
                    return ring[:, j % RING2, :]

                def release(ins):
                    if held:
                        held.pop()
                        ins.then_inc(s["slot_used"], 1)

                pe_norm(pe, 0, XS, CH, 2)
                pe_norm(pe, 1, CS, NC_ // P, 3)
                pe_norm(pe, 2, XS, CH, 4)
                for u, (sl, a, n) in enumerate(UNITS):
                    if u >= 2:
                        wait_evicted(pe, u - 2)
                    w = slot(sl)
                    for k in range(KD):
                        if u == 0:
                            pe.wait_ge(s["h_ready"], KD + k + 1)
                        last = mm(bank[u % 2][:, 0:n], w[:, k * P:(k + 1) * P], hT[:, k, a:a + n], start=(k == 0),
                                  stop=(k == KD - 1))
                        if k == 0:
                            release(last)
                    last.then_inc(s["proj_mm"], 1)
                    if u + 1 == UP or UNITS[u + 1][0] != sl:
                        held.append(sl)
                    for n_r in range(len(ROPES)):
                        if rope_unit(n_r) == u - 1:
                            rope(pe, n_r)
                for n_r in range(len(ROPES)):
                    if rope_unit(n_r) >= UP - 1:
                        rope(pe, n_r)
                for g in range(2):
                    for j in range(4):
                        w = slot((DV0, RV0)[g] + j)
                        for t in range(KT):
                            if j == 0:
                                if g:
                                    pe.wait_ge(s["evict_v"], t + 1)
                                elif t == 0:
                                    pe.wait_ge(s["rope_v"], 3 * len(ROPES))
                            for kk in range(2):
                                k = 2 * j + kk
                                last = mm(bank[2 + t], hT[:, k, t * P:(t + 1) * P], w[:, kk * 512:(kk + 1) * 512],
                                          start=(k == 0), stop=(k == KD - 1))
                                if kk == 0:
                                    release(last)
                            last.then_inc(s["dv_mm"], 1)
                        held.append(j)

                def scores(n):
                    h, q = ITEMS[n]
                    if n == 0:
                        pe.wait_ge(s["evict_v"], 2 * KT)
                        wait_evicted(pe, UP - 1)
                        wait_evicted(pe, UP - 2)
                    for m in range(2):
                        if n:
                            pe.wait_ge(s["exp_a"], 2 * (n - 1) + m + 1)
                        r = slice(64 * m, 64 * m + 64)
                        mm(bank[2 + 2 * m][:, 0:512], dq[r, h, q * P:(q + 1) * P], dk[r, h, 0:512], start=True, stop=True)
                        mm(bank[3 + 2 * m][:, 0:256], dq[r, h, q * P:(q + 1) * P], dk[r, h, 512:768], start=True, stop=True
                           ).then_inc(s["s_mm"], 1)

                def turn(n):
                    pe.wait_ge(s["mix_v"], 4 * (n + 1))
                    if n:
                        pe.wait_ge(s["at_a"], 2 * n)
                    for k in range(KT):
                        last = nc.tensor.transpose(bank4[6 + k // 4][:, k % 4, :], pbuf(n)[:, 0, k * P:(k + 1) * P], ident)
                        if k == 3 or k == KT - 1:
                            last.then_inc(s["t_mm"], 1)

                def pv(h):
                    pe.wait_ge(s["at_a"], 8 * (h + 1))
                    if h >= 2:
                        pe.wait_ge(s["att_v"], h - 1)
                    for k in range(KT):
                        last = mm(bank[h % 2], dv[:, k, h * P:(h + 1) * P], aT[:, k, :], start=(k == 0), stop=(k == KT - 1))
                    last.then_inc(s["pv_mm"], 1)

                for n in range(len(ITEMS) + 3):
                    if n < len(ITEMS):
                        scores(n)
                    if n >= 3 and ITEMS[n - 3][1] == CH - 1:
                        pv(ITEMS[n - 3][0])
                    if 2 <= n < len(ITEMS) + 2:
                        turn(n - 2)
                for n in range(len(RET) + 1):
                    if n < len(RET):
                        h, k = RET[n]
                        if n == 0:
                            pe.wait_ge(s["exp_a"], 2 * len(ITEMS))
                        if n >= 2:
                            pe.wait_ge(s["ret_v"], n - 1)
                        r = slice(64 * (h % 2), 64 * (h % 2) + 64)
                        mm(bank[2 + n % 2], rk[r, h // 2, k * P:(k + 1) * P], rq[r, h // 2, :], start=True, stop=True
                           ).then_inc(s["ret_mm"], 1)
                    if n:
                        h, k = RET[n - 1]
                        pe.wait_ge(s["ret_v"], n)
                        if k == 0 and h >= 2:
                            pe.wait_ge(s["att_v"], AH + h - 1)
                        if k == 0 and h < 2:
                            pe.wait_ge(s["exp_a"], 2 * len(ITEMS))
                        mm(bank[4 + h % 2], rv[:, k, h * P:(h + 1) * P], sr[:, (n - 1) % 2, :], start=(k == 0),
                           stop=(k == KT - 1)).then_inc(s["rv_mm"], 1)
                pe.wait_ge(s["at_a"], 2 * len(ITEMS))
                for h in range(2 * AH):
                    pe.wait_ge(s["sq_a"], h + 1)
                    for c in range(CH):
                        last = mm(bank[7][:, 4 * h + c:4 * h + c + 1], hT[:, h, c * P:(c + 1) * P], one, start=True, stop=True)
                last.then_inc(s["hsum_mm"], 1)
                pe.wait_ge(s["hsum_v"], 1)
                for h in range(2 * AH):
                    if h >= 2:
                        pe.wait_ge(s["head_v"], h - 1 if h - 2 < AH else AH + 2 * (h - 2 - AH) + 1)
                    else:
                        pe.wait_ge(s["att_v"], 2 * AH)
                    for c in range(CH):
                        last = mm(bank[2 + h % 2][:, c * P:(c + 1) * P], rnn[:, 4 * h + c:4 * h + c + 1].to_broadcast([P, P]),
                                  ident, start=True, stop=True)
                    last.then_inc(s["hrow_mm"], 1)
                for o in range(KD):
                    if o >= 2:
                        pe.wait_ge(s["x_done"], o - 1)
                    w = slot(WO0 + o)
                    for k in range(KD):
                        if o == 0:
                            pe.wait_ge(s["head_v"], k + 1 if k < AH else AH + 2 * (k - AH + 1))
                        last = mm(bank[o % 2], w[:, k * P:(k + 1) * P], mixed[:, k, :], start=(k == 0), stop=(k == KD - 1))
                        if k == 0:
                            release(last)
                    last.then_inc(s["out_mm"], 1)
                    held.append(o)
                pe_norm(pe, 3, XS, CH, 5)
                for c in range(CH):
                    if c:
                        pe.wait_ge(s["turn_v"], c)
                        pe.wait_ge(s["turn_a"], c)
                    for k in range(KD):
                        if c == 0:
                            pe.wait_ge(s["h_ready"], 2 * KD + k + 1)
                        last = nc.tensor.transpose(bank4[2 + k // 4][:, k % 4, :], h2T[:, k, c * P:(c + 1) * P], ident)
                        if k % 4 == 3:
                            last.then_inc(s["turn_mm"], 1)

            @block.scalar
            def _(act):
                af = nc.scalar.activation
                act_norm(act, 0, XT, XS, CH)
                act_norm(act, 1, CX, CS, NC_ // P)
                act_norm(act, 2, XT, XS, CH)
                for k in range(KD):
                    act.wait_ge(s["h_scaled"], k + 1)
                    act.wait_ge(s["mods"], 4)
                    af(CS(k), CS(k), ACT.Identity, bias=mod[:, k, 1:2]).then_inc(s["h_ready"], 1)
                for k in range(KD):
                    act.wait_ge(s["h_scaled"], KD + k + 1)
                    af(XS(k), XS(k), ACT.Identity, bias=mod[:, k, 0:1]).then_inc(s["h_ready"], 1)
                act.wait_ge(s["soft_v"], 2)
                af(e1, az, ACT.Exp, scale=-1.0).then_inc(s["soft_a"], 1)
                act.wait_ge(s["soft_v"], 3)
                af(ln1, w1, ACT.Ln).then_inc(s["soft_a"], 1)
                act.wait_ge(s["soft_v"], 15)
                af(lamp, lamp, ACT.Exp).then_inc(s["soft_a"], 1)

                def evict(u):
                    sl, a, n = UNITS[u]
                    act.wait_ge(s["proj_mm"], u + 1)
                    src = bank[u % 2][:, 0:n]
                    if sl < DQ0:
                        af(dk[:, sl - DK0, a:a + n], src, ACT.Copy).then_inc(s["evict_a"], 1)
                    elif sl < RK0:
                        af(dq[:, sl - DQ0, :], src, ACT.Copy).then_inc(s["evict_a"], 1)
                    elif sl < RQ0:
                        af(rk[:, sl - RK0, a:a + n], src, ACT.Copy).then_inc(s["evict_a"], 1)
                    elif sl < RG0:
                        af(rq[:, sl - RQ0, :], src, ACT.Copy).then_inc(s["evict_a"], 1)
                    else:
                        af(mixed[:, AH + sl - RG0, :], src, ACT.Silu).then_inc(s["evict_a"], 1)

                for u in range(UP):
                    evict(u)
                act.wait_ge(s["dist_in"], 16)
                for h in range(AH):
                    for d in range(2):
                        i = 2 * h + d
                        act.wait_ge(s["table_v"], 3 * h + d + 1)
                        af(tmp[:, d, :], tmp[:, d, :], ACT.Exp).then_inc(s["table_a"], 1)
                    act.wait_ge(s["table_v"], 3 * (h + 1))
                    for d in range(2):
                        af((tmp[:, 0, 0:FC], tmp[:, 1, 0:FC])[d], dist[:, (Z_CF, Z_CB)[d] - ZO:(Z_CF, Z_CB)[d] - ZO + FC],
                           ACT.Exp, scale=lg[:, 4 * d + h:4 * d + h + 1]).then_inc(s["table_a"], 1)
                for n in range(len(ITEMS) + 2):
                    if n < len(ITEMS):
                        for m in range(2):
                            act.wait_ge(s["max_v"], 4 * n + 2 * m + 2)
                            if n >= 3:
                                act.wait_ge(s["t_mm"], 2 * (n - 2))
                            af(pbuf(n)[:, m, :], ps[:, 2 + 2 * m:4 + 2 * m, :].rearrange("p b t -> p (b t)")[:, 0:GD], ACT.Exp,
                               bias=mx[:, 2 * (n % 3) + m:2 * (n % 3) + m + 1], scale=0.125,
                               accum_out=lsum[:, 2 * (n % 3) + m:2 * (n % 3) + m + 1]).then_inc(s["exp_a"], 1)
                    if n >= 2:
                        h, q = ITEMS[n - 2]
                        for half in range(2):
                            act.wait_ge(s["t_mm"], 2 * (n - 2) + half + 1)
                            if h and q == 0 and half == 0:
                                act.wait_ge(s["pv_mm"], h)
                            kk = slice(0, 4) if half == 0 else slice(4, KT)
                            m = 4 if half == 0 else KT - 4
                            af(aT[:, kk, q * P:(q + 1) * P], bank4[6 + half][:, 0:m, :], ACT.Copy).then_inc(s["at_a"], 1)
                for h in range(2 * AH):
                    act.wait_ge(s["att_v"], h + 1)
                    src = mixed[:, h, :] if h < AH else dq[:, h - AH, :]
                    af(hT[:, h, 0:S], src, ACT.Square).then_inc(s["sq_a"], 1)
                act.wait_ge(s["hsum_mm"], 1)
                af(ssn, bank[7][:, 0:32], ACT.Sqrt, bias=epsc, scale=1.0 / P).then_inc(s["hsum_a"], 1)
                act_norm(act, 3, XT, XS, CH)
                for k in range(KD):
                    act.wait_ge(s["h_scaled"], 2 * KD + k + 1)
                    af(h2T[:, k, :], h2T[:, k, :], ACT.Identity, bias=mod[:, 24 + k, 0:1]).then_inc(s["h_ready"], 1)
                for c in range(CH):
                    act.wait_ge(s["turn_mm"], 2 * c + 2)
                    af(mixed[:, 2 * c + 1, :], bank[3], ACT.Copy).then_inc(s["turn_a"], 1)

            @block.vector
            def _(dve):
                v = nc.vector
                n_of = {}

                def step(name, ins, wait=False):
                    n_of[name] = n_of.get(name, 0) + 1
                    ins.then_inc(s[name], 1)
                    if wait:
                        dve.wait_ge(s[name], n_of[name])

                dve_norm(dve, 0, XT, XS, CH)
                dve.wait_ge(s["small_in"], 16)
                for k in range(KD):
                    step("x_ready", v.scalar_tensor_tensor(XT(k), XT(k), col[:, B_FN + k:B_FN + k + 1], bank[2], ALU.mult,
                                                           ALU.mult), k == KD - 1)
                dve.wait_ge(s["ctx_in"], 16)
                dve_norm(dve, 1, CX, CS, NC_ // P)
                for j in range(2):
                    step("mods", v.tensor_tensor(mod[:, :, j], mod[:, :, j], col[:, B_ADA:B_ADA + NADA], ALU.add), j == 1)
                step("mods", v.scalar_tensor_tensor(gx, mod[:, 8:16, 0], 1.0, col[:, B_N1:B_N1 + 8], ALU.add, ALU.mult))
                step("mods", v.scalar_tensor_tensor(gc, mod[:, 8:16, 1], 1.0, col[:, B_N1:B_N1 + 8], ALU.add, ALU.mult))
                step("mods", v.scalar_tensor_tensor(g2n, mod[:, 32:40, 0], 1.0, col[:, B_N2:B_N2 + 8], ALU.add, ALU.mult), True)
                for k in range(KD):
                    step("h_scaled", v.scalar_tensor_tensor(CS(k), CX(k), gc[:, k:k + 1], bank[3][:, 0:NC_], ALU.mult, ALU.mult))
                dve_norm(dve, 2, XT, XS, CH)
                for k in range(KD):
                    step("h_scaled", v.scalar_tensor_tensor(XS(k), XT(k), gx[:, k:k + 1], bank[4], ALU.mult, ALU.mult))
                step("soft_v", v.tensor_scalar(z, col[:, B_DEC:B_DEC + 8], -1.0, None, ALU.mult), True)
                step("soft_v", v.scalar_tensor_tensor(az, z, -1.0, z, ALU.mult, ALU.max))
                dve.wait_ge(s["soft_a"], 1)
                step("soft_v", v.tensor_scalar(w1, e1, 1.0, None, ALU.add), True)
                step("soft_v", v.tensor_scalar(d1, w1, -1.0, None, ALU.add), True)
                step("soft_v", v.tensor_scalar(i0, d1, 0.0, None, ALU.is_equal), True)
                step("soft_v", v.tensor_tensor(d1, d1, i0, ALU.add), True)
                step("soft_v", v.reciprocal(r1, d1), True)
                dve.wait_ge(s["soft_a"], 2)
                step("soft_v", v.tensor_tensor(sp, ln1, i0, ALU.add), True)
                step("soft_v", v.tensor_tensor(sp, sp, e1, ALU.mult), True)
                step("soft_v", v.tensor_tensor(sp, sp, r1, ALU.mult), True)
                step("soft_v", v.scalar_tensor_tensor(sp, z, 0.0, sp, ALU.max, ALU.add), True)
                step("soft_v", v.tensor_scalar(lg, sp, -1.0, None, ALU.mult))
                lp = col[:, B_LAM:B_LAM + 256].rearrange("p (a b n) -> p a b n", a=2, b=2)
                step("soft_v", v.tensor_tensor(lprod.rearrange("p (a n) -> p a n", a=2), lp[:, :, 0, :], lp[:, :, 1, :],
                                               ALU.mult), True)
                step("soft_v", v.tensor_reduce(lamp, lprod.rearrange("p (a n) -> p a n", a=2), AX, ALU.add))
                step("soft_v", v.tensor_scalar(dn, col[:, B_DN:B_DN + 1], 1 - LAM0, None, ALU.mult))
                dve.wait_ge(s["soft_a"], 3)
                step("soft_v", v.tensor_tensor(nlam, lamp[:, 1:2], lamp[:, 0:1], ALU.subtract), True)
                step("soft_v", v.tensor_scalar(nlam, nlam, -LAM0, None, ALU.add), True)

                def rope_v(n):
                    t = rope_tile(n)
                    dve.wait_ge(s["rope_mm"], n + 1)
                    step("rope_v", v.tensor_tensor(t, t, rot[:, 128:640], ALU.mult))
                    step("rope_v", v.tensor_tensor(ropet, bank[2], rot[:, 640:1152], ALU.mult), True)
                    step("rope_v", v.tensor_tensor(t, t, ropet, ALU.add), True)

                dve.wait_ge(s["rot_in"], 16)
                for n in range(len(ROPES)):
                    rope_v(n)
                dve.wait_ge(s["dist_in"], 16)
                for h in range(AH):
                    for d in range(2):
                        a, m = (Z_DF, Z_DB)[d] - ZO, (Z_MF, Z_MB)[d] - ZO
                        step("table_v", v.scalar_tensor_tensor(tmp[:, d, :], dist[:, a:a + FX], lg[:, 4 * d + h:4 * d + h + 1],
                                                               dist[:, m:m + FX], ALU.mult, ALU.add))
                    dve.wait_ge(s["table_a"], 4 * h + 2)
                    step("table_v", v.tensor_tensor(Fx[:, h, :], tmp[:, 0, :], tmp[:, 1, :], ALU.add))
                    dve.wait_ge(s["table_a"], 4 * h + 4)
                    step("fc_v", v.tensor_tensor(Fc[:, h, :], tmp[:, 0, 0:FC], tmp[:, 1, 0:FC], ALU.add), True)
                for g in range(2):
                    dst = (dv, rv)[g]
                    for t in range(KT):
                        dve.wait_ge(s["dv_mm"], g * 24 + 18 + t + 1)
                        step("evict_v", v.tensor_copy(dst[:, t, :], bank[2 + t]), t == KT - 1)
                for n in range(len(ITEMS) + 4):
                    if n < len(ITEMS):
                        for m in range(2):
                            c = 2 * (n % 3) + m
                            dve.wait_ge(s["s_mm"], 2 * n + m + 1)
                            step("max_v", v.tensor_reduce(mx[:, c:c + 1],
                                                          ps[:, 2 + 2 * m:4 + 2 * m, :].rearrange("p b t -> p (b t)")[:, 0:GD],
                                                          AX, ALU.max), True)
                            step("max_v", v.tensor_scalar(mx[:, c:c + 1], mx[:, c:c + 1], -0.125, None, ALU.mult))
                    if 1 <= n <= len(ITEMS):
                        m = n - 1
                        c = 2 * (m % 3)
                        b = pbuf(m)
                        dve.wait_ge(s["exp_a"], 2 * m + 2)
                        step("mix_v", v.reciprocal(rl[:, c:c + 2], lsum[:, c:c + 2]), True)
                        step("mix_v", v.tensor_tensor(rl[:, c + 1:c + 2], rl[:, c + 1:c + 2], nlam, ALU.mult), True)
                        step("mix_v", v.tensor_scalar(b[:, 1, :], b[:, 1, :], rl[:, c + 1:c + 2], None, ALU.mult), True)
                        step("mix_v", v.scalar_tensor_tensor(b[:, 0, :], b[:, 0, :], rl[:, c:c + 1], b[:, 1, :], ALU.mult,
                                                             ALU.add))
                    if n >= 4 and ITEMS[n - 4][1] == CH - 1:
                        h = ITEMS[n - 4][0]
                        dve.wait_ge(s["pv_mm"], h + 1)
                        step("att_v", v.tensor_copy(mixed[:, h, :], bank[h % 2]))
                for n in range(len(RET)):
                    h, k = RET[n]
                    dve.wait_ge(s["ret_mm"], n + 1)
                    if n >= 2:
                        dve.wait_ge(s["rv_mm"], n - 1)
                    if n == 0:
                        dve.wait_ge(s["t_mm"], 2 * len(ITEMS))
                    w = Fc[:, h, P - k * P:P - k * P + S] if k < 2 else Fx[:, h, 384 - (k - 2) * P:384 - (k - 2) * P + S]
                    step("ret_v", v.scalar_tensor_tensor(sr[:, n % 2, :], bank[2 + n % 2], 0.125, w, ALU.mult, ALU.mult))
                    if n >= 1 and RET[n - 1][1] == KT - 1:
                        ret_out(dve, step, v, RET[n - 1][0])
                ret_out(dve, step, v, AH - 1)
                dve.wait_ge(s["hsum_a"], 1)
                step("hsum_v", v.reciprocal(rnn, ssn))
                for h in range(2 * AH):
                    dve.wait_ge(s["hrow_mm"], h + 1)
                    if h < AH:
                        step("head_v", v.scalar_tensor_tensor(mixed[:, h, :], mixed[:, h, :], dn, bank[2 + h % 2], ALU.mult,
                                                              ALU.mult))
                    else:
                        step("head_v", v.scalar_tensor_tensor(dq[:, h - AH, :], dq[:, h - AH, :], col[:, B_RN:B_RN + 1],
                                                              bank[2 + h % 2], ALU.mult, ALU.mult), True)
                        step("head_v", v.tensor_tensor(mixed[:, h, :], mixed[:, h, :], dq[:, h - AH, :], ALU.mult))
                for o in range(KD):
                    dve.wait_ge(s["out_mm"], o + 1)
                    step("x_done", v.scalar_tensor_tensor(xT[:, o, :], bank[o % 2], mod[:, 16 + o, 0:1], xT[:, o, :], ALU.mult,
                                                          ALU.add), o == KD - 1)
                dve.wait_ge(s["hrow_mm"], 8)
                dve_norm(dve, 3, XT, XS, CH)
                for k in range(KD):
                    step("h_scaled", v.scalar_tensor_tensor(h2T[:, k, :], XT(k), g2n[:, k:k + 1], bank[5], ALU.mult, ALU.mult))
                for c in range(CH):
                    dve.wait_ge(s["turn_mm"], 2 * c + 1)
                    step("turn_v", v.tensor_copy(mixed[:, 2 * c, :], bank[2]))

        nc.all_engine_barrier()
        with nc.Block() as block:
            @block.gpsimd
            def _(pool):
                for one_sem in list(s.values()) + w_ready:
                    pool.sem_clear(one_sem)
        nc.all_engine_barrier()


def experts(nc, stream2, route, router_w, cols2, up_w, down_w, xT, CST, mod, hT, h2rows, rows, out):
    ctx = ExitStack()
    with ctx:
        def sb(name, shape, dt=F32):
            return ctx.enter_context(nc.sbuf_tensor(name, shape, dt))

        def sem(name):
            return ctx.enter_context(nc.semaphore("c_" + name))

        ps = ctx.enter_context(nc.psum_tensor("ps3", [P, 8, 512], F32))
        bank = [ps[:, i, :] for i in range(8)]
        bank4 = [b.rearrange("p (h t) -> p h t", h=4) for b in bank]
        h2T = hT[:, :, NC_:NT]

        weights = sb("expert_weights", [P, UN, EW + EW2])
        wup, wdn = weights[:, :, 0:EW], weights[:, :, EW:EW + EW2]
        shw = weights[:, UN - 1, :].rearrange("p (b n) -> p b n", n=SLOT)
        rw = sb("router", [P, KD * NE])
        rc = sb("rc", [P, NROUTE])
        fn = sb("fn", [P, 8])
        scores, sel, selm, work, msk = (sb(n, [P, CH, NE]) for n in ("scores", "sel", "selm", "work", "msk"))
        m8 = sb("m8", [P, CH * 8, 8])
        cmp = sb("cmp", [P, CH * 64])
        cmp2 = sb("cmp2", [P, CH * 64])
        kidx = sb("kidx", [P, CH, NE])
        wts = sb("wts", [P, CH, NE])
        tab = sb("tab", [P, NE, CH, 3])
        s64 = sb("s64", [P, 4, NE])
        gsc = sb("gsc", [P, 32])
        rank = sb("rank", [P, 32])
        gneg = sb("gneg", [P, 32])
        top = sb("top", [P, CH, 8])
        wsum = sb("wsum", [P, 4])
        ej = sb("ej", [P, 1])
        erow = sb("erow", [1, P], I32)
        last_group = sb("last_group", [1, 2], I32)
        cur = sb("cur", [P, 2, CH, 3])
        hot = sb("hot", [P, 2, CH, P])
        iota = sb("iota", [P, P])
        dsti = sb("dsti", [P, UN], I32)
        toki = sb("toki", [P, UN], I32)
        sdst = sb("sdst", [P, UN], I32)
        wsl = sb("wsl", [P, UN])
        xb = sb("xb", [P, UN, D])
        xbT = sb("xbT", [P, 2, KD, P])
        sil = sb("sil", [P, 2, DE])
        g = sb("g", [P, 2, DE])
        gT = sb("gT", [P, 2, 2, P])
        y = sb("y", [P, 2, D])
        gs = y[:, 1, :].rearrange("p (t n) -> p t n", t=2)
        hs, hr = sb("hs3", [P, 4]), sb("hr3", [P, 4])

        ident = CST[:, K_ID:K_ID + P]
        one = CST[:, K_ONE:K_ONE + 1]
        epsc = CST[:, K_EPS:K_EPS + 1]
        ones = rc[:, R_ONES:R_ONES + P]

        s = {n: sem(n) for n in (
            "cpy_v may_gather may_scatter small_in shared_in logit_mm sig_a route_v pos_mm row_mm shup_mm shsil_a shg_v shdn_mm shx_v xb_v "
            "cur_v hot_v info_mm idx_v xt_mm xt_a xt_v up_mm sil_a g_v gt_mm gt_a dn_mm y_a y_v "
            "acc_mm accx_v squared norm_sum norm_sqrt norm_rec norm_row fin_v out_done").split()}
        gather_in = [sem(f"gather_in{b}") for b in range(UN)]
        scatter_out = [sem(f"scatter_out{b}") for b in range(2)]
        wup_in = [sem(f"wup_in{b}") for b in range(UN)]
        wdn_in = [sem(f"wdn_in{b}") for b in range(UN)]
        rows_in = [sem(f"rows_in{b}") for b in range(2 * CH)]
        N_MASK, N_EXPERT, N_ROUTE = 53, 74, 81

        def yt(c):
            return weights[:].rearrange("p a n -> p (a n)")[:, (c % 3) * TOPK * D:(c % 3 + 1) * TOPK * D]

        pe_norm, act_norm, dve_norm = norm_helpers(nc, s, bank, epsc, one, ident, hs, hr, D)
        XT = lambda k: xT[:, k, :]
        XS = lambda k: h2T[:, k, :]

        def later(i, u, n):
            return type(i) is not int or i * UN + u >= n

        LOOP = range(3, UN + 3)

        with nc.Block() as block:
            @block.sync
            def _(sp):
                sp.dma_start(rc[:], route).then_inc(s["small_in"], 16)
                sp.dma_start(rw[:], router_w).then_inc(s["small_in"], 16)
                sp.dma_start(fn[:], cols2[:, B_FN2:B_FN2 + 8]).then_inc(s["small_in"], 16)
                for j in range(6):
                    sp.dma_start(shw[:, j, :], stream2[SW1 + j]).then_inc(s["shared_in"], 16)

                sp.wait_ge(s["route_v"], N_ROUTE)
                n = nc.sync.value_load(last_group[0:1, 0:1], min_val=MINB // UN - 1, max_val=MAXB // UN - 1) + 1
                for b in range(UN):
                    e = nc.sync.value_load(erow[0:1, b:b + 1], min_val=0, max_val=NE - 1)
                    if b == UN - 1:
                        sp.wait_ge(s["shup_mm"], 4)
                        sp.wait_ge(s["shdn_mm"], KD)
                    sp.dma_start(wup[:, b, :], up_w[bass.ds(e, 1)].rearrange("a p n -> p (a n)")).then_inc(wup_in[b], 16)
                    sp.dma_start(wdn[:, b, :], down_w[bass.ds(e, 1)].rearrange("a p n -> p (a n)")).then_inc(wdn_in[b], 16)
                with sp.Fori(1, n) as i:
                    for b in range(UN):
                        e = nc.sync.value_load(erow[0:1, bass.ds(i * UN + b, 1)], min_val=0, max_val=NE - 1)
                        sp.wait_ge(s["up_mm"], i * UN + (b + 1 - UN))
                        sp.dma_start(wup[:, b, :], up_w[bass.ds(e, 1)].rearrange("a p n -> p (a n)")).then_inc(wup_in[b], 16)
                        sp.wait_ge(s["dn_mm"], i * (2 * UN) + 2 * (b + 1 - UN))
                        sp.dma_start(wdn[:, b, :], down_w[bass.ds(e, 1)].rearrange("a p n -> p (a n)")).then_inc(wdn_in[b], 16)
                for b in range(2):
                    sp.wait_ge(scatter_out[b], n * (8 * UN))
                for c in range(CH):
                    if c >= 3:
                        sp.wait_ge(s["acc_mm"], KD * (c - 2))
                    for half in range(2):
                        cols = slice(half * (D // 2), (half + 1) * (D // 2))
                        sp.dma_start(yt(c).rearrange("p (k n) -> p k n", k=TOPK)[:, :, cols],
                                     rows[c * P * TOPK:(c + 1) * P * TOPK, cols].rearrange("(p k) n -> p k n", k=TOPK)
                                     ).then_inc(rows_in[2 * c + half], 16)
                for k in range(0, KD, 2):
                    sp.wait_ge(s["fin_v"], k + 2)
                    sp.dma_start(out.rearrange("p (k n) -> p k n", k=KD)[:, k:k + 2, :], h2T[:, k:k + 2, :]
                                 ).then_inc(s["out_done"], 16)
                sp.wait_ge(s["out_done"], 16 * KD // 2)

            def load_groups(eng):
                eng.wait_ge(s["route_v"], N_ROUTE)
                last_i = eng.value_load(last_group[0:1, 0:1], min_val=MINB // UN - 1, max_val=MAXB // UN - 1)
                return last_i, last_i + 1

            @block.tensor
            def _(pe):
                mm = nc.tensor.matmul

                for c in range(CH):
                    if c == 0:
                        pe.wait_ge(s["small_in"], 48)
                    for k in range(KD):
                        last = mm(bank[0][:, c * NE:(c + 1) * NE], h2T[:, k, c * P:(c + 1) * P],
                                  rw[:, k * NE:(k + 1) * NE], start=(k == 0), stop=(k == KD - 1))
                last.then_inc(s["logit_mm"], 1)
                pe.wait_ge(s["shared_in"], 96)

                def shared_up(t):
                    for k in range(KD):
                        last = mm(bank[1 + t], shw[:, t, k * P:(k + 1) * P], h2T[:, k, :], start=(k == 0), stop=(k == KD - 1))
                    last.then_inc(s["shup_mm"], 1)

                shared_up(0)
                shared_up(1)
                pe.wait_ge(s["route_v"], N_MASK)
                for c in range(CH):
                    mm(bank[7][:, c * NE:(c + 1) * NE], rc[:, R_TRIS:R_TRIS + P], msk[:, c, :], start=True, stop=(c == 0))
                    for c2 in range(c):
                        mm(bank[7][:, c * NE:(c + 1) * NE], ones, msk[:, c2, :], start=False, stop=(c2 == c - 1))
                for c in range(CH):
                    last = mm(bank[7][:, 256:256 + NE], ones, msk[:, c, :], start=(c == 0), stop=(c == CH - 1))
                last.then_inc(s["pos_mm"], 1)
                shared_up(2)
                pe.wait_ge(s["route_v"], N_EXPERT)
                mm(bank[0][0:1, 0:P], ej[:], ident, start=True, stop=True).then_inc(s["row_mm"], 1)
                shared_up(3)

                def shared_down(o):
                    if o == 0:
                        pe.wait_ge(s["shg_v"], 2)
                    if o >= 2:
                        pe.wait_ge(s["shx_v"], o - 1)
                    for k in range(2):
                        w = shw[:, 4 + o // 4, (o % 4) * 256 + k * P:(o % 4) * 256 + (k + 1) * P]
                        last = mm(bank[5 + o % 2], w, gs[:, k, :], start=(k == 0), stop=(k == 1))
                    last.then_inc(s["shdn_mm"], 1)

                def info(i, u):
                    b = u % 2
                    pe.wait_ge(s["hot_v"], i * (5 * UN) + (5 * u + 4))
                    if later(i, u, 1):
                        pe.wait_ge(s["idx_v"], i * (3 * UN) + 3 * u)
                    for c in range(CH):
                        last = mm(bank[0][:, 0:2], hot[:, b, c, :], cur[:, b, c, 1:3], start=(c == 0), stop=(c == CH - 1))
                    last.then_inc(s["info_mm"], 1)

                def turn(i, u):
                    pe.wait_ge(gather_in[u % UN], i * 16 + 16 * (u // UN + 1))
                    if later(i, u, 1):
                        pe.wait_ge(s["xt_a"], i * UN + u)
                        pe.wait_ge(s["xt_v"], i * UN + u)
                    for k in range(KD):
                        last = nc.tensor.transpose(bank4[1 + k // 4][:, k % 4, :], xb[:, u % UN, k * P:(k + 1) * P], ident)
                        if k % 4 == 3:
                            last.then_inc(s["xt_mm"], 1)

                def up(i, u):
                    b = u % 2
                    pe.wait_ge(s["xt_a"], i * UN + (u + 1))
                    pe.wait_ge(s["xt_v"], i * UN + (u + 1))
                    pe.wait_ge(wup_in[u % UN], i * 16 + 16 * (u // UN + 1))
                    if later(i, u, 2):
                        pe.wait_ge(s["g_v"], i * UN + (u - 1))
                    for k in range(KD):
                        last = mm(bank[3 + b], xbT[:, b, k, :], wup[:, u % UN, k * 512:(k + 1) * 512], start=(k == 0),
                                  stop=(k == KD - 1))
                    last.then_inc(s["up_mm"], 1)

                def turn_g(i, u):
                    b = u % 2
                    pe.wait_ge(s["g_v"], i * UN + (u + 1))
                    if later(i, u, 1):
                        pe.wait_ge(s["gt_a"], i * UN + u)
                    for k in range(2):
                        last = nc.tensor.transpose(bank4[5][:, k, :], g[:, b, k * P:(k + 1) * P], ident)
                    last.then_inc(s["gt_mm"], 1)

                def down(i, u):
                    b = u % 2
                    pe.wait_ge(s["gt_a"], i * UN + (u + 1))
                    pe.wait_ge(wdn_in[u % UN], i * 16 + 16 * (u // UN + 1))
                    if later(i, u, 1):
                        pe.wait_ge(s["y_a"], i * UN + u)
                        pe.wait_ge(s["y_v"], i * UN + u)
                    for half in range(2):
                        for k in range(2):
                            last = mm(bank[6 + half], gT[:, b, k, :], wdn[:, u % UN, k * D + half * 512:k * D + half * 512 + 512],
                                      start=(k == 0), stop=(k == 1))
                        last.then_inc(s["dn_mm"], 1)

                last_i, n = load_groups(nc.tensor)
                info(0, 0)
                shared_down(0)
                info(0, 1)
                shared_down(1)
                shared_down(2)
                info(0, 2)
                for o in range(3, KD):
                    shared_down(o)
                pe.wait_ge(s["shg_v"], 2)
                pe.wait_ge(s["shx_v"], KD)
                turn(0, 0)
                up(0, 0)
                info(0, 3)
                turn(0, 1)

                def blocks(i, steps):
                    for u in steps:
                        up(i, u)
                        turn_g(i, u - 1)
                        info(i, u + 3)
                        turn(i, u + 1)
                        down(i, u - 1)

                blocks(0, (1, 2))
                with pe.Fori(0, last_i) as i:
                    blocks(i, LOOP)
                up(last_i, UN - 1)
                turn_g(last_i, UN - 2)
                down(last_i, UN - 2)
                turn_g(last_i, UN - 1)
                down(last_i, UN - 1)

                for c in range(CH):
                    if c == 0:
                        pe.wait_ge(s["xt_a"], n * UN)
                        pe.wait_ge(s["xt_v"], n * UN)
                    elif c >= 2:
                        pe.wait_ge(s["accx_v"], KD * (c - 1))
                    for k in range(KD):
                        if k % (KD // 2) == 0:
                            pe.wait_ge(rows_in[2 * c + k // (KD // 2)], 16)
                        for m in range(TOPK):
                            last = mm(bank4[1 + 4 * (c % 2) + k // 4][:, k % 4, :], yt(c)[:, m * D + k * P:m * D + (k + 1) * P], ident,
                                      start=(m == 0), stop=(m == TOPK - 1))
                        last.then_inc(s["acc_mm"], 1)
                pe_norm(pe, 0, XS, CH, 3)

            @block.scalar
            def _(act):
                af = nc.scalar.activation
                act.wait_ge(s["logit_mm"], 1)
                af(scores[:].rearrange("p c e -> p (c e)"), bank[0][:, 0:CH * NE], ACT.Sigmoid).then_inc(s["sig_a"], 1)
                for t in range(2):
                    act.wait_ge(s["shup_mm"], t + 1)
                    af(gs[:, t, :], bank[1 + t], ACT.Silu).then_inc(s["shsil_a"], 1)
                last_i, n = load_groups(nc.scalar)

                def xt(i, u):
                    b = u % 2
                    act.wait_ge(s["xt_mm"], i * (2 * UN) + (2 * u + 1))
                    if later(i, u, 2):
                        act.wait_ge(s["up_mm"], i * UN + (u - 1))
                    af(xbT[:, b, 0:4, :], bank4[1], ACT.Copy).then_inc(s["xt_a"], 1)

                def silu(i, u):
                    b = u % 2
                    act.wait_ge(s["up_mm"], i * UN + (u + 1))
                    if later(i, u, 2):
                        act.wait_ge(s["g_v"], i * UN + (u - 1))
                    af(sil[:, b, :], bank[3 + b][:, 0:DE], ACT.Silu).then_inc(s["sil_a"], 1)

                def gt(i, u):
                    b = u % 2
                    act.wait_ge(s["gt_mm"], i * UN + (u + 1))
                    af(gT[:, b, :, :], bank4[5][:, 0:2, :], ACT.Copy).then_inc(s["gt_a"], 1)

                def yev(i, u):
                    b = u % 2
                    act.wait_ge(s["dn_mm"], i * (2 * UN) + (2 * u + 1))
                    if later(i, u, 2):
                        act.wait_ge(scatter_out[b], i * (8 * UN) + 16 * (u // 2))
                    af(y[:, b, 0:512], bank[6], ACT.Copy).then_inc(s["y_a"], 1)

                xt(0, 0)
                silu(0, 0)
                xt(0, 1)

                def blocks(i, steps):
                    for u in steps:
                        gt(i, u - 1)
                        silu(i, u)
                        xt(i, u + 1)
                        yev(i, u - 1)

                blocks(0, (1, 2))
                with act.Fori(0, last_i) as i:
                    blocks(i, LOOP)
                gt(last_i, UN - 2)
                silu(last_i, UN - 1)
                yev(last_i, UN - 2)
                gt(last_i, UN - 1)
                yev(last_i, UN - 1)
                act_norm(act, 0, XT, XS, CH)

            @block.gpsimd
            def _(pool):
                last_i, n = load_groups(nc.gpsimd)

                def gather(i, u):
                    b = u % UN
                    pool.wait_ge(s["idx_v"], i * (3 * UN) + 3 * (u + 1))
                    if later(i, u, UN):
                        pool.wait_ge(s["xt_mm"], i * (2 * UN) + 2 * (u + 1 - UN))
                    pool.sem_inc(s["may_gather"], 1)
                    nc.gpsimd.indirect_dma_start(out=xb[:, b, :], out_offset=None, in_=h2rows,
                                                 in_offset=bass.IndirectOffsetOnAxis(ap=toki[:, b:b + 1], axis=0),
                                                 bounds_check=S - 1, oob_is_err=False).then_inc(gather_in[b], 16)

                def scatter(i, u):
                    b = u % 2
                    pool.wait_ge(s["y_a"], i * UN + (u + 1))
                    pool.wait_ge(s["y_v"], i * UN + (u + 1))
                    pool.wait_ge(s["cpy_v"], i * UN + (u + 1))
                    pool.sem_inc(s["may_scatter"], 1)
                    nc.gpsimd.indirect_dma_start(out=rows, out_offset=bass.IndirectOffsetOnAxis(ap=sdst[:, u % UN:u % UN + 1], axis=0),
                                                 in_=y[:, b, :], in_offset=None,
                                                 bounds_check=S * TOPK - 1, oob_is_err=False).then_inc(scatter_out[b], 16)

                pool.wait_ge(s["xb_v"], 1)
                for u in range(UN):
                    gather(0, u)

                def blocks(i, steps):
                    for u in steps:
                        gather(i, u + 3)
                        scatter(i, u - 1)

                blocks(0, (1, 2))
                with pool.Fori(0, last_i) as i:
                    blocks(i, LOOP)
                for b in range(2):
                    pool.wait_ge(gather_in[b], n * 16 + 16)
                scatter(last_i, UN - 2)
                scatter(last_i, UN - 1)

            @block.vector
            def _(dve):
                v = nc.vector
                n_of = {}

                def step(name, ins, wait=False):
                    n_of[name] = n_of.get(name, 0) + 1
                    ins.then_inc(s[name], 1)
                    if wait:
                        dve.wait_ge(s[name], n_of[name])

                R = lambda ins, wait=True: step("route_v", ins, wait)
                bias = rc[:, R_BIAS:R_BIAS + NE].unsqueeze(1).to_broadcast([P, CH, NE])
                step("xb_v", v.memset(xb[:], 0.0), True)
                dve.wait_ge(s["small_in"], 48)
                dve.wait_ge(s["sig_a"], 1)
                R(v.tensor_copy(iota[:], rc[:, R_IOTA:R_IOTA + P]), False)
                R(v.tensor_tensor(sel[:], scores[:], bias, ALU.add))
                for c in range(CH):
                    for q in range(8):
                        R(v.max(m8[:, 8 * c + q, :], sel[:, c, 8 * q:8 * q + 8]), c == CH - 1 and q == 7)
                R(v.tensor_tensor(gsc[:], m8[:, :, 0], m8[:, :, 1], ALU.add))
                g3 = gsc[:].rearrange("p (c q) -> p c q", c=CH)
                c3 = cmp[:].rearrange("p (c q r) -> p c q r", c=CH, q=8)
                c4 = cmp2[:].rearrange("p (c q r) -> p c q r", c=CH, q=8)
                other = g3.unsqueeze(2).to_broadcast([P, CH, 8, 8])
                own = g3.unsqueeze(3).to_broadcast([P, CH, 8, 8])
                tril = rc[:, R_TRIL:R_TRIL + 64].unsqueeze(1).to_broadcast([P, CH, 64])
                R(v.tensor_tensor(c3, other, own, ALU.is_gt), False)
                R(v.tensor_tensor(c4, other, own, ALU.is_equal))
                R(v.tensor_tensor(cmp2[:].rearrange("p (c n) -> p c n", c=CH), cmp2[:].rearrange("p (c n) -> p c n", c=CH),
                                  tril, ALU.mult))
                R(v.tensor_tensor(cmp[:], cmp[:], cmp2[:], ALU.add))
                R(v.tensor_reduce(rank[:], cmp[:].rearrange("p (q r) -> p q r", r=8), AX, ALU.add))
                R(v.tensor_scalar(rank[:], rank[:], 3.5, None, ALU.is_lt))
                R(v.tensor_scalar(gneg[:], rank[:], -1.0, 1e30, ALU.add, ALU.mult), False)
                sel8 = sel[:].rearrange("p c (q r) -> p (c q) r", r=8)
                selm8 = selm[:].rearrange("p c (q r) -> p (c q) r", r=8)
                R(v.tensor_tensor(selm8, sel8, rank[:].unsqueeze(2).to_broadcast([P, 32, 8]), ALU.mult))
                R(v.tensor_tensor(selm8, selm8, gneg[:].unsqueeze(2).to_broadcast([P, 32, 8]), ALU.add))
                for c in range(CH):
                    R(v.max(top[:, c, :], selm[:, c, :]), c == CH - 1)
                for c in range(CH):
                    R(v.match_replace(work[:, c, :], top[:, c, :], selm[:, c, :], -3e30), c == CH - 1)
                R(v.tensor_scalar(msk[:], work[:], -2e30, None, ALU.is_lt))
                assert n_of["route_v"] == N_MASK, n_of["route_v"]
                R(v.tensor_tensor(wts[:], scores[:], msk[:], ALU.mult))
                R(v.tensor_reduce(wsum[:], wts[:], AX, ALU.add))
                R(v.reciprocal(wsum[:], wsum[:]))
                R(v.tensor_scalar(wsum[:], wsum[:], 2.5, None, ALU.mult))
                R(v.tensor_tensor(tab[:, :, :, 2].rearrange("p e c -> p c e"), wts[:],
                                  wsum[:].unsqueeze(2).to_broadcast([P, CH, NE]), ALU.mult), False)
                for c in range(CH):
                    R(v.tensor_tensor_scan(kidx[:, c, :], ones[:, 0:NE], msk[:, c, :], 0.0, ALU.mult, ALU.add), c == CH - 1)
                R(v.tensor_tensor(kidx[:], kidx[:], msk[:], ALU.subtract))
                R(v.tensor_tensor(tab[:, :, :, 1].rearrange("p e c -> p c e"), kidx[:],
                                  rc[:, R_BASE:R_BASE + 4].unsqueeze(2).to_broadcast([P, CH, NE]), ALU.add), False)
                dve.wait_ge(s["pos_mm"], 1)
                cnt, nb, end, base = (s64[:, q, :] for q in range(4))
                R(v.tensor_copy(cnt, bank[7][:, 256:256 + NE]))
                R(v.tensor_scalar(nb, cnt, 0.5, None, ALU.is_gt))
                for q in range(1, 4):
                    R(v.scalar_tensor_tensor(nb, cnt, q * P + 0.5, nb, ALU.is_gt, ALU.add))
                R(v.tensor_tensor_scan(end, ones[:, 0:NE], nb, 0.0, ALU.mult, ALU.add))
                R(v.tensor_tensor(base, end, nb, ALU.subtract), False)
                R(v.tensor_scalar(cmp[:, 0:NE], end, rc[:, R_J:R_J + 1], None, ALU.is_le))
                R(v.tensor_reduce(ej[:], cmp[:, 0:NE], AX, ALU.add))
                R(v.tensor_scalar(ej[:], ej[:], NE - 1.0, None, ALU.min))
                assert n_of["route_v"] == N_EXPERT, n_of["route_v"]
                R(v.tensor_scalar(base, base, float(P), None, ALU.mult))
                R(v.tensor_tensor(kidx[:], bank[7][:, 0:CH * NE].rearrange("p (c e) -> p c e", c=CH),
                                  base.unsqueeze(1).to_broadcast([P, CH, NE]), ALU.add))
                R(v.scalar_tensor_tensor(kidx[:], kidx[:], 1.0, msk[:], ALU.add, ALU.mult))
                R(v.tensor_scalar(tab[:, :, :, 0].rearrange("p e c -> p c e"), kidx[:], -1.0, None, ALU.add))
                dve.wait_ge(s["row_mm"], 1)
                R(v.tensor_copy(erow[:], bank[0][0:1, 0:P]), False)
                R(v.tensor_scalar(last_group[0:1, 0:1], end[0:1, NE - 1:NE], -1.0, None, ALU.add))
                R(v.tensor_scalar(last_group[0:1, 0:1], last_group[0:1, 0:1], UN.bit_length() - 1, None, ALU.arith_shift_right))
                assert n_of["route_v"] == N_ROUTE, n_of["route_v"]

                def shared_gate(t):
                    dve.wait_ge(s["shsil_a"], t + 1)
                    dve.wait_ge(s["shup_mm"], 3 + t)
                    step("shg_v", v.tensor_tensor(gs[:, t, :], gs[:, t, :], bank[3 + t], ALU.mult))

                def shared_add(o):
                    dve.wait_ge(s["shdn_mm"], o + 1)
                    step("shx_v", v.scalar_tensor_tensor(xT[:, o, :], bank[5 + o % 2], mod[:, 40 + o, 0:1], xT[:, o, :],
                                                         ALU.mult, ALU.add), o == KD - 1)
                last_i, n = load_groups(nc.vector)

                def hot_of(i, u):
                    b = u % 2
                    has_before = later(i, u, 2)
                    j = i * UN + u
                    e = nc.vector.value_load(erow[0:1, bass.ds(j, 1)] if type(i) is not int else erow[0:1, j:j + 1],
                                             min_val=0, max_val=NE - 1)
                    if has_before:
                        dve.wait_ge(s["info_mm"], i * UN + (u - 1))
                    v.tensor_copy(cur[:, b, :, :].unsqueeze(1), tab[:, bass.ds(e, 1), :, :]).then_inc(s["cur_v"], 1)
                    dve.wait_ge(s["cur_v"], i * UN + (u + 1))
                    for c in range(CH):
                        v.tensor_scalar(hot[:, b, c, :], iota[:], cur[:, b, c, 0:1], None, ALU.is_equal).then_inc(s["hot_v"], 1)
                    v.tensor_scalar(iota[:], iota[:], float(P), None, ALU.add).then_inc(s["hot_v"], 1)
                    dve.wait_ge(s["hot_v"], i * (5 * UN) + 5 * (u + 1))

                def index(i, u):
                    b = u % UN
                    dve.wait_ge(s["info_mm"], i * UN + (u + 1))
                    if later(i, u, UN):
                        dve.wait_ge(gather_in[b], i * 16 + 16 * (u // UN))
                        dve.wait_ge(s["g_v"], i * UN + (u + 1 - UN))
                        dve.wait_ge(s["cpy_v"], i * UN + (u + 1 - UN))
                    v.tensor_scalar(dsti[:, b:b + 1], bank[0][:, 0:1], FAR, None, ALU.add).then_inc(s["idx_v"], 1)
                    v.tensor_copy(wsl[:, b:b + 1], bank[0][:, 1:2]).then_inc(s["idx_v"], 1)
                    dve.wait_ge(s["idx_v"], i * (3 * UN) + (3 * u + 1))
                    v.tensor_scalar(toki[:, b:b + 1], dsti[:, b:b + 1], 3, None, ALU.arith_shift_right).then_inc(s["idx_v"], 1)
                    dve.wait_ge(s["idx_v"], i * (3 * UN) + 3 * (u + 1))

                def xt(i, u):
                    b = u % 2
                    dve.wait_ge(s["xt_mm"], i * (2 * UN) + 2 * (u + 1))
                    if later(i, u, 2):
                        dve.wait_ge(s["up_mm"], i * UN + (u - 1))
                    v.tensor_copy(xbT[:, b, 4:8, :], bank4[2]).then_inc(s["xt_v"], 1)

                def gate(i, u):
                    b = u % 2
                    dve.wait_ge(s["sil_a"], i * UN + (u + 1))
                    if later(i, u, 2):
                        dve.wait_ge(s["gt_mm"], i * UN + (u - 1))
                    v.tensor_copy(sdst[:, u % UN:u % UN + 1], dsti[:, u % UN:u % UN + 1]).then_inc(s["cpy_v"], 1)
                    v.scalar_tensor_tensor(g[:, b, :], bank[3 + b][:, DE:2 * DE], wsl[:, u % UN:u % UN + 1], sil[:, b, :], ALU.mult,
                                           ALU.mult).then_inc(s["g_v"], 1)

                def yev(i, u):
                    b = u % 2
                    dve.wait_ge(s["dn_mm"], i * (2 * UN) + 2 * (u + 1))
                    if later(i, u, 2):
                        dve.wait_ge(scatter_out[b], i * (8 * UN) + 16 * (u // 2))
                    v.tensor_copy(y[:, b, 512:1024], bank[7]).then_inc(s["y_v"], 1)

                hot_of(0, 0)
                hot_of(0, 1)
                shared_gate(0)
                shared_gate(1)
                index(0, 0)
                shared_add(0)
                index(0, 1)
                hot_of(0, 2)
                shared_add(1)
                shared_add(2)
                index(0, 2)
                for o in range(3, KD):
                    shared_add(o)
                xt(0, 0)
                hot_of(0, 3)
                gate(0, 0)
                index(0, 3)
                xt(0, 1)

                def blocks(i, steps):
                    for u in steps:
                        hot_of(i, u + 3)
                        gate(i, u)
                        index(i, u + 3)
                        xt(i, u + 1)
                        yev(i, u - 1)

                blocks(0, (1, 2))
                with dve.Fori(0, last_i) as i:
                    blocks(i, LOOP)
                gate(last_i, UN - 1)
                yev(last_i, UN - 2)
                yev(last_i, UN - 1)

                for c in range(CH):
                    for k in range(KD):
                        if k % 4 == 0:
                            dve.wait_ge(s["acc_mm"], KD * c + k + 4)
                        step("accx_v", v.scalar_tensor_tensor(xT[:, k, c * P:(c + 1) * P], bank4[1 + 4 * (c % 2) + k // 4][:, k % 4, :],
                                                              mod[:, 40 + k, 0:1], xT[:, k, c * P:(c + 1) * P], ALU.mult,
                                                              ALU.add), c == CH - 1 and k == KD - 1)
                dve_norm(dve, 0, XT, XS, CH)
                for k in range(KD):
                    step("fin_v", v.scalar_tensor_tensor(h2T[:, k, :], XT(k), fn[:, k:k + 1], bank[3], ALU.mult, ALU.mult))

        nc.all_engine_barrier()


def tiled(w, cols):
    part = w[:, cols]
    n = part.shape[0] // P
    return np.ascontiguousarray(part.reshape(n, P, -1).transpose(1, 0, 2)).reshape(P, -1)


def span(a, n=P):
    return list(range(a, a + n))


def first_stream(i, l):
    w_in, w_uq, w_ukv, w_out = (i[n][l] for n in ("w_in", "mla_w_uq", "mla_w_ukv", "w_out"))
    slots = []
    at = {"q": 0, "k": 512, "v": 1024, "gz": 1544, "mq": 2056, "mkv": 2440, "mkr": 2696, "mz": 2760, "lx": 3784, "lz": 4296}
    for name, n in (("k", 4), ("q", 4), ("v", 4), ("gz", 4), ("lx", 4), ("lz", 4), ("mq", 3), ("mkv", 2)):
        slots += [tiled(w_in, span(at[name] + P * t)) for t in range(n)]
    slots.append(tiled(w_in, span(at["mkr"], 64) * 2))
    slots += [tiled(w_in, span(at["mz"] + P * t)) for t in range(8)]
    uq = [tiled(w_uq, span(192 * h)) for h in range(8)]
    uq += [tiled(w_uq, span(384 * j + 128, 64) + span(384 * j + 320, 64)) for j in range(4)]
    for t in range(6):
        slots.append(np.concatenate([uq[2 * t], uq[2 * t + 1], np.zeros((P, SLOT - 768), w_uq.dtype)], axis=1))
    uk = [tiled(w_ukv, span(256 * h)) for h in range(8)]
    slots += [np.concatenate(uk[4 * t:4 * t + 4], axis=1) for t in range(2)]
    for half in range(2):
        slots.append(tiled(w_ukv, sum((span(256 * (4 * half + h) + 128) for h in range(4)), [])))
    for o in range(8):
        for half in range(2):
            slots.append(tiled(w_out[1024 * half:1024 * half + 1024], span(P * o)))
    ada = [tiled(i["ada_w_2"][0], span(P * t)) for t in range(l * ADA_LAYER, (l + 1) * ADA_LAYER)]
    own = iter(slots)
    ordered = []
    for st in PLAN:
        if st[0] == "ada":
            ordered.append(ada[st[1]])
        elif st[0] == "proj" and SLOT_AT[st] == len(ordered):
            ordered.append(next(own))
    ordered += list(own)
    return np.stack(ordered)


def first_columns(i, l):
    def tiles(v):
        return np.asarray(v).reshape(-1, P).T

    def taps(w):
        return np.asarray(w).T.reshape(-1, P, 4).transpose(1, 0, 2).reshape(P, -1)

    cw = i["gdn_conv_w"][l]
    parts = [tiles(i["norm_gain"][l]), taps(np.concatenate([cw[:, 512:1024], cw[:, 0:512], cw[:, 1024:]], axis=1)),
             taps(i["lru_conv_w"][l]), tiles(i["lru_conv_b"][l]), tiles(i["lru_b_r"][l]), tiles(i["lru_b_i"][l]),
             tiles(i["lru_a_param"][l]), tiles(i["mla_q_norm"][l]), tiles(i["mla_kv_norm"][l]), tiles(i["gdn_out_norm"][l]),
             np.broadcast_to(i["gdn_a_log"][l], (P, 4)), np.broadcast_to(i["gdn_dt_bias"][l], (P, 4))]
    return np.concatenate(parts, axis=1)


def lru_blocks(i, l):
    out = np.zeros((P, LW, 2, P), np.float32)
    for g, name in enumerate(("lru_w_r", "lru_w_i")):
        w = i[name][l]
        for j in range(LW):
            for b in range(2):
                out[64 * b:64 * b + 64, j, g, 64 * b:64 * b + 64] = w[2 * j + b]
    return out.reshape(P, -1)


def constants():
    f = np.float32
    c = np.zeros((P, NCONST), f)
    r = np.arange(P)
    c[:, K_ID:K_ID + P] = np.eye(P)
    c[:, K_TRI:K_TRI + P] = r[:, None] <= r[None, :]
    c[:, K_BIG:K_BIG + P] = np.where(r[None, :] >= r[:, None], f(1e30), f(0))
    c[:, K_BIGT:K_BIGT + P] = np.where(r[None, :] < r[:, None], f(-1e30), f(0))
    perm = np.zeros((P, P), f)
    for m in range(P):
        if m % 64 < 32:
            perm[m + 32, m] = -1
        else:
            perm[m - 32, m] = 1
    c[:, K_PERM:K_PERM + P] = perm
    inv = (f(1) / (f(10000.0) ** (np.arange(0, 64, 2, dtype=f) / f(64)))).astype(f)
    ang = np.arange(S, dtype=f)[:, None] * inv[None, :]
    ang = np.concatenate([ang, ang, ang, ang], axis=1)
    c[:, K_COS:K_COS + S] = np.cos(ang).T
    c[:, K_SIN:K_SIN + S] = np.sin(ang).T
    c[:, K_ONE] = 1
    c[:, K_EPS] = EPS
    c[:, K_MHALF:] = -0.5
    masks = np.zeros((P, 2 * (LEVELS + 1) + 2, P), f)
    for li in range(LEVELS + 1):
        b = 1 << li
        m = (r[:, None] // (2 * b) == r[None, :] // (2 * b)) & (r[:, None] % (2 * b) >= b) & (r[None, :] % (2 * b) < b)
        masks[:, 2 * li], masks[:, 2 * li + 1] = m, m.T
    masks[:, -2] = np.eye(P)
    masks[:, -1] = np.where(r[None, :] > r[:, None], f(-1e30), f(0))
    return c, masks.reshape(P, -1)


def second_stream(i):
    w, wo, s1, s3, s2 = (i[n][0] for n in ("w_in_2", "w_out_2", "shared_w1_2", "shared_w3_2", "shared_w2_2"))
    slots = [tiled(w, span(512 + P * t)) for t in range(4)]
    slots += [tiled(w, span(P * t)) for t in range(4)]
    slots += [tiled(w, span(1792 + P * t)) for t in range(2)]
    slots += [tiled(w, span(1536 + P * t)) for t in range(2)]
    slots += [tiled(w, span(2560 + P * t)) for t in range(4)]
    for at in (1024, 2048):
        slots += [tiled(w[256 * j:256 * j + 256], span(at, 512)) for j in range(4)]
    slots += [tiled(wo, span(P * t)) for t in range(8)]
    for sw in (s1, s3):
        slots += [tiled(sw, span(P * t)) for t in range(2)]
    slots += [np.concatenate([tiled(s2, span(P * (4 * g + t))) for t in range(4)], axis=1) for g in range(2)]
    slots += [np.zeros_like(slots[0])] * 2
    return np.stack(slots)


def second_columns(i):
    def tiles(v):
        return np.asarray(v).reshape(-1, P).T

    lam = np.concatenate([i[n][0] for n in ("lambda_q1_2", "lambda_k1_2", "lambda_q2_2", "lambda_k2_2")])
    dec = np.concatenate([i["ret_decay_fwd_2"][0], i["ret_decay_bwd_2"][0]])
    parts = [tiles(i["final_norm"]), tiles(i["norm1_g_2"][0]), tiles(i["norm2_g_2"][0]), tiles(i["final_norm_g_2"]),
             tiles(i["ada_b_2"][0]), tiles(i["dattn_norm_g_2"][0]), tiles(i["ret_norm_g_2"][0]),
             np.broadcast_to(dec, (P, 8)), np.broadcast_to(lam, (P, 256))]
    return np.concatenate(parts, axis=1)


def expert_weights(i):
    w1, w3, w2 = (i[n][0] for n in ("exp_w1_2", "exp_w3_2", "exp_w2_2"))
    up = np.concatenate([w1, w3], axis=2).reshape(NE, KD, P, 2 * DE).transpose(0, 2, 1, 3).reshape(NE, P, EW)
    down = w2.reshape(NE, 2, P, D).transpose(0, 2, 1, 3).reshape(NE, P, EW2)
    return np.ascontiguousarray(up), np.ascontiguousarray(down)


def constants2():
    f = np.float32
    r = np.arange(P)
    c = np.zeros((P, NCONST2), f)
    for m in range(P):
        if m % 32 < 16:
            c[m + 16, Z_PERM + m] = -1
        else:
            c[m - 16, Z_PERM + m] = 1
    inv = (f(10000.0) ** (-np.arange(16, dtype=f) / f(16))).astype(f)
    t = np.arange(S)
    rows, colsn = (t // 64).astype(f), (t % 64).astype(f)
    ang = np.stack([rows[:, None] * inv, colsn[:, None] * inv], axis=1)
    ang = np.repeat(ang[:, :, None, :], 2, axis=2).reshape(S, 64)
    ang = np.concatenate([ang, ang], axis=1)
    c[:, Z_COS:Z_COS + S] = np.cos(ang).T
    c[:, Z_SIN:Z_SIN + S] = np.sin(ang).T
    d = np.arange(FX)[None, :] - 384 - r[:, None]
    c[:, Z_DF:Z_DF + FX] = np.maximum(d, 0)
    c[:, Z_MF:Z_MF + FX] = np.where(d < 0, f(-1e30), f(0))
    c[:, Z_DB:Z_DB + FX] = np.maximum(-d, 0)
    c[:, Z_MB:Z_MB + FX] = np.where(d > 0, f(-1e30), f(0))
    d = np.arange(FC)[None, :] - P - r[:, None]
    c[:, Z_CF:Z_CF + FC] = NC_ + d
    c[:, Z_CB:Z_CB + FC] = S - d
    return c


def routing_constants(i):
    f = np.float32
    r = np.arange(P)
    c = np.zeros((P, NROUTE), f)
    c[:, R_IOTA:R_IOTA + P] = r[None, :]
    c[:, R_TRIS:R_TRIS + P] = r[:, None] < r[None, :]
    c[:, R_ONES:R_ONES + P] = 1
    c[:, R_BASE:R_BASE + 4] = 8 * (128 * np.arange(4)[None, :] + r[:, None]) - FAR
    c[:, R_J] = r
    g = np.arange(8)
    c[:, R_TRIL:R_TRIL + 64] = (g[None, :] < g[:, None]).reshape(1, 64)
    c[:, R_BIAS:R_BIAS + 64] = np.broadcast_to(i["router_bias_2"][0], (P, NE))
    return c


def build(nc, x, ctx_in, cond_in, stream, cols, gates_w, lru_w, const, masks, stream2, cols2, const2, route, router_w,
          up_w, down_w, out):
    h2rows = nc.dram_tensor("h2rows", [S, D], F32, kind="Internal").ap()
    rows = nc.dram_tensor("expert_rows", [S * TOPK, D], F32, kind="Internal").ap()
    with ExitStack() as outer:
        xT = outer.enter_context(nc.sbuf_tensor("xT", [P, KD, S], F32))
        CST = outer.enter_context(nc.sbuf_tensor("CST", [P, NCONST], F32))
        mod = outer.enter_context(nc.sbuf_tensor("mod", [P, NADA, 2], F32))
        start_in = outer.enter_context(nc.semaphore("start_in"))
        with ExitStack() as first:
            cond = first.enter_context(nc.sbuf_tensor("cond", [P, KD, 2], F32))
            cond_raw = first.enter_context(nc.sbuf_tensor("cond_raw", [P, KD, 2], F32))
            mk = first.enter_context(nc.sbuf_tensor("mk", [P, 2 * (LEVELS + 1), P], U8))
            bf = first.enter_context(nc.sbuf_tensor("bf", [P, 2, P], BF16))
            staged = first.enter_context(ExitStack())
            masks_in = staged.enter_context(nc.sbuf_tensor("masks_in", [P, 2 * (LEVELS + 1) + 2, P], F32))
            with nc.Block() as block:
                @block.sync
                def _(sp):
                    sp.dma_start(cond_raw[:].rearrange("p k n -> p (k n)"), cond_in).then_inc(start_in, 16)
                    sp.dma_start(xT[:].rearrange("p k n -> p (k n)"), x).then_inc(start_in, 16)
                    sp.dma_start(CST[:], const).then_inc(start_in, 16)
                    sp.dma_start(masks_in[:].rearrange("p j n -> p (j n)"), masks).then_inc(start_in, 16)
                    sp.wait_ge(start_in, 64)

                @block.scalar
                def _(act):
                    act.wait_ge(start_in, 64)
                    nc.scalar.activation(cond[:], cond_raw[:], ACT.Silu)

                @block.vector
                def _(dve):
                    dve.wait_ge(start_in, 64)
                    nc.vector.tensor_copy(mk[:], masks_in[:, 0:2 * (LEVELS + 1), :])
                    nc.vector.tensor_copy(bf[:], masks_in[:, 2 * (LEVELS + 1):, :])
            nc.all_engine_barrier()
            staged.close()
            first_block(nc, stream, cols, gates_w, lru_w, mk, bf, xT, CST, cond, mod)
        hT = outer.enter_context(nc.sbuf_tensor("hT2", [P, KD, NT], F32))
        second_mixer(nc, stream2, ctx_in, cols2, const2, xT, CST, mod, hT, h2rows)
        experts(nc, stream2, route, router_w, cols2, up_w, down_w, xT, CST, mod, hT, h2rows, rows, out)


def by_channels(a):
    return np.ascontiguousarray(a.T.reshape(KD, P, -1).transpose(1, 0, 2)).reshape(P, -1)


def kernel(**inputs):
    import concourse.bacc as bacc
    from concourse.bass_utils import run_bass_kernel_spmd

    i = {name: np.asarray(value) for name, value in inputs.items()}
    const, masks = constants()
    up, down = expert_weights(i)
    arrays = {
        "x": by_channels(i["x"][0]),
        "ctx": by_channels(i["ctx_2"][0]),
        "cond": np.stack([i["c_2"][0].reshape(KD, P), i["c_ctx_2"].reshape(KD, P)]).transpose(2, 1, 0).reshape(P, -1),
        "stream": np.concatenate([first_stream(i, l) for l in range(L)]),
        "cols": np.stack([first_columns(i, l) for l in range(L)]),
        "gates_w": np.stack([tiled(i["w_in"][l], span(1536, 8)) for l in range(L)]),
        "lru_w": np.stack([lru_blocks(i, l) for l in range(L)]),
        "const": const,
        "masks": masks,
        "stream2": second_stream(i),
        "cols2": second_columns(i),
        "const2": constants2(),
        "route": routing_constants(i),
        "router_w": tiled(i["router_w_2"][0], span(0, NE)),
        "expert_up": up,
        "expert_down": down,
    }
    arrays = {f"in_{name}": np.ascontiguousarray(a) for name, a in arrays.items()}
    nc = bacc.Bacc("TRN2", target_bir_lowering=False, num_devices=1)
    args = [nc.dram_tensor(name, a.shape, mybir.dt.from_np(a.dtype), kind="ExternalInput").ap() for name, a in arrays.items()]
    out = nc.dram_tensor("out", [P, KD * S], F32, kind="ExternalOutput").ap()
    build(nc, *args, out)
    got = run_bass_kernel_spmd(nc, [arrays], core_ids=[0]).results[0]["out"]
    return np.ascontiguousarray(got.reshape(P, KD, S).transpose(2, 1, 0).reshape(1, S, D))
```
